# Optimizing a Trainium2 kernel written in Bass

```python
import jax, jax.numpy as jnp
from jax import lax
import numpy as np
import math

D_MODEL = 1024
BATCH = 1
SEQ = 512
DEPTH = 1

MIX_WIDTH = D_MODEL
CONV_CH = MIX_WIDTH // 2
RWKV_CH = MIX_WIDTH - CONV_CH
RWKV_HEAD = 64
RWKV_HEADS = RWKV_CH // RWKV_HEAD
CONV_WIDTH = 31
LORA_W = 64
LORA_A = 64
LORA_G = 128
RWKV_PROJ = 3 * RWKV_CH + LORA_W + LORA_A + LORA_G
IN_PROJ = 2 * CONV_CH + RWKV_PROJ
RWKV_SPLITS = [RWKV_CH, 2 * RWKV_CH, 3 * RWKV_CH, 3 * RWKV_CH + LORA_W, 3 * RWKV_CH + LORA_W + LORA_A]
PEER_HEADS = 8
PEER_NKEYS = 128
PEER_EXPERTS = PEER_NKEYS * PEER_NKEYS
PEER_DQ = 256
PEER_TOPK = 16
PEER_CHUNK = 128
RMS_EPS = 1e-6
LN_EPS = 1e-5
GN_EPS = 64e-5


F32 = jnp.float32

def rmsnorm(x, g):
    xf = x.astype(F32)
    y = xf * lax.rsqrt(jnp.mean(xf * xf, axis=-1, keepdims=True) + RMS_EPS)
    return (y * g.astype(F32)).astype(x.dtype)

def modulate(x, shift, scale):
    return x * (1 + scale[:, None, :]) + shift[:, None, :]

def conformer_conv(p_conv, w_dw, b_dw, ln_w, ln_b):
    a, b = jnp.split(p_conv, 2, axis=-1)
    y = a * jax.nn.sigmoid(b)
    y = lax.conv_general_dilated(
        y, w_dw[:, None, :], window_strides=(1,), padding=[(CONV_WIDTH - 1, 0)],
        dimension_numbers=('NWC', 'WIO', 'NWC'), feature_group_count=CONV_CH) + b_dw
    yf = y.astype(F32)
    mu = jnp.mean(yf, axis=-1, keepdims=True)
    var = jnp.mean(jnp.square(yf - mu), axis=-1, keepdims=True)
    yf = (yf - mu) * lax.rsqrt(var + LN_EPS) * ln_w.astype(F32) + ln_b.astype(F32)
    return jax.nn.silu(yf).astype(p_conv.dtype)

def token_shift(p, mu):
    prev = jnp.pad(p, ((0, 0), (1, 0), (0, 0)))[:, :-1]
    return p + mu * (prev - p)

def rwkv7_mix(p_rwkv, mu, w0, w2, a0, a2, g2, k_k, k_a, r_k, gn_w, gn_b):
    B, S, _ = p_rwkv.shape
    xs = token_shift(p_rwkv, mu)
    r, k, v, wl, al, gl = jnp.split(xs, RWKV_SPLITS, axis=-1)
    w = -jax.nn.softplus(-(w0 + jnp.tanh(wl) @ w2)) - 0.5
    decay = jnp.exp(-jnp.exp(w.astype(F32)))
    a = jax.nn.sigmoid(a0 + al @ a2)
    g = jax.nn.sigmoid(gl) @ g2
    kk = k * k_k
    k = k * (1 + (a - 1) * k_a)

    def heads(t):
        return t.reshape(B, S, RWKV_HEADS, RWKV_HEAD).astype(F32)

    kk_h = heads(kk)
    kk_h = kk_h / jnp.maximum(jnp.sqrt(jnp.sum(kk_h * kk_h, axis=-1, keepdims=True)), 1e-12)
    r_h, k_h, v_h, w_h, a_h = heads(r), heads(k), heads(v), decay.reshape(B, S, RWKV_HEADS, RWKV_HEAD), heads(a)

    def step(state, inp):
        r_t, k_t, v_t, w_t, kk_t, a_t = inp
        sa = jnp.einsum('bhij,bhj->bhi', state, -kk_t)
        state = (state * w_t[:, :, None, :]
                 + sa[..., None] * (kk_t * a_t)[:, :, None, :]
                 + v_t[..., None] * k_t[:, :, None, :])
        y_t = jnp.einsum('bhij,bhj->bhi', state, r_t)
        return state, y_t

    def seq_first(t):
        return jnp.moveaxis(t, 1, 0)

    state0 = jnp.zeros((B, RWKV_HEADS, RWKV_HEAD, RWKV_HEAD), F32)
    _, y = lax.scan(step, state0, (seq_first(r_h), seq_first(k_h), seq_first(v_h),
                                   seq_first(w_h), seq_first(kk_h), seq_first(a_h)))
    y = jnp.moveaxis(y, 0, 1)
    mean = jnp.mean(y, axis=-1, keepdims=True)
    var = jnp.mean(jnp.square(y - mean), axis=-1, keepdims=True)
    y = ((y - mean) * lax.rsqrt(var + GN_EPS)).reshape(B, S, RWKV_CH) * gn_w.astype(F32) + gn_b.astype(F32)
    bonus = jnp.sum(r_h * k_h * r_k.astype(F32), axis=-1, keepdims=True) * v_h
    y = y + bonus.reshape(B, S, RWKV_CH)
    return (y * g.astype(F32)).astype(p_rwkv.dtype)

def peer_ffn(u, w_q, sub_keys, expert_u, expert_v):
    B, S, D = u.shape
    tokens = u.reshape(-1, PEER_CHUNK, D)

    def chunk(xc):
        tc = xc.shape[0]
        q = (xc @ w_q).reshape(tc, PEER_HEADS, 2, PEER_DQ // 2)
        s = jnp.einsum('thpd,hpkd->thpk', q, sub_keys).astype(F32)
        s_top, i_top = lax.top_k(s, PEER_TOPK)
        cand = s_top[:, :, 0, :, None] + s_top[:, :, 1, None, :]
        cand_idx = i_top[:, :, 0, :, None] * PEER_NKEYS + i_top[:, :, 1, None, :]
        best, pos = lax.top_k(cand.reshape(tc, PEER_HEADS, PEER_TOPK * PEER_TOPK), PEER_TOPK)
        expert = jnp.take_along_axis(cand_idx.reshape(tc, PEER_HEADS, PEER_TOPK * PEER_TOPK), pos, axis=-1)
        gate = jax.nn.softmax(best, axis=-1)
        ue = jnp.take(expert_u, expert, axis=0)
        ve = jnp.take(expert_v, expert, axis=0)
        h = jax.nn.gelu(jnp.einsum('thkd,td->thk', ue, xc).astype(F32), approximate=False)
        return jnp.einsum('thk,thkd->td', (gate * h).astype(xc.dtype), ve)

    out = lax.map(chunk, tokens)
    return out.reshape(B, S, D)

def first_inputs(seed: int = 0) -> dict:
    key = jax.random.key(seed)
    ks = iter(jax.random.split(key, 32))

    def nrm(shape, scale):
        return scale * jax.random.normal(next(ks), shape, jnp.float32)

    def gain(shape):
        return 1.0 + nrm(shape, 0.02)

    L = DEPTH
    return {
        'x': nrm((BATCH, SEQ, D_MODEL), 1.0),
        'c': nrm((BATCH, D_MODEL), 1.0),
        'ada_w': nrm((L, D_MODEL, 6 * D_MODEL), D_MODEL ** -0.5),
        'ada_b': nrm((L, 6 * D_MODEL), 0.02),
        'norm_mix_g': gain((L, D_MODEL)),
        'w_in': nrm((L, D_MODEL, IN_PROJ), D_MODEL ** -0.5),
        'conv_dw_w': nrm((L, CONV_WIDTH, CONV_CH), CONV_WIDTH ** -0.5),
        'conv_dw_b': nrm((L, CONV_CH), 0.02),
        'conv_ln_w': gain((L, CONV_CH)),
        'conv_ln_b': nrm((L, CONV_CH), 0.02),
        'rwkv_mu': jax.random.uniform(next(ks), (L, RWKV_PROJ), jnp.float32),
        'rwkv_w0': jax.random.uniform(next(ks), (L, RWKV_CH), jnp.float32, -6.0, 1.0),
        'rwkv_w2': nrm((L, LORA_W, RWKV_CH), 0.5 * LORA_W ** -0.5),
        'rwkv_a0': nrm((L, RWKV_CH), 0.1),
        'rwkv_a2': nrm((L, LORA_A, RWKV_CH), 0.5 * LORA_A ** -0.5),
        'rwkv_g2': nrm((L, LORA_G, RWKV_CH), LORA_G ** -0.5),
        'rwkv_k_k': 0.85 + nrm((L, RWKV_CH), 0.02),
        'rwkv_k_a': gain((L, RWKV_CH)),
        'rwkv_r_k': nrm((L, RWKV_HEADS, RWKV_HEAD), 0.1),
        'rwkv_gn_w': gain((L, RWKV_CH)),
        'rwkv_gn_b': nrm((L, RWKV_CH), 0.02),
        'w_out': nrm((L, MIX_WIDTH, D_MODEL), MIX_WIDTH ** -0.5),
        'norm_ffn_g': gain((L, D_MODEL)),
        'peer_w_q': nrm((L, D_MODEL, PEER_HEADS * PEER_DQ), D_MODEL ** -0.5),
        'peer_sub_keys': nrm((L, PEER_HEADS, 2, PEER_NKEYS, PEER_DQ // 2), (PEER_DQ // 2) ** -0.5),
        'peer_u': nrm((L, PEER_EXPERTS, D_MODEL), D_MODEL ** -0.5),
        'peer_v': nrm((L, PEER_EXPERTS, D_MODEL), (PEER_HEADS * PEER_TOPK) ** -0.5),
        'final_g': gain((D_MODEL,)),
    }

def first_block(x, c, ada_w, ada_b, norm_mix_g, w_in, conv_dw_w, conv_dw_b, conv_ln_w, conv_ln_b,
              rwkv_mu, rwkv_w0, rwkv_w2, rwkv_a0, rwkv_a2, rwkv_g2, rwkv_k_k, rwkv_k_a, rwkv_r_k,
              rwkv_gn_w, rwkv_gn_b, w_out, norm_ffn_g, peer_w_q, peer_sub_keys, peer_u, peer_v, final_g):
    for l in range(DEPTH):
        mod = jax.nn.silu(c) @ ada_w[l] + ada_b[l]
        sh_mix, sc_mix, gt_mix, sh_ffn, sc_ffn, gt_ffn = jnp.split(mod, 6, axis=-1)

        u = modulate(rmsnorm(x, norm_mix_g[l]), sh_mix, sc_mix)
        p = u @ w_in[l]
        y_conv = conformer_conv(p[..., :2 * CONV_CH], conv_dw_w[l], conv_dw_b[l], conv_ln_w[l], conv_ln_b[l])
        y_rwkv = rwkv7_mix(p[..., 2 * CONV_CH:], rwkv_mu[l], rwkv_w0[l], rwkv_w2[l], rwkv_a0[l], rwkv_a2[l],
                           rwkv_g2[l], rwkv_k_k[l], rwkv_k_a[l], rwkv_r_k[l], rwkv_gn_w[l], rwkv_gn_b[l])
        mix = jnp.concatenate([y_conv, y_rwkv], axis=-1) @ w_out[l]
        x = x + gt_mix[:, None, :] * mix

        u = modulate(rmsnorm(x, norm_ffn_g[l]), sh_ffn, sc_ffn)
        x = x + gt_ffn[:, None, :] * peer_ffn(u, peer_w_q[l], peer_sub_keys[l], peer_u[l], peer_v[l])
    return rmsnorm(x, final_g)


DEPTH_2 = 2

N_A = DEPTH_2 // 2
N_B = DEPTH_2 - N_A

DIFF_HEADS = 8
DIFF_HEAD_DIM = 64
DIFF_V_DIM = 2 * DIFF_HEAD_DIM
DIFF_QK_WIDTH = DIFF_HEADS * 2 * DIFF_HEAD_DIM
DIFF_V_WIDTH = DIFF_HEADS * DIFF_V_DIM

MLA_HEADS = 8
MLA_NOPE = 128
MLA_ROPE = 64
MLA_V = 128
Q_LORA = 384
KV_LORA = 256

D_FF = 4 * D_MODEL

ROPE_THETA = 10000.0
EPS = 1e-6
SUBLN_EPS = 1e-5
Q_BLOCK = 128


def rms_norm(x, g, eps=EPS):
    xf = x.astype(jnp.float32)
    y = xf * lax.rsqrt(jnp.mean(xf * xf, axis=-1, keepdims=True) + eps)
    return (y * g.astype(jnp.float32)).astype(x.dtype)

def rope_tables(seq, dim):
    pos = jnp.arange(seq, dtype=jnp.float32)
    inv_freq = ROPE_THETA ** (-jnp.arange(0, dim, 2, dtype=jnp.float32) / dim)
    ang = pos[:, None] * inv_freq[None, :]
    return jnp.cos(ang), jnp.sin(ang)

def apply_rope(x, cos, sin):
    half = x.shape[-1] // 2
    x1, x2 = x[..., :half], x[..., half:]
    c = cos[None, :, None, :].astype(x.dtype)
    s = sin[None, :, None, :].astype(x.dtype)
    return jnp.concatenate([x1 * c - x2 * s, x2 * c + x1 * s], axis=-1)

def causal_mask(i, seq):
    q_pos = i * Q_BLOCK + jnp.arange(Q_BLOCK)
    k_pos = jnp.arange(seq)
    return k_pos[None, :] <= q_pos[:, None]

def diff_attention(hn, w_qkv, w_o, lq1, lk1, lq2, lk2, subln_g, lambda_init, cos, sin):
    B, S, _ = hn.shape
    H, d = DIFF_HEADS, DIFF_HEAD_DIM
    qkv = hn @ w_qkv
    q, k, v = jnp.split(qkv, [DIFF_QK_WIDTH, 2 * DIFF_QK_WIDTH], axis=-1)
    q = apply_rope(q.reshape(B, S, 2 * H, d), cos, sin).reshape(B, S, H, 2, d)
    k = apply_rope(k.reshape(B, S, 2 * H, d), cos, sin).reshape(B, S, H, 2, d)
    v = v.reshape(B, S, H, DIFF_V_DIM)
    lam = (jnp.exp(jnp.sum(lq1.astype(jnp.float32) * lk1.astype(jnp.float32)))
           - jnp.exp(jnp.sum(lq2.astype(jnp.float32) * lk2.astype(jnp.float32)))
           + lambda_init)
    scale = d ** -0.5
    nb = S // Q_BLOCK
    qb = q.reshape(B, nb, Q_BLOCK, H, 2, d).transpose(1, 0, 2, 3, 4, 5)

    def block(args):
        q_blk, i = args
        s = jnp.einsum('bqhcd,bkhcd->bhcqk', q_blk, k).astype(jnp.float32) * scale
        s = jnp.where(causal_mask(i, S)[None, None, None], s, -jnp.inf)
        p = jax.nn.softmax(s, axis=-1)
        a = p[:, :, 0] - lam * p[:, :, 1]
        return jnp.einsum('bhqk,bkhe->bqhe', a.astype(v.dtype), v)

    o = lax.map(block, (qb, jnp.arange(nb)))
    o = o.transpose(1, 0, 2, 3, 4).reshape(B, S, H, DIFF_V_DIM)
    o = rms_norm(o, subln_g, SUBLN_EPS) * (1.0 - lambda_init)
    return o.reshape(B, S, DIFF_V_WIDTH) @ w_o

def mla_shared_kv(h, kv_in_norm_g, w_dkv, kv_norm_g, w_ukv, cos, sin):
    B, S, _ = h.shape
    hn = rms_norm(h, kv_in_norm_g)
    ckv = hn @ w_dkv
    c, k_rope = ckv[..., :KV_LORA], ckv[..., KV_LORA:]
    c = rms_norm(c, kv_norm_g)
    kv = (c @ w_ukv).reshape(B, S, MLA_HEADS, MLA_NOPE + MLA_V)
    k_nope, v = kv[..., :MLA_NOPE], kv[..., MLA_NOPE:]
    k_rope = apply_rope(k_rope[:, :, None, :], cos, sin)[:, :, 0, :]
    return k_nope, k_rope, v

def mla_attention(hn, w_dq, q_norm_g, w_uq, w_o, k_nope, k_rope, v, cos, sin):
    B, S, _ = hn.shape
    H = MLA_HEADS
    cq = rms_norm(hn @ w_dq, q_norm_g)
    q = (cq @ w_uq).reshape(B, S, H, MLA_NOPE + MLA_ROPE)
    q_nope = q[..., :MLA_NOPE]
    q_rope = apply_rope(q[..., MLA_NOPE:], cos, sin)
    scale = (MLA_NOPE + MLA_ROPE) ** -0.5
    nb = S // Q_BLOCK
    qn_b = q_nope.reshape(B, nb, Q_BLOCK, H, MLA_NOPE).transpose(1, 0, 2, 3, 4)
    qr_b = q_rope.reshape(B, nb, Q_BLOCK, H, MLA_ROPE).transpose(1, 0, 2, 3, 4)

    def block(args):
        qn, qr, i = args
        s = (jnp.einsum('bqhd,bkhd->bhqk', qn, k_nope)
             + jnp.einsum('bqhr,bkr->bhqk', qr, k_rope)).astype(jnp.float32) * scale
        s = jnp.where(causal_mask(i, S)[None, None], s, -jnp.inf)
        p = jax.nn.softmax(s, axis=-1)
        return jnp.einsum('bhqk,bkhe->bqhe', p.astype(v.dtype), v)

    o = lax.map(block, (qn_b, qr_b, jnp.arange(nb)))
    o = o.transpose(1, 0, 2, 3, 4).reshape(B, S, H * MLA_V)
    return o @ w_o

def sq_relu_mlp(hn, w_up, w_down):
    return jnp.square(jax.nn.relu(hn @ w_up)) @ w_down

def _w(key, shape, fan_in):
    return jax.random.normal(key, shape, jnp.float32) * fan_in ** -0.5

def _g(key, shape):
    return 1.0 + 0.02 * jax.random.normal(key, shape, jnp.float32)

def second_inputs(seed: int = 0) -> dict:
    key = jax.random.key(seed)
    ks = jax.random.split(key, 24)
    return {
        "x": jax.random.normal(ks[0], (BATCH, SEQ, D_MODEL), jnp.float32),
        "attn_norm_g": _g(ks[1], (DEPTH_2, D_MODEL)),
        "w_qkv_a": _w(ks[2], (N_A, D_MODEL, 2 * DIFF_QK_WIDTH + DIFF_V_WIDTH), D_MODEL),
        "lambda_q1": 0.1 * jax.random.normal(ks[3], (N_A, DIFF_HEAD_DIM), jnp.float32),
        "lambda_k1": 0.1 * jax.random.normal(ks[4], (N_A, DIFF_HEAD_DIM), jnp.float32),
        "lambda_q2": 0.1 * jax.random.normal(ks[5], (N_A, DIFF_HEAD_DIM), jnp.float32),
        "lambda_k2": 0.1 * jax.random.normal(ks[6], (N_A, DIFF_HEAD_DIM), jnp.float32),
        "subln_g": _g(ks[7], (N_A, DIFF_V_DIM)),
        "w_o_a": _w(ks[8], (N_A, DIFF_V_WIDTH, D_MODEL), DIFF_V_WIDTH),
        "kv_in_norm_g": _g(ks[9], (D_MODEL,)),
        "w_dkv": _w(ks[10], (D_MODEL, KV_LORA + MLA_ROPE), D_MODEL),
        "kv_norm_g": _g(ks[11], (KV_LORA,)),
        "w_ukv": _w(ks[12], (KV_LORA, MLA_HEADS * (MLA_NOPE + MLA_V)), KV_LORA),
        "w_dq": _w(ks[13], (N_B, D_MODEL, Q_LORA), D_MODEL),
        "q_norm_g": _g(ks[14], (N_B, Q_LORA)),
        "w_uq": _w(ks[15], (N_B, Q_LORA, MLA_HEADS * (MLA_NOPE + MLA_ROPE)), Q_LORA),
        "w_o_b": _w(ks[16], (N_B, MLA_HEADS * MLA_V, D_MODEL), MLA_HEADS * MLA_V),
        "mlp_norm_g": _g(ks[17], (DEPTH_2, D_MODEL)),
        "w_up": _w(ks[18], (DEPTH_2, D_MODEL, D_FF), D_MODEL),
        "w_down": _w(ks[19], (DEPTH_2, D_FF, D_MODEL), D_FF),
        "final_norm_g": _g(ks[20], (D_MODEL,)),
    }

def second_block(x, attn_norm_g, w_qkv_a, lambda_q1, lambda_k1, lambda_q2, lambda_k2, subln_g, w_o_a,
              kv_in_norm_g, w_dkv, kv_norm_g, w_ukv, w_dq, q_norm_g, w_uq, w_o_b,
              mlp_norm_g, w_up, w_down, final_norm_g):
    S = x.shape[1]
    cos_a, sin_a = rope_tables(S, DIFF_HEAD_DIM)
    cos_b, sin_b = rope_tables(S, MLA_ROPE)
    h = x
    k_nope = k_rope = v = None
    for l in range(DEPTH_2):
        if l < N_A:
            lambda_init = 0.8 - 0.6 * math.exp(-0.3 * l)
            hn = rms_norm(h, attn_norm_g[l])
            h = h + diff_attention(hn, w_qkv_a[l], w_o_a[l], lambda_q1[l], lambda_k1[l],
                                   lambda_q2[l], lambda_k2[l], subln_g[l], lambda_init,
                                   cos_a, sin_a)
        else:
            if l == N_A:
                k_nope, k_rope, v = mla_shared_kv(h, kv_in_norm_g, w_dkv, kv_norm_g, w_ukv,
                                                  cos_b, sin_b)
            j = l - N_A
            hn = rms_norm(h, attn_norm_g[l])
            h = h + mla_attention(hn, w_dq[j], q_norm_g[j], w_uq[j], w_o_b[j],
                                  k_nope, k_rope, v, cos_b, sin_b)
        h = h + sq_relu_mlp(rms_norm(h, mlp_norm_g[l]), w_up[l], w_down[l])
    return rms_norm(h, final_norm_g)


def setup_inputs(seed=0):
    out = dict(first_inputs(seed))
    for name, value in second_inputs(seed + 1).items():
        if name != "x":
            out[name + "_2"] = value
    return out


def reference(
    x, c, ada_w, ada_b, norm_mix_g, w_in, conv_dw_w, conv_dw_b, conv_ln_w, conv_ln_b, rwkv_mu,
    rwkv_w0, rwkv_w2, rwkv_a0, rwkv_a2, rwkv_g2, rwkv_k_k, rwkv_k_a, rwkv_r_k, rwkv_gn_w,
    rwkv_gn_b, w_out, norm_ffn_g, peer_w_q, peer_sub_keys, peer_u, peer_v, final_g,
    attn_norm_g_2, w_qkv_a_2, lambda_q1_2, lambda_k1_2, lambda_q2_2, lambda_k2_2, subln_g_2,
    w_o_a_2, kv_in_norm_g_2, w_dkv_2, kv_norm_g_2, w_ukv_2, w_dq_2, q_norm_g_2, w_uq_2, w_o_b_2,
    mlp_norm_g_2, w_up_2, w_down_2, final_norm_g_2,
):
    x = first_block(
        x, c, ada_w, ada_b, norm_mix_g, w_in, conv_dw_w, conv_dw_b, conv_ln_w, conv_ln_b,
        rwkv_mu, rwkv_w0, rwkv_w2, rwkv_a0, rwkv_a2, rwkv_g2, rwkv_k_k, rwkv_k_a, rwkv_r_k,
        rwkv_gn_w, rwkv_gn_b, w_out, norm_ffn_g, peer_w_q, peer_sub_keys, peer_u, peer_v,
        final_g,
    )
    return second_block(
        x, attn_norm_g_2, w_qkv_a_2, lambda_q1_2, lambda_k1_2, lambda_q2_2, lambda_k2_2,
        subln_g_2, w_o_a_2, kv_in_norm_g_2, w_dkv_2, kv_norm_g_2, w_ukv_2, w_dq_2, q_norm_g_2,
        w_uq_2, w_o_b_2, mlp_norm_g_2, w_up_2, w_down_2, final_norm_g_2,
    )


_drawn_inputs = setup_inputs


def setup_inputs(seed=0):
    import zlib

    import numpy as np

    out = dict(_drawn_inputs(seed))
    spreads = {}
    factors = {'norm_mix_g': 4.313,
     'conv_ln_w': 4.015,
     'conv_ln_b': 3.507,
     'rwkv_a0': 3.829,
     'rwkv_k_k': 2.708,
     'rwkv_k_a': 2.687,
     'rwkv_gn_w': 7.374,
     'rwkv_gn_b': 3.138,
     'norm_ffn_g': 8.0,
     'attn_norm_g_2': 3.04,
     'lambda_q2_2': 8.0,
     'lambda_k2_2': 6.97,
     'subln_g_2': 4.493,
     'kv_in_norm_g_2': 8.0,
     'kv_norm_g_2': 8.0,
     'q_norm_g_2': 8.0,
     'mlp_norm_g_2': 2.766,
     'final_norm_g_2': 8.018,
     'lambda_q1_2': 6.306,
     'lambda_k1_2': 3.106}
    for name, (base, spread) in spreads.items():
        noise = np.random.default_rng([zlib.crc32(name.encode()), seed]).standard_normal(out[name].shape)
        drawn = base * np.exp(spread * noise) if base else spread * noise
        out[name] = __import__('jax').numpy.asarray(drawn.astype(out[name].dtype))
    for name, factor in factors.items():
        out[name] = (out[name] * factor).astype(out[name].dtype)
    return out
```

```python
from contextlib import ExitStack
import math

import numpy as np
import concourse.bass as bass
from concourse import mybir

F32 = mybir.dt.float32
U32 = mybir.dt.uint32
ALU = mybir.AluOpType
ACT = mybir.ActivationFunctionType
AX = mybir.AxisListType.X

D, S, H = 1024, 512, 8
NEG = -1.0e30
NBANK = 8
SLOT = 4096
NSLOT = 4
CW = 31
CDECAY = math.exp(-0.5)

CONST = ["ident", "ones", "bd", "rot", "iota", "causal", "strict", "incl", "m1",
         "t1", "t2", "t4", "t8", "t16", "t32"]
CCOL = {n: 128 * i for i, n in enumerate(CONST)}
NCONST = 128 * len(CONST) + 512

VEC = [("c", 8), ("ada_b", 48), ("norm_mix_g", 8), ("conv_dw_w", 4 * CW), ("conv_dw_b", 4), ("conv_ln_w", 4),
       ("conv_ln_b", 4), ("rwkv_mu", 14), ("rwkv_w0", 4), ("rwkv_a0", 4), ("rwkv_k_k", 4), ("rwkv_k_a", 4),
       ("rwkv_r_k", 4), ("rwkv_gn_w", 4), ("rwkv_gn_b", 4), ("norm_ffn_g", 8), ("final_g", 8),
       ("attn_norm_g_2", 16), ("subln_g_2", 1), ("kv_in_norm_g_2", 8), ("kv_norm_g_2", 2), ("q_norm_g_2", 3),
       ("mlp_norm_g_2", 16), ("final_norm_g_2", 8), ("lambda", 4)]
VCOL = {}
NVEC = 0
for _n, _w in VEC:
    VCOL[_n] = NVEC
    NVEC += _w


def shape_constants():
    i = np.arange(128)
    r, c = i[:, None], i[None, :]
    same = (r // 64) == (c // 64)
    m = {"ident": r == c, "ones": np.ones((128, 128)), "bd": same, "iota": np.broadcast_to(c, (128, 128)),
         "causal": np.where(c <= r, 0.0, NEG), "strict": same & (r < c), "incl": same & (r <= c),
         "m1": (r // 2 == c // 2) & (r % 2 == 1) & (c % 2 == 0)}
    for b in (1, 2, 4, 8, 16, 32):
        m[f"t{b}"] = (r // (2 * b) == c // (2 * b)) & (r % (2 * b) < b) & (c % (2 * b) >= b)
    rot = np.zeros((128, 128))
    for o in (0, 64):
        for j in range(32):
            rot[o + 32 + j, o + j] = -1.0
            rot[o + j, o + 32 + j] = 1.0
    m["rot"] = rot
    scan = np.broadcast_to((np.arange(512) % 64 != 0), (128, 512))
    table = np.concatenate([np.asarray(m[n], np.float32) for n in CONST] + [scan.astype(np.float32)], axis=1)
    freq = (np.float32(10000.0) ** (-np.arange(0, 64, 2, dtype=np.float32) / np.float32(64))).astype(np.float32)
    ang = np.arange(S, dtype=np.float32)[None, :] * freq[:, None]
    cs = np.concatenate([np.tile(np.cos(ang), (4, 1)), np.tile(np.sin(ang), (4, 1))], axis=1).astype(np.float32)
    return np.ascontiguousarray(table), np.ascontiguousarray(cs)


class Prog:

    def __init__(self, nc, ctx):
        self.nc, self.ctx = nc, ctx
        self.q = {e: [] for e in ("pe", "act", "dve", "pool", "sp")}
        self.sem, self.cnt = {}, {}
        self.known = {e: {} for e in self.q}
        self.gate = {e: [] for e in self.q}
        for e in ("pe", "act", "dve", "pool"):
            self.new_sem(e)
        self.bank_free = [[] for _ in range(NBANK)]
        self.nbank = 0
        self.slots = [0, 1, 2, 3]
        self.slot_free = [[] for _ in range(NSLOT)]
        self.nload = 0
        self.stores = []
        for s in range(NSLOT):
            self.new_sem(f"slot{s}")

    def new_sem(self, name):
        self.sem[name] = self.ctx.enter_context(self.nc.semaphore("s_" + name))
        self.cnt[name] = 0

    def waits(self, eng, tokens):
        need = {}
        for t in tokens:
            if t is not None and self.known[eng].get(t[0], 0) < t[1]:
                need[t[0]] = max(need.get(t[0], 0), t[1])
        self.known[eng].update(need)
        return sorted(need.items())

    def op(self, eng, fn, after=(), inc=True, serial=True):
        tokens = list(after) + self.gate[eng]
        self.gate[eng] = []
        if eng != "pe" and serial:
            tokens.append((eng, self.cnt[eng]))
        w = self.waits(eng, tokens)
        if inc:
            self.cnt[eng] += 1
        self.q[eng].append((w, fn, eng if inc else None, 1))
        return (eng, self.cnt[eng])

    def dma(self, sem, out, in_, after=(), eng="sp"):
        if sem not in self.sem:
            self.new_sem(sem)
        tokens = list(after) + self.gate[eng]
        self.gate[eng] = []
        w = self.waits(eng, tokens)
        self.cnt[sem] += 16
        self.q[eng].append((w, lambda e: e.dma_start(out, in_), sem, 16))
        return (sem, self.cnt[sem])

    def done(self):
        return [(e, self.cnt[e]) for e in ("pe", "act", "dve", "pool")]

    def phase(self):
        t = self.done()
        for e in ("pe", "act", "dve", "pool"):
            self.gate[e] = self.gate[e] + t
        return t

    def bank(self):
        b = self.nbank % NBANK
        self.nbank += 1
        return b

    def mm(self, out, lhsT, rhs, start, stop, after=(), inc=False):
        return self.op("pe", lambda e: e.matmul(out, lhsT, rhs, start=start, stop=stop), after, inc)

    def group(self, b, out, pairs, after=()):
        t = None
        for i, (l, r) in enumerate(pairs):
            t = self.mm(out, l, r, i == 0, i == len(pairs) - 1,
                        list(after) + self.bank_free[b] if i == 0 else (), inc=i == len(pairs) - 1)
        return t

    def load(self, width, dst_src):
        s = self.slots[self.nload % len(self.slots)]
        self.nload += 1
        t = None
        for f, src in dst_src:
            t = self.dma(f"slot{s}", f(self.ring[:, s * SLOT:s * SLOT + width]), src, self.slot_free[s])
        return s, self.ring[:, s * SLOT:s * SLOT + width], t

    def tt(self, out, a, b, op, after=(), eng="dve"):
        return self.op(eng, lambda e: e.tensor_tensor(out, a, b, op), after)

    def ts(self, out, a, s1, s2, op0, op1=None, after=(), eng="dve"):
        if op1 is None:
            return self.op(eng, lambda e: e.tensor_scalar(out, a, s1, None, op0), after)
        return self.op(eng, lambda e: e.tensor_scalar(out, a, s1, s2, op0, op1), after)

    def stt(self, out, a, s, b, op0, op1, after=(), eng="dve"):
        return self.op(eng, lambda e: e.scalar_tensor_tensor(out=out, in0=a, scalar=s, in1=b, op0=op0, op1=op1), after)

    def act(self, out, in_, func, after=(), bias=0.0, scale=1.0, accum=None):
        if func == ACT.Copy:
            return self.op("act", lambda e: e.copy(out, in_), after)
        if accum is not None:
            return self.op("act", lambda e: e.activation(out, in_, func, bias=bias, scale=scale, accum_out=accum), after)
        return self.op("act", lambda e: e.activation(out, in_, func, bias=bias, scale=scale), after)

    def copy(self, out, in_, after=(), eng="dve"):
        if eng == "act":
            return self.op("act", lambda e: e.copy(out, in_), after)
        return self.op(eng, lambda e: e.tensor_copy(out, in_), after)

    def memset(self, out, v, after=(), eng="dve"):
        return self.op(eng, lambda e: e.memset(out, v), after)

    def recip(self, out, in_, after=()):
        return self.op("dve", lambda e: e.reciprocal(out, in_), after)

    def reduce(self, out, in_, op, after=()):
        return self.op("dve", lambda e: e.tensor_reduce(out, in_, AX, op), after)

    def play(self, name, e):
        for w, fn, sem, n in self.q[name]:
            for s, v in w:
                e.wait_ge(self.sem[s], v)
            ins = fn(e)
            if sem is not None:
                ins.then_inc(self.sem[sem], n)


def fmat(ap, n=512):
    return ap.rearrange("p (k n) -> p k n", n=n)


class Net:
    def __init__(self, nc, ctx, dram, stop):
        self.P = P = Prog(nc, ctx)
        self.d, self.stop_at = dram, stop
        total = 52800
        self.mem = ctx.enter_context(nc.sbuf_tensor("mem", [128, total], F32))
        self.ps = ctx.enter_context(nc.psum_tensor("ps", [128, NBANK, 512], F32))
        at = 0

        def region(n):
            nonlocal at
            at += n
            return self.mem[:, at - n:at]

        self.xT = fmat(region(4096))
        self.const = region(NCONST)
        self.vec = region(NVEC)
        self.modv = region(48)
        self.small = region(256)
        P.ring = region(NSLOT * SLOT)
        self.un = region(4096)
        self.scr = region(24576)
        assert at <= total, at
        self.uT = fmat(self.un)
        self.scanm = self.const[:, 128 * len(CONST):NCONST]

    def C(self, name):
        return self.const[:, CCOL[name]:CCOL[name] + 128]

    def V(self, name, i=0, n=1):
        return self.vec[:, VCOL[name] + i:VCOL[name] + i + n]

    def bk(self, b):
        return self.ps[:, b, :]

    def half(self, i):
        if i < 12:
            return self.scr[:, 2048 * i:2048 * (i + 1)]
        if i < 14:
            return self.un[:, 2048 * (i - 12):2048 * (i - 11)]
        return self.P.ring[:, 2 * SLOT + 2048 * (i - 14):2 * SLOT + 2048 * (i - 13)]

    def rms(self, src, n, dim, eps, gain, dst, after=(), tmp=None, shift=None, center_scale=None):
        P = self.P
        b = P.bank()
        tmp = self.rtmp if tmp is None else tmp
        t = None
        for i in range(n):
            t = P.act(dst(i), src(i), ACT.Square, after)
            t = P.mm(self.bk(b), self.C("ones"), dst(i), i == 0, i == n - 1,
                     [t] + (P.bank_free[b] if i == 0 else []), inc=True)
        t = P.ts(tmp, self.bk(b), 1.0 / dim, eps, ALU.mult, ALU.add, [t])
        P.bank_free[b] = [t]
        t = P.act(tmp, tmp, ACT.Sqrt, [t])
        t = P.recip(tmp, tmp, [t])
        out = []
        for i in range(n):
            t = P.stt(dst(i), src(i), gain(i), tmp, ALU.mult, ALU.mult, [t])
            if shift is not None:
                t2 = P.act(dst(i), dst(i), ACT.Identity, [t], bias=shift(i))
                out.append(t2)
            else:
                out.append(t)
        return out

    def w_tiles(self, W, n0, n1, after=()):
        nk = W.shape[0] // 128
        n = n1 - n0
        src = W.rearrange("(k p) n -> p k n", p=128)[:, :, n0:n1]
        s, ap, t = self.P.load(nk * n, [(lambda a: a.rearrange("p (k n) -> p k n", n=n), src)])
        return s, ap.rearrange("p (k n) -> p k n", n=n), t

    def gemm(self, W, src, src_tok, evac, n_cols=None, chunk=512, first=0):
        P = self.P
        N = W.shape[1] if n_cols is None else n_cols
        nk = W.shape[0] // 128
        for n0 in range(0, N, chunk):
            n1 = min(N, n0 + chunk)
            s, w, tw = self.w_tiles(W, n0, n1)
            t = None
            for j in range((n1 - n0) // 128):
                b = P.bank()
                for k in range(nk):
                    after = [src_tok[k]] if src_tok else []
                    if k == 0:
                        after = after + [tw] + P.bank_free[b]
                    t = P.mm(self.bk(b), w[:, k, 128 * j:128 * j + 128], src(k), k == 0, k == nk - 1,
                             after, inc=k == nk - 1)
                P.bank_free[b] = [evac(first + n0 // 128 + j, b, t)]
            P.slot_free[s] = [t]

    def mod_cols(self, chunks):
        P = self.P
        t = None
        for ch in chunks:
            s, w, tw = self.w_tiles(self.d["ada_w"], 512 * ch, 512 * ch + 512)
            b = P.bank()
            for j in range(4):
                t = P.group(b, self.ps[:, b, j:j + 1],
                            [(w[:, k, 128 * j:128 * j + 128], self.small[:, k:k + 1]) for k in range(8)],
                            [tw, self.t_silu])
            P.slot_free[s] = [t]
            t = P.tt(self.modv[:, 4 * ch:4 * ch + 4], self.ps[:, b, 0:4], self.V("ada_b", 4 * ch, 4), ALU.add, [t])
            P.bank_free[b] = [t]
        return t

    def start(self):
        P = self.P
        d = self.d
        self.t_c = P.dma("cst", self.const, d["consts"])
        self.t_v = P.dma("vec", self.vec, d["vecs"])
        self.t_x = P.dma("x", self.xT, d["xT"].rearrange("(k p) n -> p k n", p=128))
        self.t_silu = P.act(self.small[:, 0:8], self.V("c", 0, 8), ACT.Silu, [self.t_v])
        for e in ("pe", "act", "dve", "pool"):
            P.gate[e] = [self.t_c, self.t_v, self.t_x]

    def mixing(self):
        P, d = self.P, self.d
        h = self.half
        self.rtmp = self.scr[:, 24064:24576]
        t = self.mod_cols(range(4))
        g1 = self.small[:, 8:16]
        t = P.stt(g1, self.modv[:, 8:16], 1.0, self.V("norm_mix_g", 0, 8), ALU.add, ALU.mult, [t])
        tu = self.rms(lambda i: self.xT[:, i, :], 8, D, 1e-6, lambda i: g1[:, i:i + 1],
                      lambda i: self.uT[:, i, :], shift=lambda i: self.modv[:, i:i + 1])
        omu = self.small[:, 16:30]
        P.ts(omu, self.V("rwkv_mu", 0, 14), -1.0, 1.0, ALU.mult, ALU.add)
        oka = self.small[:, 30:34]
        P.ts(oka, self.V("rwkv_k_a", 0, 4), -1.0, 1.0, ALU.mult, ALU.add)
        P.slots = [0, 1, 2]
        P.nload = 0
        r, k_, v = fmat(h(0)), fmat(h(9)), fmat(h(4))
        gated = fmat(h(11))
        lo = fmat(h(16)[:, 0:1024])
        w2a2, g2 = h(16)[:, 1024:1536], h(16)[:, 1536:2048]
        slot3 = P.slot_free[3]
        t_w2 = P.dma("w2", w2a2[0:64, :], d["rwkv_w2"], slot3)
        t_w2 = P.dma("w2", w2a2[64:128, :], d["rwkv_a2"], slot3)
        t_g2 = P.dma("g2", g2, d["rwkv_g2"], slot3)
        held = {}
        sig = fmat(h(8))

        def evac(j, b, t):
            if j < 4:
                return P.copy(gated[:, j, :], self.bk(b), [t], eng="act")
            if j < 8:
                i = j - 4
                t = P.act(sig[:, i, :], self.bk(b), ACT.Sigmoid, [t])
                P.tt(gated[:, i, :], gated[:, i, :], sig[:, i, :], ALU.mult, [t])
                return t
            i = j - 8
            dst = (r, k_, v)[i // 4][:, i % 4, :] if i < 12 else lo[:, i - 12, :]
            t = P.ts(dst, self.bk(b), omu[:, i:i + 1], None, ALU.mult, after=[t])
            return P.stt(dst[:, 1:S], self.ps[:, b, 0:S - 1], self.V("rwkv_mu", i), dst[:, 1:S],
                         ALU.mult, ALU.add, [t])

        self.gemm(d["w_in"], lambda k: self.uT[:, k, :], tu, evac)
        t_in = P.done()
        conv = fmat(h(8))
        self.t_conv = None
        for i in range(4):
            wt = lambda j: self.V("conv_dw_w", CW * i + j)
            t = P.ts(conv[:, i, :], gated[:, i, :], wt(CW - 1), self.V("conv_dw_b", i), ALU.mult, ALU.add,
                     after=t_in)
        self.conv_todo = [(i, sh) for i in range(4) for sh in range(1, CW)]
        self.conv, self.gated = conv, gated
        self.rwkv(t_in, r, k_, v, lo, w2a2, g2, t_w2, t_g2, oka)

    def conv_some(self, n):
        P = self.P
        for i, sh in self.conv_todo[:n]:
            P.stt(self.conv[:, i, sh:], self.gated[:, i, :S - sh], self.V("conv_dw_w", CW * i + CW - 1 - sh),
                  self.conv[:, i, sh:], ALU.mult, ALU.add)
        self.conv_todo = self.conv_todo[n:]

    def rwkv(self, t_in, r, k_, v, lo, w2a2, g2, t_w2, t_g2, oka):
        P, h = self.P, self.half
        sg, cum, a = fmat(h(10)), fmat(h(12)), fmat(h(13))
        kk, pd, pi = fmat(h(14)), fmat(h(15)), fmat(h(17))
        tmp = fmat(h(7))
        Rf, Af, Bf, Kf = r, fmat(h(1)), fmat(h(2)), fmat(h(3))
        g, bonus = fmat(h(5)), fmat(h(6))
        t0 = P.act(lo[0:64, 0, :], lo[0:64, 0, :], ACT.Tanh, t_in)
        t1 = P.act(lo[:, 1, :], lo[:, 1, :], ACT.Sigmoid)
        for q in range(4):
            c = slice(128 * q, 128 * q + 128)
            b = P.bank()
            t = P.group(b, self.bk(b), [(w2a2[0:64, c], lo[0:64, 0, :])], [t0, t_w2])
            t = P.act(sg[:, q, :], self.bk(b), ACT.Sigmoid, [t], bias=self.V("rwkv_w0", q))
            P.bank_free[b] = [t]
            b = P.bank()
            t = P.group(b, self.bk(b), [(w2a2[64:128, c], lo[64:128, 0, :])])
            t = P.act(a[:, q, :], self.bk(b), ACT.Sigmoid, [t], bias=self.V("rwkv_a0", q))
            P.bank_free[b] = [t]
            b = P.bank()
            t = P.group(b, self.bk(b), [(g2[:, c], lo[:, 1, :])], [t1, t_g2])
            t = P.copy(g[:, q, :], self.bk(b), [t], eng="act")
            P.bank_free[b] = [t]
        for q in range(4):
            cq, sq = cum[:, q, :], sg[:, q, :]
            P.op("dve", lambda e, cq=cq, sq=sq: e.tensor_tensor_scan(cq, self.scanm, sq, 0.0, ALU.mult, ALU.add),
                 [t])
        tc = P.tt(sg, cum, sg, ALU.subtract)
        t_p = P.act(pd, cum, ACT.Exp, [tc], scale=-CDECAY)
        t_i = P.act(pi, cum, ACT.Exp, scale=CDECAY)
        t_pp = P.act(sg, sg, ACT.Exp, scale=-CDECAY)
        for q in range(4):
            t = P.ts(kk[:, q, :], k_[:, q, :], self.V("rwkv_k_k", q), None, ALU.mult)
            t = P.tt(tmp[:, q, :], kk[:, q, :], kk[:, q, :], ALU.mult)
            b = P.bank()
            t = P.group(b, self.bk(b), [(self.C("bd"), tmp[:, q, :])], [t])
            t = P.ts(Af[:, q, :], self.bk(b), 1e-24, None, ALU.max, after=[t])
            P.bank_free[b] = [t]
        t = P.act(Af, Af, ACT.Sqrt, [t])
        P.recip(Af, Af, [t])
        t_kk = P.tt(kk, kk, Af, ALU.mult)
        P.stt(Af, kk, -1.0, sg, ALU.mult, ALU.mult, [t_pp])
        P.tt(Bf, kk, a, ALU.mult)
        P.tt(Bf, Bf, pi, ALU.mult)
        for q in range(4):
            P.ts(tmp[:, q, :], a[:, q, :], self.V("rwkv_k_a", q), oka[:, q:q + 1], ALU.mult, ALU.add)
        P.tt(k_, k_, tmp, ALU.mult)
        P.tt(Kf, k_, pi, ALU.mult)
        for q in range(4):
            t = P.stt(tmp[:, q, :], r[:, q, :], self.V("rwkv_r_k", q), k_[:, q, :], ALU.mult, ALU.mult)
            b = P.bank()
            t = P.group(b, self.bk(b), [(self.C("bd"), tmp[:, q, :])], [t])
            t = P.tt(bonus[:, q, :], self.bk(b), v[:, q, :], ALU.mult, [t])
            P.bank_free[b] = [t]
        P.tt(Rf, r, pd, ALU.mult)
        pc = self.small[:, 64:96]
        P.copy(pc.rearrange("p (q c) -> p q c", q=4), pd[:, :, 63:512:64])
        if self.stop_at == "rprep":
            return
        self.chunks(Rf, Af, Bf, Kf, v, pc)
        y = fmat(h(7))
        sq, rs = fmat(h(9)), fmat(h(10))
        yc = fmat(h(12))
        self.conv_some(len(self.conv_todo))
        ph = P.phase()
        for q in range(4):
            b = P.bank()
            t = P.group(b, self.bk(b), [(self.C("bd"), y[:, q, :])])
            t = P.stt(yc[:, q, :], self.bk(b), -1.0 / 64, y[:, q, :], ALU.mult, ALU.add, [t])
            P.bank_free[b] = [t]
            t = P.act(sq[:, q, :], yc[:, q, :], ACT.Square, [t])
            b = P.bank()
            t = P.group(b, self.bk(b), [(self.C("bd"), sq[:, q, :])], [t])
            t = P.ts(rs[:, q, :], self.bk(b), 1.0 / 64, 64e-5, ALU.mult, ALU.add, after=[t])
            P.bank_free[b] = [t]
        t = P.act(rs, rs, ACT.Sqrt, [t])
        P.recip(rs, rs, [t])
        P.tt(yc, yc, rs, ALU.mult)
        for q in range(4):
            P.ts(yc[:, q, :], yc[:, q, :], self.V("rwkv_gn_w", q), self.V("rwkv_gn_b", q), ALU.mult, ALU.add)
        P.tt(yc, yc, bonus, ALU.add)
        t_y = P.tt(y, yc, g, ALU.mult)
        conv = self.conv
        b = P.bank()
        t = P.group(b, self.bk(b), [(self.C("ones"), conv[:, i, :]) for i in range(4)])
        mu = self.half(13)[:, 0:512]
        t = P.ts(mu, self.bk(b), 1.0 / 512, None, ALU.mult, after=[t] + [t_y])
        P.bank_free[b] = [t]
        b = P.bank()
        for i in range(4):
            t = P.tt(conv[:, i, :], conv[:, i, :], mu, ALU.subtract)
            t = P.act(sq[:, i, :], conv[:, i, :], ACT.Square, [t])
            t = P.mm(self.bk(b), self.C("ones"), sq[:, i, :], i == 0, i == 3,
                     [t] + (P.bank_free[b] if i == 0 else []), inc=True)
        t = P.ts(mu, self.bk(b), 1.0 / 512, 1e-5, ALU.mult, ALU.add, after=[t])
        P.bank_free[b] = [t]
        t = P.act(mu, mu, ACT.Sqrt, [t])
        P.recip(mu, mu, [t])
        for i in range(4):
            t = P.tt(conv[:, i, :], conv[:, i, :], mu, ALU.mult)
            t = P.act(conv[:, i, :], conv[:, i, :], ACT.Silu, [t], bias=self.V("conv_ln_b", i),
                      scale=self.V("conv_ln_w", i))
        src = lambda k: (conv[:, k, :] if k < 4 else y[:, k - 4, :])
        P.slots = [0, 1]
        P.nload = 0
        P.slot_free = [f + ph for f in P.slot_free]
        toks = [t] * 4 + [t_y] * 4

        def evac(j, b, t):
            return P.stt(self.xT[:, j, :], self.bk(b), self.modv[:, 16 + j:17 + j], self.xT[:, j, :],
                         ALU.mult, ALU.add, [t])

        self.gemm(self.d["w_out"], src, toks, evac)
        P.slots = [0, 1, 2, 3]
        P.nload = 0
        end = P.phase()
        P.slot_free = [f + end for f in P.slot_free]

    def chunks(self, Rf, Af, Bf, Kf, v, pc):
        P, h = self.P, self.half
        mats = []
        for i in (9, 10, 12, 13, 14, 15, 16, 17):
            mats += [h(i)[:, 0:1024], h(i)[:, 1024:2048]]
        (Ab, Bb, Kb, Rb, Vb, TB, TK, TV, MT, Ml, X, XT, W, NT, RBT, RKT) = mats
        st = [P.ring[:, SLOT:SLOT + 512], P.ring[:, SLOT + 512:SLOT + 1024]]
        Z, SA = P.ring[:, SLOT + 1024:SLOT + 1536], P.ring[:, SLOT + 1536:SLOT + 2048]
        P.slots = [0]
        P.nload = 0
        y = fmat(h(7))
        P.phase()
        for m in (Ab, Bb, Kb, Rb, Vb):
            P.memset(m, 0.0, eng="pool")
        P.memset(st[0], 0.0, eng="pool")
        t_zero = P.cnt["pool"]
        cur = 0

        def m4(ap):
            return ap.rearrange("p (u n) -> p u n", n=128)

        def bc(c):
            return c.unsqueeze(1).broadcast_to([128, 4, 128])

        rest = {}
        for gidx in range(4):
            ld = None
            free = P.done()
            for n, (src, dst) in enumerate(((Af, Ab), (Bf, Bb), (Kf, Kb), (Rf, Rb), (v, Vb))):
                for hd in range(2):
                    p = slice(64 * hd, 64 * hd + 64)
                    for cc in range(2):
                        o = m4(dst)[p, 4 * cc:4 * cc + 4, 64 * hd:64 * hd + 64]
                        s = src[p, :, 64 * (2 * gidx + cc):64 * (2 * gidx + cc) + 64]
                        ld = P.copy(o, s, free, eng="pool")
                        free = []
            t_bd = ld

            def product(l, rr, dst, mask, copy_to=None, mask2=None):
                toks = []
                for cc in range(2):
                    b = P.bank()
                    t = None
                    for q in range(4):
                        u = 4 * cc + q
                        t = P.mm(self.ps[:, b, 128 * q:128 * q + 128], m4(l)[:, u, :], m4(rr)[:, u, :], True, True,
                                 [t_bd] + P.bank_free[b] if q == 0 else (), inc=q == 3)
                    o = dst[:, 512 * cc:512 * cc + 512]
                    t = P.tt(m4(o), m4(self.bk(b)), bc(mask), ALU.mult, [t])
                    P.bank_free[b] = [t]
                    toks.append(t)
                return toks

            product(Ab, Bb, X, self.C("m1"))
            tm = product(Bb, Ab, MT, self.C("strict"))
            product(Kb, Ab, NT, self.C("strict"))
            product(Bb, Rb, RBT, self.C("incl"))
            product(Kb, Rb, RKT, self.C("incl"))
            for cc in range(2):
                c = slice(512 * cc, 512 * cc + 512)
                P.tt(m4(X[:, c]), m4(X[:, c]), bc(self.C("ident")), ALU.add)
                P.tt(m4(XT[:, c]), m4(MT[:, c]), bc(self.C("t1")), ALU.mult)
                tx = P.tt(m4(XT[:, c]), m4(XT[:, c]), bc(self.C("ident")), ALU.add)
            for src, dst in ((Bb, TB), (Kb, TK), (Vb, TV)):
                for cc in range(2):
                    b = P.bank()
                    for q in range(4):
                        u = 4 * cc + q
                        o, i_ = self.ps[:, b, 128 * q:128 * q + 128], m4(src)[:, u, :]
                        t = P.op("pe", lambda e, o=o, i_=i_: e.transpose(o, i_, self.C("ident")),
                                 [t_bd] + P.bank_free[b] if q == 0 else (), inc=q == 3)
                    t = P.copy(dst[:, 512 * cc:512 * cc + 512], self.bk(b), [t], eng="act")
                    P.bank_free[b] = [t]
            t_tr = t
            t_x = {0: tx, 1: tx}
            t_pe = {0: None, 1: None}
            for lv in (2, 4, 8, 16, 32):
                tw = {}
                for cc in range(2):
                    c = slice(512 * cc, 512 * cc + 512)
                    t = P.tt(m4(Ml[:, c]), m4(MT[:, c]), bc(self.C(f"t{lv}")), ALU.mult,
                             [tm[1], t_pe[cc]], eng="pool")
                    b = P.bank()
                    for q in range(4):
                        u = 4 * cc + q
                        tp = P.mm(self.ps[:, b, 128 * q:128 * q + 128], m4(Ml)[:, u, :], m4(X)[:, u, :], True, True,
                                  [t, t_x[cc]] + P.bank_free[b] if q == 0 else (), inc=q == 3)
                    tw[cc] = P.copy(W[:, c], self.bk(b), [tp], eng="act")
                    P.bank_free[b] = [tw[cc]]
                for cc in range(2):
                    c = slice(512 * cc, 512 * cc + 512)
                    outs = [(XT, W, X), (W, XT, XT)] if lv < 32 else [(W, XT, XT)]
                    done = []
                    for l, rr, dst in outs:
                        b = P.bank()
                        for q in range(4):
                            u = 4 * cc + q
                            tp = P.mm(self.ps[:, b, 128 * q:128 * q + 128], m4(l)[:, u, :], m4(rr)[:, u, :],
                                      True, True, [tw[cc]] + P.bank_free[b] if q == 0 else (), inc=q == 3)
                        done.append((b, tp, dst))
                    for b, tp, dst in done:
                        t_x[cc] = P.tt(dst[:, c], dst[:, c], self.bk(b), ALU.add, [tp, done[-1][1]])
                        P.bank_free[b] = [t_x[cc]]
                    t_pe[cc] = done[-1][1]
            self.mod_cols([4 + 2 * gidx, 5 + 2 * gidx])
            self.conv_some(20)
            for cc in range(2):
                S0, S1 = st[cur], st[1 - cur]
                ch = 2 * gidx + cc
                t_st = [self.t_state, ("pool", t_zero)]
                b = P.bank()
                for q in range(4):
                    u = 4 * cc + q
                    o = self.ps[:, b, 128 * q:128 * q + 128]
                    P.mm(o, m4(NT)[:, u, :], m4(TV)[:, u, :], True, False, [t_tr] + P.bank_free[b] + t_st)
                    t = P.mm(o, m4(Ab)[:, u, :], m4(S0)[:, q, :], False, True, (), inc=True)
                tz = P.copy(Z, self.bk(b), [t], eng="act")
                P.bank_free[b] = [tz]
                b = P.bank()
                for q in range(4):
                    u = 4 * cc + q
                    t = P.mm(self.ps[:, b, 128 * q:128 * q + 128], m4(XT)[:, u, :], m4(Z)[:, q, :], True, True,
                             [tz, t_x[cc]] + P.bank_free[b] if q == 0 else (), inc=q == 3)
                ts = P.copy(SA, self.bk(b), [t, self.t_y])
                P.bank_free[b] = [ts]
                b = P.bank()
                for q in range(4):
                    u = 4 * cc + q
                    o = self.ps[:, b, 128 * q:128 * q + 128]
                    P.mm(o, self.C("ident"), m4(S0)[:, q, :], True, False, P.bank_free[b] if q == 0 else ())
                    P.mm(o, m4(TK)[:, u, :], m4(TV)[:, u, :], False, False)
                    t = P.mm(o, m4(TB)[:, u, :], m4(SA)[:, q, :], False, True, [ts], inc=True)
                pcc = pc.rearrange("p (q c) -> p q c", q=4)[:, :, ch:ch + 1].broadcast_to([128, 4, 128])
                self.t_state = P.tt(m4(S1), m4(self.bk(b)), pcc, ALU.mult, [t, self.t_y])
                P.bank_free[b] = [self.t_state]
                b = P.bank()
                for q in range(4):
                    u = 4 * cc + q
                    o = self.ps[:, b, 128 * q:128 * q + 128]
                    P.mm(o, m4(S0)[:, q, :], m4(Rb)[:, u, :], True, False, P.bank_free[b] if q == 0 else ())
                    P.mm(o, m4(TV)[:, u, :], m4(RKT)[:, u, :], False, False)
                    t = P.mm(o, m4(SA)[:, q, :], m4(RBT)[:, u, :], False, True, (), inc=q == 3)
                self.t_y = t
                for hd in range(2):
                    p = slice(64 * hd, 64 * hd + 64)
                    t = P.copy(y[p, :, 64 * ch:64 * ch + 64],
                               m4(self.bk(b))[p, :, 64 * hd:64 * hd + 64], [t], eng="act")
                P.bank_free[b] = [t]
                cur = 1 - cur

    def peer(self):
        P, d = self.P, self.d
        scr = self.scr
        U = 4096
        self.rtmp = scr[:, 24064:24576]
        gf = self.small[:, 8:16]
        P.stt(gf, self.modv[:, 32:40], 1.0, self.V("norm_ffn_g", 0, 8), ALU.add, ALU.mult)
        tu = self.rms(lambda i: self.xT[:, i, :], 8, D, 1e-6, lambda i: gf[:, i:i + 1],
                      lambda i: self.uT[:, i, :], shift=lambda i: self.modv[:, 24 + i:25 + i], after=P.done())
        qF = fmat(scr[:, 0:2 * U])
        keys = scr[:, 2 * U:2 * U + 2048]
        t_keys = P.dma("keys", keys, d["keysT"], P.done())

        def evac(j, b, t):
            return P.copy(qF[:, j, :], self.bk(b), [t], eng="act" if j % 2 else "dve")

        self.gemm(d["peer_w_q"], lambda k: self.uT[:, k, :], tu, evac)
        t_q = P.done()
        base = 2 * U + 2048
        sc = scr[:, base:base + 2048].rearrange("p (j n) -> p j n", n=128)
        base += 2048
        cand = scr[:, base:base + 2048].rearrange("p (h a b) -> p h a b", h=8, a=16)
        base += 2048
        eq = scr[:, base:base + 2048].rearrange("p (h a b) -> p h a b", h=8, a=16)
        base += 2048
        sm = []
        for w in (256, 256, 256, 128, 128, 128, 128, 128, 128, 128, 8, 8):
            sm.append(scr[:, base:base + w])
            base += w
        vals, idxu, idxf, best, posu, tmpu, ai, bi, i1, i2, s8, m8 = sm
        gate = tmpu
        IA, IB, WG = (scr[:, base + 512 * i:base + 512 * i + 512] for i in range(3))
        base += 1536
        gk = scr[:, base:base + 128]
        base += 128
        it16 = self.C("iota")[:, 0:16]
        v3 = vals.rearrange("p (j k) -> p j k", k=16)
        x3 = idxu.bitcast(U32).rearrange("p (j k) -> p j k", k=16)
        f4 = idxf.rearrange("p (h two k) -> p h two k", two=2, k=16)
        v4 = vals.rearrange("p (h two k) -> p h two k", two=2, k=16)
        b3 = best.rearrange("p (h k) -> p h k", k=16)
        p3 = posu.bitcast(U32).rearrange("p (h k) -> p h k", k=16)

        def top16(src, val, idx):
            for half in range(2):
                vv, ii = val[:, 8 * half:8 * half + 8], idx[:, 8 * half:8 * half + 8]
                P.op("dve", lambda e, vv=vv: e.max(vv, src))
                P.op("dve", lambda e, vv=vv, ii=ii: e.max_index(ii, vv, src))
                if half == 0:
                    P.op("dve", lambda e, vv=vv: e.match_replace(src, vv, src, -3.0e38))

        for tt in range(4):
            ts_ = slice(128 * tt, 128 * tt + 128)
            for j0 in range(0, 16, 4):
                b = P.bank()
                for j in range(j0, j0 + 4):
                    t = P.mm(self.ps[:, b, 128 * (j - j0):128 * (j - j0) + 128], qF[:, j, ts_],
                             keys[:, 128 * j:128 * j + 128], True, True,
                             t_q + [t_keys] + P.bank_free[b] if j == j0 else (), inc=j == j0 + 3)
                t = P.copy(sc[:, j0:j0 + 4, :], self.bk(b), [t, ("dve", P.cnt["dve"])], eng="act")
                P.bank_free[b] = [t]
            P.gate["dve"] = P.gate["dve"] + [t]
            for j in range(16):
                top16(sc[:, j, :], v3[:, j, :], x3[:, j, :])
            P.copy(idxf, idxu.bitcast(U32))
            for hh in range(8):
                P.tt(cand[:, hh], v4[:, hh, 0, :].unsqueeze(2).broadcast_to([128, 16, 16]),
                     v4[:, hh, 1, :].unsqueeze(1).broadcast_to([128, 16, 16]), ALU.add)
                top16(cand[:, hh].rearrange("p a b -> p (a b)"), b3[:, hh, :], p3[:, hh, :])
            g3 = gate.rearrange("p (h k) -> p h k", k=16)
            t = P.tt(g3, b3, b3[:, :, 0:1].broadcast_to([128, 8, 16]), ALU.subtract, [("pe", P.cnt["pe"])])
            t = P.act(gate, gate, ACT.Exp, [t])
            P.reduce(s8, g3, ALU.add, [t])
            P.recip(s8, s8)
            tg = P.tt(g3, g3, s8.unsqueeze(2).broadcast_to([128, 8, 16]), ALU.mult)
            a_u, b_u = ai.bitcast(U32), bi.bitcast(U32)
            pu = posu.bitcast(U32)
            P.ts(a_u, pu, 4, None, ALU.logical_shift_right)
            P.ts(b_u, pu, 15, None, ALU.bitwise_and)
            for src, side, dst in ((a_u, 0, i1), (b_u, 1, i2)):
                t = P.copy(gk, src)
                P.tt(eq, gk.rearrange("p (h k) -> p h k", k=16).unsqueeze(3).broadcast_to([128, 8, 16, 16]),
                     it16.unsqueeze(1).unsqueeze(1).broadcast_to([128, 8, 16, 16]), ALU.is_equal)
                P.tt(eq, eq, f4[:, :, side, :].unsqueeze(2).broadcast_to([128, 8, 16, 16]), ALU.mult)
                ti = P.reduce(dst.rearrange("p (h k) -> p h k", k=16), eq, ALU.add)
            b = P.bank()
            for n, src in enumerate((i1, i2, gate)):
                o = self.ps[:, b, 128 * n:128 * n + 128]
                t = P.op("pe", lambda e, o=o, src=src: e.transpose(o, src, self.C("ident")),
                         [ti, tg] + P.bank_free[b] if n == 0 else (), inc=n == 2)
            for n, dst in enumerate((IA, IB, WG)):
                t = P.copy(dst[:, ts_], self.ps[:, b, 128 * n:128 * n + 128], [t], eng="act")
            P.bank_free[b] = [t]
        ph = P.phase()
        G = d["gates"]
        stage = [scr[:, 0:U].rearrange("p (k t) -> p k t", t=32), scr[:, U:2 * U].rearrange("p (k t) -> p k t", t=32)]
        st_free = [[], []]
        oh = [scr[:, 2 * U + 1024 * i:2 * U + 1024 * i + 1024] for i in range(4)]
        oh_free = [[] for _ in range(4)]
        iota = self.C("iota")
        t_store = []
        for blk in range(16):
            s = blk % 2
            for q in range(8):
                n = blk * 8 + q
                o = oh[n % 4]
                B4, A4 = o[:, 0:512], o[:, 512:1024]
                t0 = blk * 32 + 4 * q
                for i in range(4):
                    tb = P.ts(B4[:, 128 * i:128 * i + 128], iota, IB[:, t0 + i:t0 + i + 1], None, ALU.is_equal,
                              after=oh_free[n % 4], eng="pool")
                for i in range(4):
                    ta = P.ts(A4[:, 128 * i:128 * i + 128], iota, IA[:, t0 + i:t0 + i + 1],
                              WG[:, t0 + i:t0 + i + 1], ALU.is_equal, ALU.mult, after=oh_free[n % 4])
                b = P.bank()
                for i in range(4):
                    c = slice(128 * i, 128 * i + 128)
                    t = P.mm(self.ps[:, b, c], B4[:, c], A4[:, c], True, True,
                             [ta, tb] + P.bank_free[b] if i == 0 else (), inc=i == 3)
                oh_free[n % 4] = [t]
                t = P.copy(stage[s][:, :, 4 * q:4 * q + 4].rearrange("p k t -> p t k"),
                           self.bk(b).rearrange("p (t k) -> p t k", k=128), [t] + st_free[s],
                           eng="act")
                P.bank_free[b] = [t]
            ts_ = P.dma(f"gst{s}", G[blk], stage[s].rearrange("p k t -> p (k t)"), [t])
            st_free[s] = [ts_]
            t_store.append(ts_)
        ph = P.phase()
        Gt = [scr[:, U * i:U * i + U] for i in (0, 1)]
        Wt = [fmat(scr[:, U * i:U * i + U]) for i in (2, 3)]
        acc = fmat(scr[:, 4 * U:5 * U])
        gel = [scr[:, 5 * U + 512 * i:5 * U + 512 * i + 512] for i in range(4)]
        gel_free = [[] for _ in range(4)]
        gt_free = [[P.cnt and ("pe", P.cnt["pe"]), ("act", P.cnt["act"])]] * 2
        wt_free = [[], []]
        Gr = G.rearrange("b p (k t) -> p b k t", t=32)

        def scores(g):
            tg = P.dma(f"gld{g % 2}", Gt[g % 2].rearrange("p (b k t) -> p b (k t)", b=16, t=32),
                       Gr[:, :, 8 * g:8 * g + 8, :].rearrange("p b k t -> p b (k t)"), t_store[-2:] + gt_free[g % 2] + ph)
            gv = Gt[g % 2].rearrange("p (b k t) -> p b k t", b=16, t=32)
            for half in range(2):
                s, w, tw = self.w_tiles(d["peer_uT"], 1024 * g + 512 * half, 1024 * g + 512 * half + 512)
                for j in range(4):
                    e = 4 * half + j
                    b = P.bank()
                    t = P.group(b, self.bk(b), [(w[:, k, 128 * j:128 * j + 128], self.uT[:, k, :]) for k in range(8)],
                                [tw])
                    x = gel[e % 4]
                    t2 = P.act(x, self.bk(b), ACT.Gelu, [t] + gel_free[e % 4])
                    P.bank_free[b] = [t2]
                    t2 = P.tt(Wt[g % 2][:, e, :].rearrange("p (b t) -> p b t", t=32),
                              x.rearrange("p (b t) -> p b t", t=32), gv[:, :, e, :], ALU.mult,
                              [t2, tg] + wt_free[g % 2])
                    gel_free[e % 4] = [t2]
                P.slot_free[s] = [t]
            gt_free[g % 2] = [t2]
            return t2

        def values(g, tw_):
            v2 = []
            for half in range(2):
                src = d["peer_v"][1024 * g + 512 * half:1024 * g + 512 * half + 512, :]
                s, w, tv = P.load(4096, [(lambda a: a.rearrange("p (k n) -> p k n", n=1024),
                                          src.rearrange("(k p) n -> p k n", p=128))])
                v2.append((s, w.rearrange("p (k n) -> p k n", n=1024), tv))
            for j in range(8):
                b = P.bank()
                t = P.group(b, self.bk(b), [(v2[k // 4][1][:, k % 4, 128 * j:128 * j + 128], Wt[g % 2][:, k, :])
                                            for k in range(8)], [tw_, v2[0][2], v2[1][2]])
                if g == 0:
                    t2 = P.copy(acc[:, j, :], self.bk(b), [t])
                else:
                    t2 = P.tt(acc[:, j, :], acc[:, j, :], self.bk(b), ALU.add, [t])
                P.bank_free[b] = [t2]
            for s, _, _ in v2:
                P.slot_free[s] = [t]
            wt_free[g % 2] = [t]

        tok = {0: scores(0)}
        for g in range(16):
            if g < 15:
                tok[g + 1] = scores(g + 1)
            values(g, tok[g])
        for j in range(8):
            P.stt(self.xT[:, j, :], acc[:, j, :], self.modv[:, 40 + j:41 + j], self.xT[:, j, :], ALU.mult, ALU.add)
        P.phase()

    def norm_to_x(self, gain):
        P = self.P
        self.rms(lambda i: self.xT[:, i, :], 8, D, 1e-6, gain, lambda i: self.uT[:, i, :], after=P.done())
        for i in range(8):
            P.copy(self.xT[:, i, :], self.uT[:, i, :])
        P.phase()

    def norm_u(self, name, off):
        P = self.P
        return self.rms(lambda i: self.xT[:, i, :], 8, D, 1e-6, lambda i: self.V(name, off + i),
                        lambda i: self.uT[:, i, :], after=P.done())

    def add_x(self, j, b, t):
        return self.P.tt(self.xT[:, j, :], self.xT[:, j, :], self.bk(b), ALU.add, [t])

    def rope(self, x, t, tmp):
        P = self.P
        b = P.bank()
        t = P.group(b, self.bk(b), [(self.C("rot"), x)], [t])
        t1 = P.tt(tmp, self.bk(b), self.rs, ALU.mult, [t])
        P.bank_free[b] = [t1]
        P.tt(x, x, self.rc, ALU.mult)
        return P.tt(x, x, tmp, ALU.add)

    def values_T(self, W, src, nk, n, dst, tok, view):
        P = self.P
        for c0 in range(0, n, 512):
            w, tw, s = view(c0)
            for tt in range(4):
                b = P.bank()
                t = P.group(b, self.bk(b), [(src(k)[:, 128 * tt:128 * tt + 128], w(k)) for k in range(nk)],
                            [tw] + tok)
                t2 = P.copy(dst[:, tt, c0:c0 + 512], self.bk(b), [t], eng="act")
                P.bank_free[b] = [t2]
            if s is not None:
                P.slot_free[s] = [t]

    def softmax_rows(self, b, width, scale, e, stat, tok):
        P = self.P
        P.reduce(stat[:, 0:1], self.ps[:, b, 0:width], ALU.max, [tok])
        t = P.ts(stat[:, 1:2], stat[:, 0:1], -scale, None, ALU.mult)
        t = P.act(e[:, 0:width], self.ps[:, b, 0:width], ACT.Exp, [t], bias=stat[:, 1:2], scale=scale,
                  accum=stat[:, 2:3])
        P.bank_free[b] = [t]
        return P.recip(stat[:, 3:4], stat[:, 2:3], [t])

    def turn(self, a, aT, nb, t, free):
        P = self.P
        b = P.bank()
        for kb in range(nb):
            o, i_ = self.ps[:, b, 128 * kb:128 * kb + 128], a[:, 128 * kb:128 * kb + 128]
            t = P.op("pe", lambda e, o=o, i_=i_: e.transpose(o, i_, self.C("ident")),
                     [t] + P.bank_free[b] if kb == 0 else (), inc=kb == nb - 1)
        t2 = P.copy(aT[:, 0:128 * nb], self.ps[:, b, 0:128 * nb], [t] + free, eng="act")
        P.bank_free[b] = [t2]
        return t2, t

    def diff(self):
        P, d, scr = self.P, self.d, self.scr
        U = 4096
        self.rtmp = scr[:, 24064:24576]
        self.rc, self.rs = scr[:, 20480:20992], scr[:, 20992:21504]
        t_cs = P.dma("rope", scr[:, 20480:21504], d["rope"], P.done())
        lp = self.small[:, 100:102]
        P.tt(lp[:, 0:1], self.V("lambda", 0), self.V("lambda", 1), ALU.mult)
        t = P.tt(lp[:, 1:2], self.V("lambda", 2), self.V("lambda", 3), ALU.mult)
        b = P.bank()
        t = P.group(b, self.ps[:, b, 0:2], [(self.C("ones"), lp)], [t])
        t = P.act(lp, self.ps[:, b, 0:2], ACT.Exp, [t])
        P.bank_free[b] = [t]
        nl = self.small[:, 102:103]
        P.tt(nl, lp[:, 1:2], lp[:, 0:1], ALU.subtract, [t])
        P.ts(nl, nl, -0.2, None, ALU.add)
        sg8 = self.small[:, 103:104]
        P.ts(sg8, self.V("subln_g_2"), 0.8, None, ALU.mult)
        tu = self.norm_u("attn_norm_g_2", 0)
        q, k = fmat(scr[:, 0:U]), fmat(scr[:, U:2 * U])
        v = scr[:, 2 * U:3 * U].rearrange("p (t n) -> p t n", n=1024)
        o = fmat(scr[:, 3 * U:4 * U])
        tmps = [scr[:, 21504 + 512 * i:22016 + 512 * i] for i in range(5)]
        P.gate["dve"] = P.gate["dve"] + [t_cs]

        def evac(j, b, t):
            x = q[:, j, :] if j < 8 else k[:, j - 8, :]
            t = P.copy(x, self.bk(b), [t], eng="act")
            return self_rope(x, t) or t

        def self_rope(x, t):
            roped.append((x, t))

        roped = []
        self.gemm(d["w_qkv_a_2"], lambda kk: self.uT[:, kk, :], tu, evac, n_cols=2048)
        for x, t in roped:
            tr = self.rope(x, t, tmps[0])

        def view(c0):
            s, w, tw = self.w_tiles(d["w_qkv_a_2"], 2048 + c0, 2560 + c0)
            return (lambda kk: w[:, kk, :]), tw, s

        self.values_T(None, lambda kk: self.uT[:, kk, :], 8, 1024, v, [tr], view)
        ph = P.done()
        E = [[scr[:, 4 * U + 1024 * i:4 * U + 1024 * i + 512], scr[:, 4 * U + 1024 * i + 512:4 * U + 1024 * i + 1024]]
             for i in range(2)]
        aT = [scr[:, 4 * U + 2048 + 512 * i:4 * U + 2560 + 512 * i] for i in range(4)]
        at_free = [[] for _ in range(4)]
        e_free = [[], []]
        n = 0
        for hh in range(8):
            bo = None
            for qb in range(4):
                w = 128 * (qb + 1)
                qs = slice(128 * qb, 128 * qb + 128)
                ee = E[n % 2]
                st = [self.small[:, 104 + 8 * (n % 2):108 + 8 * (n % 2)], self.small[:, 108 + 8 * (n % 2):112 + 8 * (n % 2)]]
                for c in range(2):
                    p = slice(64 * c, 64 * c + 64)
                    b = P.bank()
                    P.mm(self.ps[:, b, 0:w], q[p, hh, qs], k[p, hh, 0:w], True, False, ph + P.bank_free[b])
                    t = P.mm(self.ps[:, b, 128 * qb:w], self.C("ident"), self.C("causal"), False, True, (), inc=True)
                    P.gate["act"] = P.gate["act"] + e_free[n % 2]
                    self.softmax_rows(b, w, 0.125, ee[c], st[c], t)
                P.ts(st[1][:, 3:4], st[1][:, 3:4], nl, None, ALU.mult)
                P.ts(ee[1][:, 0:w], ee[1][:, 0:w], st[1][:, 3:4], None, ALU.mult)
                t = P.stt(ee[0][:, 0:w], ee[0][:, 0:w], st[0][:, 3:4], ee[1][:, 0:w], ALU.mult, ALU.add)
                ta, tp = self.turn(ee[0], aT[n % 4], qb + 1, t, at_free[n % 4])
                e_free[n % 2] = [tp]
                b = P.bank()
                t = P.group(b, self.ps[:, b, 0:128], [(v[:, kb, 128 * hh:128 * hh + 128],
                                                       aT[n % 4][:, 128 * kb:128 * kb + 128]) for kb in range(qb + 1)],
                            [ta])
                at_free[n % 4] = [t]
                t = P.copy(o[:, hh, qs], self.ps[:, b, 0:128], [t], eng="act")
                P.bank_free[b] = [t]
                n += 1
            b = P.bank()
            t = P.act(tmps[1], o[:, hh, :], ACT.Square, [("pe", P.cnt["pe"])])
            t = P.group(b, self.bk(b), [(self.C("ones"), tmps[1])], [t])
            t = P.ts(tmps[2], self.bk(b), 1.0 / 128, 1e-5, ALU.mult, ALU.add, after=[t])
            P.bank_free[b] = [t]
            t = P.act(tmps[2], tmps[2], ACT.Sqrt, [t])
            P.recip(tmps[2], tmps[2], [t])
            to = P.stt(o[:, hh, :], o[:, hh, :], sg8, tmps[2], ALU.mult, ALU.mult)
        self.gemm(d["w_o_a_2"], lambda kk: o[:, kk, :], [to] * 8, self.add_x)
        P.phase()

    def mlp(self, l):
        P, d, scr = self.P, self.d, self.scr
        self.rtmp = scr[:, 24064:24576]
        up = fmat(scr[:, 0:16384])
        tu = self.norm_u("mlp_norm_g_2", 8 * l)
        rl = [scr[:, 16384 + 512 * i:16896 + 512 * i] for i in range(4)]

        def evac(j, b, t):
            t = P.act(rl[j % 4], self.bk(b), ACT.Relu, [t, ("dve", P.cnt["dve"])])
            self.t_up = P.tt(up[:, j, :], rl[j % 4], rl[j % 4], ALU.mult, [t])
            return t

        self.gemm(d[f"w_up_2_{l}"], lambda kk: self.uT[:, kk, :], tu, evac)
        W = d[f"w_down_2_{l}"]
        for nh in range(2):
            banks = [P.bank() for _ in range(4)]
            for kc in range(4):
                s, w, tw = P.load(4096, [(lambda a: a.rearrange("p (k n) -> p k n", n=512),
                                          W[1024 * kc:1024 * kc + 1024, 512 * nh:512 * nh + 512]
                                          .rearrange("(k p) n -> p k n", p=128))])
                w = w.rearrange("p (k n) -> p k n", n=512)
                for j, b in enumerate(banks):
                    for k in range(8):
                        t = P.mm(self.bk(b), w[:, k, 128 * j:128 * j + 128], up[:, 8 * kc + k, :],
                                 kc == 0 and k == 0, kc == 3 and k == 7,
                                 [tw, self.t_up] + (P.bank_free[b] if kc == 0 else []) if k == 0 else (), inc=k == 7)
                    if kc == 3:
                        P.bank_free[b] = [self.add_x(4 * nh + j, b, t)]
                P.slot_free[s] = [t]
        P.phase()

    def mla(self):
        P, d, scr = self.P, self.d, self.scr
        U = 4096
        self.rtmp = scr[:, 24064:24576]
        self.rc, self.rs = scr[:, 20480:20992], scr[:, 20992:21504]
        t_cs = P.dma("rope", scr[:, 20480:21504], d["rope"], P.done())
        tmps = [scr[:, 21504 + 512 * i:22016 + 512 * i] for i in range(5)]
        P.gate["dve"] = P.gate["dve"] + [t_cs]
        kn = fmat(scr[:, 0:U])
        v = scr[:, U:2 * U].rearrange("p (t n) -> p t n", n=1024)
        qn = fmat(scr[:, 2 * U:3 * U])
        qr = fmat(scr[:, 3 * U:3 * U + 2048])
        kr = fmat(scr[:, 3 * U + 2048:3 * U + 3072])
        c2 = fmat(scr[:, 3 * U + 3072:4 * U])
        cq = fmat(scr[:, 4 * U:4 * U + 1536])
        tu = self.norm_u("kv_in_norm_g_2", 0)
        W = d["w_dkv_2"].rearrange("(k p) n -> p k n", p=128)
        s, w, tw = P.load(8 * 384, [
            (lambda a: a.rearrange("p (k n) -> p k n", n=384)[:, :, 0:320], W),
            (lambda a: a.rearrange("p (k n) -> p k n", n=384)[:, :, 320:384], W[:, :, 256:320])])
        w = w.rearrange("p (k n) -> p k n", n=384)
        for j in range(3):
            b = P.bank()
            t = P.group(b, self.bk(b), [(w[:, k, 128 * j:128 * j + 128], self.uT[:, k, :]) for k in range(8)],
                        [tw] + tu)
            t2 = P.copy(c2[:, j, :] if j < 2 else tmps[1], self.bk(b), [t], eng="act")
            P.bank_free[b] = [t2]
        P.slot_free[s] = [t]
        tr = self.rope(tmps[1], t2, tmps[0])
        P.memset(kr, 0.0)
        P.copy(kr[0:64, 0, :], tmps[1][0:64, :])
        tk = P.copy(kr[64:128, 1, :], tmps[1][64:128, :])
        tc = self.rms(lambda i: c2[:, i, :], 2, 256, 1e-6, lambda i: self.V("kv_norm_g_2", i),
                      lambda i: (tmps[2], tmps[3])[i])
        cn = (tmps[2], tmps[3])
        Wk = d["w_ukv_2"].rearrange("(k p) n -> p k n", p=128)
        s, w, tw = P.load(4096, [(lambda a: a.rearrange("p (k n) -> p k n", n=2048), Wk)])
        w = w.rearrange("p (k n) -> p k n", n=2048)
        for j in range(8):
            b = P.bank()
            t = P.group(b, self.bk(b), [(w[:, k, 256 * j:256 * j + 128], cn[k]) for k in range(2)], [tw] + tc)
            t2 = P.copy(kn[:, j, :], self.bk(b), [t], eng="act" if j % 2 else "dve")
            P.bank_free[b] = [t2]
        wv = w.rearrange("p k (h n) -> p k h n", n=256)
        for c in range(2):
            for tt in range(4):
                b = P.bank()
                t = P.group(b, self.bk(b), [(cn[k][:, 128 * tt:128 * tt + 128], wv[:, k, 4 * c:4 * c + 4, 128:256])
                                            for k in range(2)])
                t2 = P.copy(v[:, tt, 512 * c:512 * c + 512], self.bk(b), [t], eng="act" if tt % 2 else "dve")
                P.bank_free[b] = [t2]
        P.slot_free[s] = [t]
        tu = self.norm_u("attn_norm_g_2", 8)
        s, w, tw = self.w_tiles(d["w_dq_2"], 0, 384)
        for j in range(3):
            b = P.bank()
            t = P.group(b, self.bk(b), [(w[:, k, 128 * j:128 * j + 128], self.uT[:, k, :]) for k in range(8)],
                        [tw] + tu)
            t2 = P.copy(cq[:, j, :], self.bk(b), [t], eng="act")
            P.bank_free[b] = [t2]
        P.slot_free[s] = [t]
        un = self.uT
        tc = self.rms(lambda i: cq[:, i, :], 3, 384, 1e-6, lambda i: self.V("q_norm_g_2", i),
                      lambda i: un[:, i, :], after=[t2, t])
        for half in range(2):
            Wq = d["w_uq_2"].rearrange("(k p) (h n) -> p k h n", p=128, n=192)[:, :, 4 * half:4 * half + 4, :]
            a3 = lambda a: a.rearrange("p (k n) -> p k n", n=768)
            s, w, tw = P.load(3 * 768, [
                (lambda a, k=k: a3(a)[:, k, 0:512].rearrange("p (h n) -> p h n", n=128), Wq[:, k, :, 0:128])
                for k in range(3)] + [
                (lambda a, k=k: a3(a)[:, k, 512:768].rearrange("p (h n) -> p h n", n=64), Wq[:, k, :, 128:192])
                for k in range(3)])
            w = a3(w)
            for j in range(4):
                b = P.bank()
                t = P.group(b, self.bk(b), [(w[:, k, 128 * j:128 * j + 128], un[:, k, :]) for k in range(3)], [tw] + tc)
                t2 = P.copy(qn[:, 4 * half + j, :], self.bk(b), [t], eng="act")
                P.bank_free[b] = [t2]
            for j in range(2):
                b = P.bank()
                t = P.group(b, self.bk(b), [(w[:, k, 512 + 128 * j:640 + 128 * j], un[:, k, :]) for k in range(3)])
                x = qr[:, 2 * half + j, :]
                t2 = P.copy(x, self.bk(b), [t], eng="act")
                P.bank_free[b] = [t2]
                tr = self.rope(x, t2, tmps[0])
            P.slot_free[s] = [t]
        ph = P.done()
        o = fmat(self.un)
        E = [scr[:, 4 * U + 512 * i:4 * U + 512 * i + 512] for i in range(2)]
        aT = [scr[:, 4 * U + 1024 + 512 * i:4 * U + 1536 + 512 * i] for i in range(4)]
        at_free = [[] for _ in range(4)]
        e_free = [[], []]
        scale = 192.0 ** -0.5
        n = 0
        for hh in range(8):
            for qb in range(4):
                w = 128 * (qb + 1)
                qs = slice(128 * qb, 128 * qb + 128)
                ee = E[n % 2]
                st = self.small[:, 104 + 4 * (n % 2):108 + 4 * (n % 2)]
                b = P.bank()
                P.mm(self.ps[:, b, 0:w], qn[:, hh, qs], kn[:, hh, 0:w], True, False, ph + P.bank_free[b])
                P.mm(self.ps[:, b, 0:w], qr[:, hh // 2, qs], kr[:, hh % 2, 0:w], False, False)
                t = P.mm(self.ps[:, b, 128 * qb:w], self.C("ident"), self.C("causal"), False, True, (), inc=True)
                P.gate["act"] = P.gate["act"] + ph + e_free[n % 2]
                self.softmax_rows(b, w, scale, ee, st, t)
                t = P.ts(ee[:, 0:w], ee[:, 0:w], st[:, 3:4], None, ALU.mult)
                ta, tp = self.turn(ee, aT[n % 4], qb + 1, t, at_free[n % 4])
                e_free[n % 2] = [tp]
                b = P.bank()
                t = P.group(b, self.ps[:, b, 0:128], [(v[:, kb, 128 * hh:128 * hh + 128],
                                                       aT[n % 4][:, 128 * kb:128 * kb + 128]) for kb in range(qb + 1)],
                            [ta])
                at_free[n % 4] = [t]
                t = P.copy(o[:, hh, qs], self.ps[:, b, 0:128], [t], eng="act")
                P.bank_free[b] = [t]
                n += 1
        self.gemm(d["w_o_b_2"], lambda kk: o[:, kk, :], [t] * 8, self.add_x)
        P.phase()

    def dump(self, outs, ap, name="out"):
        self.P.dma(name, outs, ap, self.P.done())

    def program(self, out, stop):
        xo = out.rearrange("(k p) n -> p k n", p=128)
        self.start()
        steps = [("mix", self.mixing), ("peer", self.peer), ("peern", lambda: self.norm_to_x(lambda i: self.V("final_g", i))),
                 ("h1", self.diff), ("h2", lambda: self.mlp(0)), ("h3", self.mla), ("h4", lambda: self.mlp(1)),
                 ("final", lambda: self.norm_to_x(lambda i: self.V("final_norm_g_2", i)))]
        skip = stop is not None and stop.startswith("only:")
        if stop == "only:peer":
            self.mod_cols(range(12))
        for name, step in steps:
            if skip and name != stop[5:]:
                continue
            step()
            if name == stop or skip:
                break
        self.dump(xo, self.xT)


def build(nc, dram, out, stop=None):
    with ExitStack() as ctx:
        dram = {**dram, "gates": nc.dram_tensor("gates", (16, 128, 4096), F32).ap()}
        n = Net(nc, ctx, dram, stop)
        P = n.P
        n.t_state = n.t_y = None
        n.program(out, stop)
        final = [(s, v) for s, v in P.cnt.items() if s.startswith("out")]
        P.q["sp"].append((final, lambda e: None, None, 0))
        block = ctx.enter_context(nc.Block())

        @block.sync
        def _(e):
            P.play("sp", e)

        @block.gpsimd
        def _(e):
            P.play("pool", e)

        @block.vector
        def _(e):
            P.play("dve", e)

        @block.scalar
        def _(e):
            P.play("act", e)

        @block.tensor
        def _(e):
            P.play("pe", e)


def columns(a):
    return a.reshape(-1, 128).T


def lay_out(x):
    z = {n: np.asarray(a) for n, a in x.items()}
    arr = {}
    arr["consts"], arr["rope"] = shape_constants()
    pack = []
    for n, w in VEC:
        if n == "conv_dw_w":
            a = z[n][0].reshape(CW, 4, 128).transpose(2, 1, 0).reshape(128, 4 * CW)
        elif n == "lambda":
            a = np.zeros((128, 4), np.float32)
            for i, m in enumerate(("lambda_q1_2", "lambda_k1_2", "lambda_q2_2", "lambda_k2_2")):
                a[0:64, i] = z[m][0]
        else:
            a = columns(z[n])
        assert a.shape == (128, w), n
        pack.append(a)
    arr["vecs"] = np.concatenate(pack, axis=1)
    arr["xT"] = z["x"][0].T
    for n in ("ada_w", "w_in", "rwkv_w2", "rwkv_a2", "rwkv_g2", "w_out", "peer_w_q", "peer_v", "w_qkv_a_2", "w_o_a_2",
              "w_dq_2", "w_uq_2", "w_o_b_2"):
        arr[n] = z[n][0]
    for n in ("w_dkv_2", "w_ukv_2"):
        arr[n] = z[n]
    for n in ("w_up_2", "w_down_2"):
        arr[n + "_0"], arr[n + "_1"] = z[n][0], z[n][1]
    arr["peer_uT"] = z["peer_u"][0].T
    arr["keysT"] = z["peer_sub_keys"][0].transpose(3, 0, 1, 2).reshape(128, 2048)
    return {n: np.ascontiguousarray(a) for n, a in arr.items()}


def kernel(**inputs):
    import concourse.bacc as bacc
    from concourse.bass_utils import run_bass_kernel_spmd

    nc = bacc.Bacc("TRN2", target_bir_lowering=False, num_devices=1)
    arrays, dram = {}, {}
    for n, a in lay_out(inputs).items():
        arrays["in_" + n] = a
        dram[n] = nc.dram_tensor("in_" + n, a.shape, F32, kind="ExternalInput").ap()
    out = nc.dram_tensor("out_x", (D, S), F32, kind="ExternalOutput").ap()
    build(nc, dram, out)
    r = run_bass_kernel_spmd(nc, [arrays], core_ids=[0])
    return np.ascontiguousarray(r.results[0]["out_x"].T)[None]
```

```python
from contextlib import ExitStack
import math

import numpy as np
import concourse.bass as bass
from concourse import mybir

F32 = mybir.dt.float32
F32R = mybir.dt.float32r
U32 = mybir.dt.uint32
ALU = mybir.AluOpType
ACT = mybir.ActivationFunctionType
AX = mybir.AxisListType.X

D, S, H = 1024, 512, 8
NEG = -1.0e30
NBANK = 8
NSLOT = 4
COLS = 53120
A_U = 5504
A_W0 = A_U + 8192
A_RAW = A_W0 + 8192
A_W2 = A_RAW + 8192
A_T = A_W2 + 8192
A_G = A_T + 8192
A_GEL = A_G + 4096
A_TMP = A_GEL + 2048
CW = 31
CDECAY = math.exp(-0.5)

CONST = ["ident", "ones", "bd", "rot", "iota", "causal", "strict", "incl", "m1",
         "t1", "t2", "t4", "t8", "t16", "t32"]
CCOL = {n: 128 * i for i, n in enumerate(CONST)}
NC1 = 768
NC2 = 128 * 9 + 512

VEC = [("c", 8), ("ada_b", 48), ("norm_mix_g", 8), ("conv_dw_w", 4 * CW), ("conv_dw_b", 4), ("conv_ln_w", 4),
       ("conv_ln_b", 4), ("rwkv_mu", 14), ("rwkv_w0", 4), ("rwkv_a0", 4), ("rwkv_k_k", 4), ("rwkv_k_a", 4),
       ("rwkv_r_k", 4), ("rwkv_gn_w", 4), ("rwkv_gn_b", 4), ("norm_ffn_g", 8), ("final_g", 8),
       ("attn_norm_g_2", 16), ("subln_g_2", 1), ("kv_in_norm_g_2", 8), ("kv_norm_g_2", 2), ("q_norm_g_2", 3),
       ("mlp_norm_g_2", 16), ("final_norm_g_2", 8), ("lambda", 4)]
VCOL = {}
NVEC = 0
for _n, _w in VEC:
    VCOL[_n] = NVEC
    NVEC += _w


def shape_constants():
    i = np.arange(128)
    r, c = i[:, None], i[None, :]
    same = (r // 64) == (c // 64)
    m = {"ident": r == c, "ones": np.ones((128, 128)), "bd": same, "iota": np.broadcast_to(c, (128, 128)),
         "causal": np.where(c <= r, 0.0, NEG), "strict": same & (r < c), "incl": same & (r <= c),
         "m1": (r // 2 == c // 2) & (r % 2 == 1) & (c % 2 == 0)}
    for b in (1, 2, 4, 8, 16, 32):
        m[f"t{b}"] = (r // (2 * b) == c // (2 * b)) & (r % (2 * b) < b) & (c % (2 * b) >= b)
    rot = np.zeros((128, 128))
    for o in (0, 64):
        for j in range(32):
            rot[o + 32 + j, o + j] = -1.0
            rot[o + j, o + 32 + j] = 1.0
    m["rot"] = rot
    scan = np.broadcast_to((np.arange(512) % 64 != 0), (128, 512))
    table = np.concatenate([np.asarray(m[n], np.float32) for n in CONST] + [scan.astype(np.float32)], axis=1)
    freq = (np.float32(10000.0) ** (-np.arange(0, 64, 2, dtype=np.float32) / np.float32(64))).astype(np.float32)
    ang = np.arange(S, dtype=np.float32)[None, :] * freq[:, None]
    cs = np.concatenate([np.tile(np.cos(ang), (4, 1)), np.tile(np.sin(ang), (4, 1))], axis=1).astype(np.float32)
    return np.ascontiguousarray(table), np.ascontiguousarray(cs)


TILES = {"ada_w": (2048, 24, 8), "w_in": (2048, 11, 8), "w_out": (2048, 4, 8), "peer_w_q": (2048, 8, 8),
         "peer_uT": (2048, 64, 8), "peer_v": (2048, 64, 2), "w_qkv_a_2": (2048, 12, 8), "w_o_a_2": (2048, 4, 8),
         "w_dkv_2": (1024, 3, 8), "ukv_k": (2048, 1, 2), "ukv_v": (2048, 1, 2), "w_dq_2": (1024, 3, 8),
         "uq_n": (1536, 2, 3), "uq_r": (1536, 1, 3), "w_o_b_2": (2048, 4, 8),
         "w_up_2_0": (2048, 16, 8), "w_up_2_1": (2048, 16, 8), "w_down_2_0": (2048, 16, 2),
         "w_down_2_1": (2048, 16, 2)}


def tiled(w, width, n, nk):
    if w.shape[0] == 128 * nk:
        return w.reshape(nk, 128, n, width // nk).transpose(2, 1, 0, 3).reshape(-1)
    return w.reshape(n, nk, 128, w.shape[1]).transpose(0, 2, 1, 3).reshape(-1)


class Prog:

    def __init__(self, nc, ctx):
        self.nc, self.ctx = nc, ctx
        self.q = {e: [] for e in ("pe", "act", "dve", "pool", "sp")}
        self.sem, self.cnt = {}, {}
        self.known = {e: {} for e in self.q}
        self.gate = {e: [] for e in self.q}
        for e in ("pe", "act", "dve", "pool"):
            self.new_sem(e)
        self.bank_free = [[] for _ in range(NBANK)]
        self.nbank = 0
        self.lag = 0

    def new_sem(self, name):
        self.sem[name] = self.ctx.enter_context(self.nc.semaphore("s_" + name))
        self.cnt[name] = 0

    def waits(self, eng, tokens):
        need = {}
        for t in tokens:
            if t is not None and self.known[eng].get(t[0], 0) < t[1]:
                need[t[0]] = max(need.get(t[0], 0), t[1])
        self.known[eng].update(need)
        return sorted(need.items())

    def op(self, eng, fn, after=(), inc=True):
        tokens = list(after) + self.gate[eng]
        self.gate[eng] = []
        if eng != "pe" and self.lag is not None:
            tokens.append((eng, self.cnt[eng] - self.lag))
        w = self.waits(eng, tokens)
        if inc:
            self.cnt[eng] += 1
        self.q[eng].append((w, fn, eng if inc else None, 1))
        return (eng, self.cnt[eng])

    def dma(self, sem, out, in_, after=(), eng="sp"):
        if sem not in self.sem:
            self.new_sem(sem)
        tokens = list(after) + self.gate[eng]
        self.gate[eng] = []
        w = self.waits(eng, tokens)
        self.cnt[sem] += 16
        self.q[eng].append((w, lambda e: e.dma_start(out, in_), sem, 16))
        return (sem, self.cnt[sem])

    def done(self):
        return [(e, self.cnt[e]) for e in ("pe", "act", "dve", "pool")]

    def phase(self):
        t = self.done()
        for e in ("pe", "act", "dve", "pool"):
            self.gate[e] = self.gate[e] + t
        return t

    def bank(self):
        b = self.nbank % NBANK
        self.nbank += 1
        return b

    def mm(self, out, lhsT, rhs, start, stop, after=(), inc=False):
        return self.op("pe", lambda e: e.matmul(out, lhsT, rhs, start=start, stop=stop), after, inc)

    def group(self, b, out, pairs, after=()):
        t = None
        for i, (l, r) in enumerate(pairs):
            t = self.mm(out, l, r, i == 0, i == len(pairs) - 1,
                        list(after) + self.bank_free[b] if i == 0 else (), inc=i == len(pairs) - 1)
        return t

    def tt(self, out, a, b, op, after=(), eng="dve"):
        return self.op(eng, lambda e: e.tensor_tensor(out, a, b, op), after)

    def ts(self, out, a, s1, s2, op0, op1=None, after=(), eng="dve"):
        if op1 is None:
            return self.op(eng, lambda e: e.tensor_scalar(out, a, s1, None, op0), after)
        return self.op(eng, lambda e: e.tensor_scalar(out, a, s1, s2, op0, op1), after)

    def stt(self, out, a, s, b, op0, op1, after=(), eng="dve"):
        return self.op(eng, lambda e: e.scalar_tensor_tensor(out=out, in0=a, scalar=s, in1=b, op0=op0, op1=op1), after)

    def act(self, out, in_, func, after=(), bias=0.0, scale=1.0, accum=None):
        if func == ACT.Copy:
            return self.op("act", lambda e: e.copy(out, in_), after)
        if accum is not None:
            return self.op("act", lambda e: e.activation(out, in_, func, bias=bias, scale=scale, accum_out=accum), after)
        return self.op("act", lambda e: e.activation(out, in_, func, bias=bias, scale=scale), after)

    def copy(self, out, in_, after=(), eng="dve"):
        if eng == "act":
            return self.op("act", lambda e: e.copy(out, in_), after)
        return self.op(eng, lambda e: e.tensor_copy(out, in_), after)

    def memset(self, out, v, after=(), eng="dve"):
        return self.op(eng, lambda e: e.memset(out, v), after)

    def recip(self, out, in_, after=()):
        return self.op("dve", lambda e: e.reciprocal(out, in_), after)

    def reduce(self, out, in_, op, after=()):
        return self.op("dve", lambda e: e.tensor_reduce(out, in_, AX, op), after)

    def play(self, name, e):
        for w, fn, sem, n in self.q[name]:
            for s, v in w:
                e.wait_ge(self.sem[s], v)
            ins = fn(e)
            if sem is not None:
                ins.then_inc(self.sem[sem], n)


def fmat(ap, n=512):
    return ap.rearrange("p (k n) -> p k n", n=n)


class Net:
    def __init__(self, nc, ctx, dram, stop):
        self.P = P = Prog(nc, ctx)
        self.d, self.stop_at = dram, stop
        base, total = 16512, COLS

        def plain(name, a0, a1):
            return nc.alloc_sbuf_tensor_at(name, [128, a1 - a0], F32, offset=base + 4 * a0)

        self.ps = ctx.enter_context(nc.psum_tensor("ps", [128, NBANK, 512], F32))
        m = plain("kept", 0, A_U)
        self.xT = fmat(m[:, 0:4096])
        self.const = m[:, 4096:4096 + NC1]
        at = 4096 + NC1
        self.vec = m[:, at:at + NVEC]
        self.modv = m[:, at + NVEC:at + NVEC + 48]
        self.small = m[:, at + NVEC + 48:at + NVEC + 304]
        assert at + NVEC + 304 <= A_U

        def split(name, at, n):
            return nc.alloc_sbuf_tensor_at(name, [128, n], F32R, offset=base + 4 * at)

        self.uh, self.ul = fmat(split("uh", A_U, 4096)[:, :]), fmat(split("ul", A_U + 4096, 4096)[:, :])
        self.wh, self.wl = [], []
        for i, o in enumerate((A_W0, A_W0 + 4096, A_W2, A_W2 + 4096)):
            self.wh.append(split(f"wh{i}", o, 2048)[:, :])
            self.wl.append(split(f"wl{i}", o + 2048, 2048)[:, :])
        self.th, self.tl = [], []
        for i in range(2):
            self.th.append(fmat(split(f"th{i}", A_T + 4096 * i, 2048)[:, :]))
            self.tl.append(fmat(split(f"tl{i}", A_T + 4096 * i + 2048, 2048)[:, :]))
        self.raw = [plain(f"raw{i}", A_RAW + 2048 * i, A_RAW + 2048 * i + 2048)[:, :] for i in range(4)]
        scr = plain("scratch", A_W2, total)
        self.rtmp = scr[:, A_TMP - A_W2:A_TMP - A_W2 + 512]
        self.scr = scr[:, 0:A_TMP - A_W2]
        self.gel = [scr[:, A_GEL - A_W2 + 512 * i:A_GEL - A_W2 + 512 * i + 512] for i in range(4)]
        self.raw_free, self.split_free = [[] for _ in range(4)], [[] for _ in range(4)]
        self.diag_free, self.lo_dve = [], 0
        self.un = plain("un", A_U, A_U + 8192)[:, :]
        self.w01 = plain("w01", A_W0, A_W0 + 8192)[:, :]

    def C(self, name):
        a = CCOL[name]
        return self.const[:, a:a + 128] if a < NC1 else self.masks[:, a - NC1:a - NC1 + 128]

    def V(self, name, i=0, n=1):
        return self.vec[:, VCOL[name] + i:VCOL[name] + i + n]

    def bk(self, b):
        return self.ps[:, b, :]

    def half(self, i):
        if i < 11:
            return self.scr[:, 2048 * i:2048 * (i + 1)]
        if i < 15:
            return self.un[:, 2048 * (i - 11):2048 * (i - 10)]
        return self.w01[:, 2048 * (i - 15):2048 * (i - 14)]

    def ring(self, raws, splits):
        self.raws, self.splits, self.nraw, self.nsplit = raws, splits, 0, 0

    def fetch(self, name, i):
        width, n = TILES[name][0], TILES[name][1]
        r = self.raws[self.nraw % len(self.raws)]
        self.nraw += 1
        at = i * 128 * width
        src = self.d[name][at:at + 128 * width].rearrange("(p w) -> p w", p=128)
        t = self.P.dma(f"raw{r}", self.raw[r][:, 0:width], src, self.raw_free[r])
        return r, width, t

    def load(self, n):
        while len(self.loaded) < n:
            self.loaded.append(self.fetch(*self.todo[len(self.loaded)]))

    def prepare(self, n):
        P = self.P
        self.load(n + 1)
        r, width, t = self.loaded[n]
        h = self.splits[self.nsplit % len(self.splits)]
        self.nsplit += 1
        wh, wl, w = self.wh[h][:, 0:width], self.wl[h][:, 0:width], self.raw[r][:, 0:width]
        t = P.act(wh, w, ACT.Copy, [t] + self.split_free[h])
        eng = "dve" if self.lo_dve and self.nsplit % self.lo_dve == 0 else "pool"
        t = P.tt(wl, w, wh.bitcast(F32), ALU.subtract, [t] + self.split_free[h], eng=eng)
        self.raw_free[r] = [t]
        return h, wh, wl, t

    def stream(self, todo, loads=0):
        self.todo, self.ready, self.taken, self.loaded = list(todo), [], 0, []
        if loads:
            self.load(loads)
        else:
            self.ahead(2, 0)

    def ahead(self, n, held=1):
        n = min(n, len(self.splits) - held)
        while len(self.ready) < min(len(self.todo), self.taken + n):
            self.ready.append(self.prepare(len(self.ready)))

    def take(self):
        self.ahead(1)
        c = self.ready[self.taken]
        self.taken += 1
        return c

    def split(self, hi, lo, x, after, eng="dve", bias=None):
        P = self.P
        if bias is None:
            t = P.act(hi, x, ACT.Copy, after)
            return P.tt(lo, x, hi.bitcast(F32), ALU.subtract, [t], eng=eng)
        t = P.act(hi, x, ACT.Identity, after, bias=bias)
        return P.stt(lo, x, bias, hi.bitcast(F32), ALU.add, ALU.subtract, [t])

    @staticmethod
    def terms(wh, wl, xh, xl):
        return [(wh, xh), (wh, xl), (wl, xh)]

    def rstd(self, b, stat, scale, eps, t):
        P = self.P
        t = P.ts(stat, stat, scale, eps, ALU.mult, ALU.add, [t])
        t = P.act(stat, stat, ACT.Sqrt, [t])
        t = P.recip(stat, stat, [t])
        return self.spread(b, stat)

    def spread(self, b, stat):
        P = self.P
        t = None
        for i in range(4):
            dg = self.rtmp[:, 128 * i:128 * i + 128]
            t = P.ts(dg, self.C("ident"), stat[:, i:i + 1], None, ALU.mult, after=self.diag_free)
            t = P.mm(self.ps[:, b, 128 * i:128 * i + 128], self.C("ones"), dg, True, True,
                     [t] + (P.bank_free[b] if i == 0 else []), inc=True)
        self.diag_free = [t]
        return t

    def squares(self, src, n, after=()):
        P = self.P
        acc, sq = self.gel[0], self.gel[1:3]
        sq_free = [[], []]
        for i in range(n):
            o = acc if i == 0 else sq[i % 2]
            t = P.act(o, src(i), ACT.Square, list(after) + sq_free[i % 2])
            if i:
                t = P.tt(acc, acc, o, ALU.add, [t])
                sq_free[i % 2] = [t]
        return self.token_sums(acc, self.small[:, 200:204], t)

    def token_sums(self, acc, stat, t):
        P = self.P
        b = P.bank()
        for i in range(4):
            t = P.mm(self.ps[:, b, i:i + 1], acc[:, 128 * i:128 * i + 128], self.C("ones")[:, 0:1], True, True,
                     [t] + P.bank_free[b] if i == 0 else (), inc=i == 3)
        t = P.copy(stat, self.ps[:, b, 0:4], [t])
        P.bank_free[b] = [t]
        return t

    def rms(self, src, n, dim, eps, gain, dst, after=(), t=None):
        P = self.P
        t = self.squares(src, n, after) if t is None else t
        b = P.bank()
        t = self.rstd(b, self.small[:, 200:204], 1.0 / dim, eps, t)
        out, free, made = [], [[], [], [], []], None
        for i in range(n + 1):
            y = self.gel[i % 4]
            if i < n:
                t = P.stt(y, src(i), gain(i), self.bk(b), ALU.mult, ALU.mult, [t] + free[i % 4])
                P.bank_free[b] = [t]
            if made is not None:
                out.append(dst(*made))
                free[made[0] % 4] = [out[-1]]
            made = (i, y, t)
        return out

    def head_rsqrt(self, sq, t, scale, eps, least, R):
        P = self.P
        stat = self.small[:, 204:236]
        b = P.bank()
        for q in range(4):
            for i in range(4):
                c = 8 * i + 2 * q
                t = P.mm(self.ps[:, b, c:c + 2], sq[:, q, 128 * i:128 * i + 128], self.C("bd")[:, 0:128:64], True, True,
                         [t] + P.bank_free[b] if q == i == 0 else (), inc=q == i == 3)
        if least is None:
            t = P.ts(stat, self.ps[:, b, 0:32], scale, eps, ALU.mult, ALU.add, [t])
        else:
            t = P.ts(stat, self.ps[:, b, 0:32], least, None, ALU.max, after=[t])
        P.bank_free[b] = [t]
        t = P.act(stat, stat, ACT.Sqrt, [t])
        P.recip(stat, stat, [t])
        banks = [P.bank() for _ in range(4)]
        free = [[], []]
        for i in range(4):
            r = R[i % 2]
            t = P.copy(r.rearrange("p (h n) -> p h n", n=64),
                       stat[:, 8 * i:8 * i + 8].unsqueeze(2).broadcast_to([128, 8, 64]), free[i % 2])
            for q in range(4):
                t = P.mm(self.ps[:, banks[q], 128 * i:128 * i + 128], r[:, 128 * q:128 * q + 128], self.C("ident"),
                         True, True, [t] + (P.bank_free[banks[q]] if i == 0 else []), inc=q == 3)
            free[i % 2] = [t]
        return banks, t

    def gemm(self, name, xh, xl, tok, evac, chunks=None, preset=False):
        P = self.P
        width, n, nk = TILES[name]
        cw = width // nk
        chunks = range(n) if chunks is None else chunks
        if not preset:
            self.stream([(name, c) for c in chunks])
        for c in chunks:
            h, wh, wl, tw = self.take()
            wh, wl = (a.rearrange("p (k n) -> p k n", n=cw) for a in (wh, wl))
            t = None
            for j in range(cw // 128):
                b = P.bank()
                s = slice(128 * j, 128 * j + 128)
                for k in range(nk):
                    for i, (l, r) in enumerate(self.terms(wh[:, k, s], wl[:, k, s], xh(k), xl(k))):
                        first, last = k == 0 and i == 0, k == nk - 1 and i == 2
                        after = ([tok[k]] if i == 0 else []) + ([tw] + P.bank_free[b] if first else [])
                        t = P.mm(self.bk(b), l, r, first, last, after, inc=last)
                if j == 0:
                    self.ahead(2)
                P.bank_free[b] = [evac(c * (cw // 128) + j, b, t)]
            self.split_free[h] = [t]
            self.ahead(2, 0)

    def mod_load(self, chunks, places, after=()):
        out = []
        for n, (ch, place) in enumerate(zip(chunks, places)):
            at = ch * 128 * 2048
            src = self.d["ada_w"][at:at + 128 * 2048].rearrange("(p w) -> p w", p=128)
            out.append((self.P.dma(f"ada{n}", place, src, after), place))
        return out

    def mod_product(self, w, t, eng):
        P = self.P
        c = self.small[:, 0:8].unsqueeze(2).broadcast_to([128, 8, 256])
        t = P.tt(w, w, c, ALU.mult, [t, self.t_silu], eng=eng)
        for m in (4, 2, 1):
            t = P.tt(w[:, 0:m, :], w[:, 0:m, :], w[:, m:2 * m, :], ALU.add, eng=eng)
        return t

    def mod_batch(self, chunks, loads=None, engines=()):
        P = self.P
        b = P.bank()
        for n, ch in enumerate(chunks):
            if loads is None:
                r, width, tw = self.fetch("ada_w", ch)
                w = self.raw[r]
            else:
                tw, w = loads[n]
            eng = engines[n] if n < len(engines) else "pe"
            w = w.rearrange("p (k n) -> p k n", n=256)
            if eng in ("dve", "pool"):
                tw = self.mod_product(w, tw, eng)
            for j in range(2):
                s = slice(128 * j, 128 * j + 128)
                pairs = [(w[:, k, s], self.small[:, k:k + 1]) for k in range(8)]
                if eng != "pe":
                    pairs = [(w[:, 0, s], self.C("ones")[:, 0:1])]
                t = P.group(b, self.ps[:, b, 2 * n + j:2 * n + j + 1], pairs, [tw, self.t_silu])
            if loads is None:
                self.raw_free[r] = [t]
        n, at = 2 * len(chunks), 2 * chunks[0]

        def finish():
            P.bank_free[b] = [P.tt(self.modv[:, at:at + n], self.ps[:, b, 0:n], self.V("ada_b", at, n), ALU.add, [t])]
            return P.bank_free[b][0]
        return finish

    def start(self):
        P = self.P
        d = self.d
        self.t_c = P.dma("cst", self.const, d["consts"])
        self.masks = self.raw[3]
        self.raw_free[3] = [self.t_c]
        self.scanm = self.raw[3][:, 1152:1664]
        self.t_c = P.dma("cst", self.masks[:, 0:NC2], d["masks"])
        self.raw_free[3] = [self.t_c]
        self.ring([0, 1, 2], [0, 1])
        self.t_v = P.dma("vec", self.vec, d["vecs"])
        self.t_x = P.dma("x", self.xT, d["xT"].rearrange("(k p) n -> p k n", p=128))
        self.t_silu = P.act(self.small[:, 0:8], self.V("c", 0, 8), ACT.Silu, [self.t_v])
        for e in ("pe", "act", "dve", "pool"):
            P.gate[e] = [self.t_c, self.t_v, self.t_x]

    def to_u(self, shift=None):
        def dst(i, y, t):
            return self.split(self.uh[:, i, :], self.ul[:, i, :], y, [t], bias=None if shift is None else shift(i))
        return dst

    def mixing(self):
        P, d = self.P, self.d
        h = self.half
        src = lambda i: self.xT[:, i, :]
        t_sq = self.squares(src, 8)
        t = self.mod_batch(range(8), self.mod_load(range(8), [h(i) for i in (0, 1, 2, 3, 4, 5, 7, 8)]),
                           ("pe", "pool", "dve", "dve", "pool", "dve", "pe", "dve"))()
        g1 = self.small[:, 8:16]
        t = P.stt(g1, self.modv[:, 8:16], 1.0, self.V("norm_mix_g", 0, 8), ALU.add, ALU.mult, [t])
        self.stream([("w_in", c) for c in (2, 3, 0, 1, 10, 6, 7, 4, 5, 8, 9)])
        self.ada = self.mod_load(range(8, 13), [h(i) for i in (1, 2, 3, 7, 5)], [t])
        tu = self.rms(src, 8, D, 1e-6, lambda i: g1[:, i:i + 1], self.to_u(lambda i: self.modv[:, i:i + 1]), t=t_sq)
        omu = self.small[:, 16:30]
        P.ts(omu, self.V("rwkv_mu", 0, 14), -1.0, 1.0, ALU.mult, ALU.add)
        oka = self.small[:, 30:34]
        P.ts(oka, self.V("rwkv_k_a", 0, 4), -1.0, 1.0, ALU.mult, ALU.add)
        r, k_, v = fmat(h(0)), fmat(h(10)), fmat(h(4))
        gated, conv, sig = fmat(h(9)), fmat(h(8)), fmat(h(10))
        lo = fmat(h(6)[:, 0:1024])
        w2a2, g2 = h(6)[:, 1024:1536], h(6)[:, 1536:2048]
        t_w2 = P.dma("w2", w2a2[0:64, :], d["rwkv_w2"])
        t_w2 = P.dma("w2", w2a2[64:128, :], d["rwkv_a2"])
        t_g2 = P.dma("g2", g2, d["rwkv_g2"])
        self.conv, self.gated = conv, gated
        self.conv_todo = [(i, sh) for i in range(4) for sh in range(1, CW)]
        self.sig_tok = {}

        def evac(j, b, t):
            if j in (0, 20, 12, 8, 16):
                n = (0, 20, 12, 8, 16).index(j)
                tw, w = self.ada[n]
                self.ada[n] = (self.mod_product(w.rearrange("p (k n) -> p k n", n=256), tw, "pool"), w)
            if 4 <= j < 8:
                self.sig_tok[j - 4] = P.act(sig[:, j - 4, :], self.bk(b), ACT.Sigmoid, [t, tu[-1]])
                return self.sig_tok[j - 4]
            if j < 4:
                t = P.tt(gated[:, j, :], self.bk(b), sig[:, j, :], ALU.mult, [t, self.sig_tok[j]])
                P.ts(conv[:, j, :], gated[:, j, :], self.V("conv_dw_w", CW * j + CW - 1), self.V("conv_dw_b", j),
                     ALU.mult, ALU.add)
                return t
            i = j - 8
            dst = (r, k_, v)[i // 4][:, i % 4, :] if i < 12 else lo[:, i - 12, :]
            t = P.ts(dst, self.bk(b), omu[:, i:i + 1], None, ALU.mult, after=[t, tu[-1]])
            t = P.stt(dst[:, 1:S], self.ps[:, b, 0:S - 1], self.V("rwkv_mu", i), dst[:, 1:S],
                      ALU.mult, ALU.add, [t])
            self.conv_some(7)
            return t

        uh, ul = (lambda k: self.uh[:, k, :]), (lambda k: self.ul[:, k, :])
        self.gemm("w_in", uh, ul, tu, evac, chunks=(2, 3, 0, 1, 10, 6, 7, 4, 5, 8, 9), preset=True)
        self.rwkv(r, k_, v, lo, w2a2, g2, t_w2, t_g2, oka)

    def conv_some(self, n):
        P = self.P
        for i, sh in self.conv_todo[:n]:
            P.stt(self.conv[:, i, sh:], self.gated[:, i, :S - sh], self.V("conv_dw_w", CW * i + CW - 1 - sh),
                  self.conv[:, i, sh:], ALU.mult, ALU.add)
        self.conv_todo = self.conv_todo[n:]

    def conv_norm(self, x2):
        P, conv = self.P, self.conv
        sq, mu = x2[:, 0:512], x2[:, 512:1024]
        b = P.bank()
        t = P.group(b, self.bk(b), [(self.C("ones"), conv[:, i, :]) for i in range(4)])
        t = P.ts(mu, self.bk(b), 1.0 / 512, None, ALU.mult, after=[t])
        P.bank_free[b] = [t]
        yield
        for i in range(4):
            t = P.tt(conv[:, i, :], conv[:, i, :], mu, ALU.subtract)
            yield
        for i in range(4):
            t = P.act(sq if i else mu, conv[:, i, :], ACT.Square, [t, ("dve", P.cnt["dve"])])
            if i:
                t = P.tt(mu, mu, sq, ALU.add, [t])
            yield
        stat = self.small[:, 236:240]
        t = self.token_sums(mu, stat, t)
        b = P.bank()
        t = self.rstd(b, stat, 1.0 / 512, 1e-5, t)
        t = P.copy(mu, self.bk(b), [t])
        P.bank_free[b] = [t]
        yield
        for i in range(4):
            t = P.tt(conv[:, i, :], conv[:, i, :], mu, ALU.mult)
            self.t_conv = P.act(conv[:, i, :], conv[:, i, :], ACT.Silu, [t], bias=self.V("conv_ln_b", i),
                                scale=self.V("conv_ln_w", i))
            yield

    def rwkv(self, r, k_, v, lo, w2a2, g2, t_w2, t_g2, oka):
        P, h = self.P, self.half
        sg, cum, a = fmat(h(11)), fmat(h(12)), fmat(h(13))
        kk, pd, pi = fmat(h(14)), fmat(h(15)), fmat(h(16))
        tmp, sq = fmat(h(17)), fmat(h(18))
        Rf, Af, Bf, Kf = r, fmat(h(1)), fmat(h(2)), fmat(h(3))
        g, bonus = fmat(h(5)), fmat(h(7))
        t_in = [("pe", P.cnt["pe"]), ("dve", P.cnt["dve"])]
        R = [h(17)[:, 0:512], h(17)[:, 512:1024]]
        self.mod_batch(range(13, 16))()
        for q in range(4):
            t_sq = P.act(sq[:, q, :], k_[:, q, :], ACT.Square, t_in, scale=self.V("rwkv_k_k", q))
        t0 = P.act(lo[0:64, 0, :], lo[0:64, 0, :], ACT.Tanh, t_in)
        t1 = P.act(lo[:, 1, :], lo[:, 1, :], ACT.Sigmoid)
        sums = []
        for q in range(4):
            c = slice(128 * q, 128 * q + 128)
            b = P.bank()
            t = P.group(b, self.bk(b), [(w2a2[0:64, c], lo[0:64, 0, :])], [t0, t_w2])
            t = P.act(sg[:, q, :], self.bk(b), ACT.Sigmoid, [t], bias=self.V("rwkv_w0", q))
            P.bank_free[b] = [t]
            cq, sq_ = cum[:, q, :], sg[:, q, :]
            P.op("dve", lambda e, cq=cq, sq_=sq_: e.tensor_tensor_scan(cq, self.scanm, sq_, 0.0, ALU.mult, ALU.add),
                 [t])
            b = P.bank()
            t = P.group(b, self.bk(b), [(w2a2[64:128, c], lo[64:128, 0, :])])
            t = P.act(a[:, q, :], self.bk(b), ACT.Sigmoid, [t], bias=self.V("rwkv_a0", q))
            P.bank_free[b] = [t]
        finish_ada = self.mod_batch(range(8, 13), self.ada, ["made"] * 5)
        for q in range(4):
            c = slice(128 * q, 128 * q + 128)
            b = P.bank()
            t = P.group(b, self.bk(b), [(g2[:, c], lo[:, 1, :])], [t1, t_g2])
            t = P.copy(g[:, q, :], self.bk(b), [t], eng="act")
            P.bank_free[b] = [t]
        self.conv_some(len(self.conv_todo))
        finish_ada()
        tc = P.tt(sg, cum, sg, ALU.subtract)
        banks, t_rs = self.head_rsqrt(sq, t_sq, None, None, 1e-24, R)
        t_i = P.act(pi, cum, ACT.Exp, [tc], scale=CDECAY)
        t_pp = P.act(sg, sg, ACT.Exp, scale=-CDECAY)
        t_p = P.act(pd, cum, ACT.Exp, scale=-CDECAY)
        finish = self.mod_batch(range(16, 18), None, ["pool"] * 2)
        for q in range(4):
            t = P.stt(kk[:, q, :], k_[:, q, :], self.V("rwkv_k_k", q), self.bk(banks[q]), ALU.mult, ALU.mult, [t_rs])
            P.bank_free[banks[q]] = [t]
        finish()
        P.tt(Bf, kk, a, ALU.mult)
        P.tt(Bf, Bf, pi, ALU.mult, [t_i])
        for q in range(4):
            P.ts(tmp[:, q, :], a[:, q, :], self.V("rwkv_k_a", q), oka[:, q:q + 1], ALU.mult, ALU.add)
        t_k = P.tt(k_, k_, tmp, ALU.mult)
        P.tt(Kf, k_, pi, ALU.mult, [t_k, t_i], eng="pool")
        P.stt(Af, kk, -1.0, sg, ALU.mult, ALU.mult, [t_pp])
        bank = []
        for q in range(4):
            t = P.stt(tmp[:, q, :], r[:, q, :], self.V("rwkv_r_k", q), k_[:, q, :], ALU.mult, ALU.mult)
            b = P.bank()
            bank.append((b, P.group(b, self.bk(b), [(self.C("bd"), tmp[:, q, :])], [t])))
        P.tt(Rf, r, pd, ALU.mult, [t_p])
        finish = self.mod_batch(range(18, 20), None, ["pool"] * 2)
        pc = self.small[:, 64:96]
        P.copy(pc.rearrange("p (q c) -> p q c", q=4), pd[:, :, 63:512:64])
        for q in range(4):
            t = P.tt(bonus[:, q, :], self.bk(bank[q][0]), v[:, q, :], ALU.mult, [bank[q][1]])
            P.bank_free[bank[q][0]] = [t]
        finish()
        if self.stop_at == "rprep":
            return
        y = fmat(h(6))
        self.chunks(Rf, Af, Bf, Kf, v, pc, y)
        sq, yc = fmat(h(10)), fmat(h(1))
        R = [h(2)[:, 0:512], h(2)[:, 512:1024]]
        ph = P.phase()
        self.split_free = [f + ph for f in self.split_free]
        self.raw_free = [f + ph for f in self.raw_free]
        self.stream([("w_out", c) for c in range(4)])
        toks = [None] * 8
        conv = self.conv
        for q in range(4):
            b = P.bank()
            t = P.group(b, self.bk(b), [(self.C("bd"), y[:, q, :])])
            t = P.stt(yc[:, q, :], self.bk(b), -1.0 / 64, y[:, q, :], ALU.mult, ALU.add, [t])
            P.bank_free[b] = [t]
            t_sq = P.act(sq[:, q, :], yc[:, q, :], ACT.Square, [t])
        for i in range(4):
            toks[i] = self.split(self.uh[:, i, :], self.ul[:, i, :], conv[:, i, :], [])
        banks, t = self.head_rsqrt(sq, t_sq, 1.0 / 64, 64e-5, None, R)
        for q in range(4):
            t = P.stt(yc[:, q, :], yc[:, q, :], self.V("rwkv_gn_w", q), self.bk(banks[q]), ALU.mult, ALU.mult, [t])
            P.bank_free[banks[q]] = [t]
            P.stt(yc[:, q, :], yc[:, q, :], self.V("rwkv_gn_b", q), bonus[:, q, :], ALU.add, ALU.add)
            t = P.tt(y[:, q, :], yc[:, q, :], g[:, q, :], ALU.mult)
            toks[4 + q] = self.split(self.uh[:, 4 + q, :], self.ul[:, 4 + q, :], y[:, q, :], [t])

        def evac(j, b, t):
            return P.stt(self.xT[:, j, :], self.bk(b), self.modv[:, 16 + j:17 + j], self.xT[:, j, :],
                         ALU.mult, ALU.add, [t])

        self.gemm("w_out", lambda k: self.uh[:, k, :], lambda k: self.ul[:, k, :], toks, evac, preset=True)
        end = P.phase()
        self.split_free = [f + end for f in self.split_free]
        self.raw_free = [f + end for f in self.raw_free]

    def chunks(self, Rf, Af, Bf, Kf, v, pc, y):
        P, h = self.P, self.half
        mats = []
        for m in [h(i) for i in range(9, 18)] + self.raw[0:3]:
            mats += [m[:, 0:1024], m[:, 1024:2048]]
        sets = [mats[0:9], mats[9:18]]
        Bb, KM, VW, MT, X, spare = mats[18:24]
        st = [h(18)[:, 0:512], h(18)[:, 512:1024]]
        Z, SA = h(18)[:, 1024:1536], h(18)[:, 1536:2048]
        P.phase()
        for e, ms in (("pool", (Bb, KM, VW)), ("dve", (sets[0][0], sets[0][1])),
                      ("pool", (sets[1][0], sets[1][1], st[0]))):
            for m in ms:
                P.memset(m, 0.0, eng=e)
        zero = [("pool", P.cnt["pool"]), ("dve", P.cnt["dve"])]
        self.t_state = self.t_y = None
        ident = self.C("ident")

        def m4(ap):
            return ap.rearrange("p (u n) -> p u n", n=128)

        def bc(c):
            return c.unsqueeze(1).broadcast_to([128, 4, 128])

        inverse, ran = {}, {}

        def invert(g):
            Ab, Rb, TB, TK, TV, XT, NT, RBT, RKT = sets[g % 2]
            t_bd = []
            own = zero + ran.get(g - 2, [])
            shared = zero + inverse.get(g - 1, [])
            for n, (src, dst, free) in enumerate(((Bf, Bb, shared), (Af, Ab, own), (Kf, KM, shared), (v, VW, shared),
                                                  (Rf, Rb, own))):
                for hd in range(2):
                    p = slice(64 * hd, 64 * hd + 64)
                    for cc in range(2):
                        o = m4(dst)[p, 4 * cc:4 * cc + 4, 64 * hd:64 * hd + 64]
                        s = src[p, :, 64 * (2 * g + cc):64 * (2 * g + cc) + 64]
                        eng = ("act", "dve", "act", "pool", "dve")[n]
                        ld = P.copy(o, s, free, eng=eng)
                t_bd.append(ld)
            yield

            def product(l, rr, dst, mask, after):
                for cc in range(2):
                    b = P.bank()
                    for q in range(4):
                        u = 4 * cc + q
                        t = P.mm(self.ps[:, b, 128 * q:128 * q + 128], m4(l)[:, u, :], m4(rr)[:, u, :], True, True,
                                 after + P.bank_free[b] if q == 0 else (), inc=q == 3)
                    o = dst[:, 512 * cc:512 * cc + 512]
                    t = P.tt(m4(o), m4(self.bk(b)), bc(mask), ALU.mult, [t] + own)
                    P.bank_free[b] = [t]
                    tl.append(t)
                    yield

            tl = []
            yield from product(Bb, Ab, MT, self.C("strict"), t_bd[0:2])
            tm = list(tl)
            yield from product(Ab, Bb, X, self.C("m1"), [])
            t_x = {}
            for cc in range(2):
                c = slice(512 * cc, 512 * cc + 512)
                P.tt(m4(X[:, c]), m4(X[:, c]), bc(ident), ALU.add)
                P.tt(m4(XT[:, c]), m4(MT[:, c]), bc(self.C("t1")), ALU.mult)
                t_x[cc] = P.tt(m4(XT[:, c]), m4(XT[:, c]), bc(ident), ALU.add)
                yield
            for src, dst, ready in ((Bb, TB, []), (KM, TK, [t_bd[2]]), (VW, TV, [t_bd[3]])):
                for cc in range(2):
                    b = P.bank()
                    for q in range(4):
                        u = 4 * cc + q
                        o, i_ = self.ps[:, b, 128 * q:128 * q + 128], m4(src)[:, u, :]
                        t = P.op("pe", lambda e, o=o, i_=i_: e.transpose(o, i_, ident),
                                 ready + P.bank_free[b] if q == 0 else (), inc=q == 3)
                    t = P.copy(dst[:, 512 * cc:512 * cc + 512], self.bk(b), [t] + own, eng="act")
                    P.bank_free[b] = [t]
                    yield
            t_tr = t
            yield from product(KM, Ab, NT, self.C("strict"), [])
            yield from product(KM, Rb, RKT, self.C("incl"), [t_bd[4]])
            t_pe = [t_tr, ("pe", P.cnt["pe"])]
            t_pe = {0: list(t_pe), 1: list(t_pe)}
            extra = product(Bb, Rb, RBT, self.C("incl"), [])
            for lv in (2, 4, 8, 16, 32):
                tw = {}
                for cc in range(2):
                    c = slice(512 * cc, 512 * cc + 512)
                    t = P.tt(m4(KM[:, c]), m4(MT[:, c]), bc(self.C(f"t{lv}")), ALU.mult, tm + t_pe[cc], eng="pool")
                    b = P.bank()
                    for q in range(4):
                        u = 4 * cc + q
                        tp = P.mm(self.ps[:, b, 128 * q:128 * q + 128], m4(KM)[:, u, :], m4(X)[:, u, :], True, True,
                                  [t, t_x[cc]] + P.bank_free[b] if q == 0 else (), inc=q == 3)
                    tw[cc] = P.copy(VW[:, c], self.bk(b), [tp], eng="act")
                    P.bank_free[b] = [tw[cc]]
                    yield
                if lv == 2:
                    yield from extra
                for cc in range(2):
                    c = slice(512 * cc, 512 * cc + 512)
                    done = []
                    for l, rr, dst in ([(XT, VW, X), (VW, XT, XT)] if lv < 32 else [(VW, XT, XT)]):
                        b = P.bank()
                        for q in range(4):
                            u = 4 * cc + q
                            tp = P.mm(self.ps[:, b, 128 * q:128 * q + 128], m4(l)[:, u, :], m4(rr)[:, u, :],
                                      True, True, [tw[cc]] + P.bank_free[b] if q == 0 else (), inc=q == 3)
                        done.append((b, tp, dst))
                    for b, tp, dst in done:
                        t_x[cc] = P.tt(dst[:, c], dst[:, c], self.bk(b), ALU.add, [tp, done[-1][1]])
                        P.bank_free[b] = [t_x[cc]]
                    t_pe[cc] = [done[-1][1]]
                    yield
            self.t_inverse = {g: dict(t_x), **{k: w for k, w in self.t_inverse.items() if k == g - 1}}
            inverse[g] = [("pe", P.cnt["pe"]), ("dve", P.cnt["dve"])]

        def run(g):
            Ab, Rb, TB, TK, TV, XT, NT, RBT, RKT = sets[g % 2]
            t_x = self.t_inverse[g]
            for cc in range(2):
                ch = 2 * g + cc
                S0, S1 = st[ch % 2], st[1 - ch % 2]
                b = P.bank()
                for q in range(4):
                    u = 4 * cc + q
                    o = self.ps[:, b, 128 * q:128 * q + 128]
                    P.mm(o, m4(NT)[:, u, :], m4(TV)[:, u, :], True, False,
                         P.bank_free[b] + zero + [self.t_state] + inverse[g] if q == 0 else ())
                    t = P.mm(o, m4(Ab)[:, u, :], m4(S0)[:, q, :], False, True, (), inc=q == 3)
                tz = P.copy(Z, self.bk(b), [t], eng="act")
                P.bank_free[b] = [tz]
                yield
                b = P.bank()
                for q in range(4):
                    u = 4 * cc + q
                    t = P.mm(self.ps[:, b, 128 * q:128 * q + 128], m4(XT)[:, u, :], m4(Z)[:, q, :], True, True,
                             [tz, t_x[cc]] + P.bank_free[b] if q == 0 else (), inc=q == 3)
                ts = P.copy(SA, self.bk(b), [t, self.t_y])
                P.bank_free[b] = [ts]
                yield
                b = P.bank()
                for q in range(4):
                    u = 4 * cc + q
                    o = self.ps[:, b, 128 * q:128 * q + 128]
                    P.mm(o, ident, m4(S0)[:, q, :], True, False, P.bank_free[b] if q == 0 else ())
                    P.mm(o, m4(TK)[:, u, :], m4(TV)[:, u, :], False, False)
                    t = P.mm(o, m4(TB)[:, u, :], m4(SA)[:, q, :], False, True, [ts], inc=q == 3)
                pcc = pc.rearrange("p (q c) -> p q c", q=4)[:, :, ch:ch + 1].broadcast_to([128, 4, 128])
                self.t_state = P.tt(m4(S1), m4(self.bk(b)), pcc, ALU.mult, [t, self.t_y])
                P.bank_free[b] = [self.t_state]
                yield
                b = P.bank()
                for q in range(4):
                    u = 4 * cc + q
                    o = self.ps[:, b, 128 * q:128 * q + 128]
                    P.mm(o, m4(S0)[:, q, :], m4(Rb)[:, u, :], True, False, P.bank_free[b] if q == 0 else ())
                    P.mm(o, m4(TV)[:, u, :], m4(RKT)[:, u, :], False, False)
                    t = P.mm(o, m4(SA)[:, q, :], m4(RBT)[:, u, :], False, True, (), inc=q == 3)
                self.t_y = t
                for hd in range(2):
                    p = slice(64 * hd, 64 * hd + 64)
                    t = P.copy(y[p, :, 64 * ch:64 * ch + 64],
                               m4(self.bk(b))[p, :, 64 * hd:64 * hd + 64], [t], eng="act")
                P.bank_free[b] = [t]
                yield
            ran[g] = [self.t_y]

        self.t_inverse = {}
        norm = self.conv_norm(spare)
        for _ in invert(0):
            next(norm, None)
        for _ in norm:
            pass
        for g in range(4):
            inv = invert(g + 1) if g < 3 else iter(())
            for _ in run(g):
                for _ in range(4):
                    next(inv, None)
            for _ in inv:
                pass

    def peer(self):
        P, d = self.P, self.d
        scr = self.scr
        U = 4096
        self.ring([0, 1, 2, 3], [0, 1])
        self.stream([("peer_w_q", c) for c in range(8)])
        gf = self.small[:, 8:16]
        P.stt(gf, self.modv[:, 32:40], 1.0, self.V("norm_ffn_g", 0, 8), ALU.add, ALU.mult)
        tu = self.rms(lambda i: self.xT[:, i, :], 8, D, 1e-6, lambda i: gf[:, i:i + 1],
                      self.to_u(lambda i: self.modv[:, 24 + i:25 + i]))
        qF = fmat(scr[:, 0:2 * U])
        keys = scr[:, 2 * U:2 * U + 2048]
        t_keys = P.dma("keys", keys, d["keysT"], P.done())

        def evac(j, b, t):
            return P.copy(qF[:, j, :], self.bk(b), [t], eng="act" if j % 2 else "dve")

        self.gemm("peer_w_q", lambda k: self.uh[:, k, :], lambda k: self.ul[:, k, :], tu, evac, preset=True)
        t_q = P.done()
        base = 2 * U + 2048
        sc = scr[:, base:base + 2048].rearrange("p (j n) -> p j n", n=128)
        base += 2048
        cand = scr[:, base:base + 2048].rearrange("p (h a b) -> p h a b", h=8, a=16)
        base += 2048
        eq = sc.rearrange("p j n -> p (j n)").rearrange("p (h a b) -> p h a b", h=8, a=16)
        sm = []
        for w in (256, 256, 256, 128, 128, 128, 128, 128, 128, 128, 8, 8):
            sm.append(scr[:, base:base + w])
            base += w
        vals, idxu, idxf, best, posu, tmpu, ai, bi, i1, i2, s8, m8 = sm
        gate = tmpu
        IA, IB, WG = (scr[:, base + 512 * i:base + 512 * i + 512] for i in range(3))
        NA, NW = self.raw[0][:, 0:512], self.raw[0][:, 512:1024]
        base += 1536
        gk = scr[:, base:base + 128]
        base += 128
        it16 = self.C("iota")[:, 0:16]
        v3 = vals.rearrange("p (j k) -> p j k", k=16)
        x3 = idxu.bitcast(U32).rearrange("p (j k) -> p j k", k=16)
        f4 = idxf.rearrange("p (h two k) -> p h two k", two=2, k=16)
        v4 = vals.rearrange("p (h two k) -> p h two k", two=2, k=16)
        b3 = best.rearrange("p (h k) -> p h k", k=16)
        p3 = posu.bitcast(U32).rearrange("p (h k) -> p h k", k=16)

        def top16(rows):
            P.lag = 1
            for half in range(2):
                parts = [(s_, v_[:, 8 * half:8 * half + 8], i_[:, 8 * half:8 * half + 8]) for s_, v_, i_ in rows]
                for s_, vv, ii in parts:
                    P.op("dve", lambda e, s_=s_, vv=vv: e.max(vv, s_))
                for s_, vv, ii in parts:
                    P.op("dve", lambda e, s_=s_, vv=vv, ii=ii: e.max_index(ii, vv, s_))
                if half == 0:
                    for s_, vv, ii in parts:
                        P.op("dve", lambda e, s_=s_, vv=vv: e.match_replace(s_, vv, s_, -3.0e38))
            P.lag = 0

        def choose(tt):
            ts_ = slice(128 * tt, 128 * tt + 128)
            t_sc = []
            for j0 in range(0, 16, 4):
                b = P.bank()
                for j in range(j0, j0 + 4):
                    t = P.mm(self.ps[:, b, 128 * (j - j0):128 * (j - j0) + 128], qF[:, j, ts_],
                             keys[:, 128 * j:128 * j + 128], True, True,
                             t_q + [t_keys] + P.bank_free[b] if j == j0 else (), inc=j == j0 + 3)
                t = P.copy(sc[:, j0:j0 + 4, :], self.bk(b), [t, ("dve", P.cnt["dve"])], eng="act")
                P.bank_free[b] = [t]
                t_sc.append(t)
            for j in range(0, 16, 2):
                P.gate["dve"] = P.gate["dve"] + [t_sc[j // 4]]
                top16([(sc[:, i, :], v3[:, i, :], x3[:, i, :]) for i in (j, j + 1)])
                yield
                yield
            P.copy(idxf, idxu.bitcast(U32))
            for h0 in range(0, 8, 2):
                for hh in (h0, h0 + 1):
                    P.tt(cand[:, hh], v4[:, hh, 0, :].unsqueeze(2).broadcast_to([128, 16, 16]),
                         v4[:, hh, 1, :].unsqueeze(1).broadcast_to([128, 16, 16]), ALU.add)
                    P.lag = 1
                top16([(cand[:, hh].rearrange("p a b -> p (a b)"), b3[:, hh, :], p3[:, hh, :])
                       for hh in (h0, h0 + 1)])
                yield
                yield
            g3 = gate.rearrange("p (h k) -> p h k", k=16)
            t = P.tt(g3, b3, b3[:, :, 0:1].broadcast_to([128, 8, 16]), ALU.subtract, self.t_turned)
            t = P.act(gate, gate, ACT.Exp, [t])
            a_u, b_u = ai.bitcast(U32), bi.bitcast(U32)
            pu = posu.bitcast(U32)
            P.ts(a_u, pu, 4, None, ALU.logical_shift_right)
            P.ts(b_u, pu, 15, None, ALU.bitwise_and)
            P.reduce(s8, g3, ALU.add, [t])
            P.recip(s8, s8)
            tg = P.tt(g3, g3, s8.unsqueeze(2).broadcast_to([128, 8, 16]), ALU.mult)
            for src, side, dst in ((a_u, 0, i1), (b_u, 1, i2)):
                P.copy(gk, src)
                P.tt(eq, gk.rearrange("p (h k) -> p h k", k=16).unsqueeze(3).broadcast_to([128, 8, 16, 16]),
                     it16.unsqueeze(1).unsqueeze(1).broadcast_to([128, 8, 16, 16]), ALU.is_equal)
                yield
                P.tt(eq, eq, f4[:, :, side, :].unsqueeze(2).broadcast_to([128, 8, 16, 16]), ALU.mult)
                yield
                ti = P.reduce(dst.rearrange("p (h k) -> p h k", k=16), eq, ALU.add)
                yield
            b = P.bank()
            for n, src in enumerate((i1, i2, gate)):
                o = self.ps[:, b, 128 * n:128 * n + 128]
                t = P.op("pe", lambda e, o=o, src=src: e.transpose(o, src, self.C("ident")),
                         [ti, tg] + P.bank_free[b] if n == 0 else (), inc=n == 2)
            self.t_turned = [t]
            for n, dst in enumerate((IA, IB, WG)):
                t = P.copy(dst[:, ts_], self.ps[:, b, 128 * n:128 * n + 128], [t], eng="act")
            for src, dst in ((0, NA), (2, NW)):
                t = P.act(dst[:, ts_], self.ps[:, b, 128 * src:128 * src + 128], ACT.Identity, [t] + t_q, scale=-1.0)
            P.bank_free[b] = [t]
            self.t_choice[tt] = t
            yield

        G = d["gates"]
        stage = [self.w01[:, 0:U].rearrange("p (k t) -> p k t", t=32),
                 self.w01[:, U:2 * U].rearrange("p (k t) -> p k t", t=32)]
        st_free = [t_q, t_q]
        oh = [scr[:, base + 1024 * i:base + 1024 * i + 1024] for i in range(3)]
        assert base + 3072 <= 22528
        oh_free = [[] for _ in range(3)]
        iota = self.C("iota")
        t_store = []

        def put_down():
            if self.placed is None:
                return
            blk, q, b, t = self.placed
            self.placed, s = None, blk % 2
            t = P.copy(stage[s][:, :, 4 * q:4 * q + 4].rearrange("p k t -> p t k"),
                       self.bk(b).rearrange("p (t k) -> p t k", k=128), [t] + st_free[s], eng="act")
            P.bank_free[b] = [t]
            if q == 7:
                st_free[s] = [P.dma(f"gst{s}", G[blk], stage[s].rearrange("p k t -> p (k t)"), [t])]
                t_store.append(st_free[s][0])

        self.placed, self.put_down = None, put_down

        def place(tt, b_dve, acts):
            for blk in range(4 * tt, 4 * tt + 4):
                for q in range(8):
                    n = blk * 8 + q
                    o = oh[n % 3]
                    B4, A4 = o[:, 0:512], o[:, 512:1024]
                    t0 = blk * 32 + 4 * q
                    free = oh_free[n % 3] + [self.t_choice[tt]]
                    tb = []
                    P.lag = None
                    if q % 8 in b_dve:
                        tb.append(P.tt(B4.rearrange("p (t n) -> p t n", n=128),
                                       iota.unsqueeze(1).broadcast_to([128, 4, 128]),
                                       IB[:, t0:t0 + 4].unsqueeze(2).broadcast_to([128, 4, 128]),
                                       ALU.is_equal, after=free))
                    else:
                        for i in range(4):
                            tb.append(P.ts(B4[:, 128 * i:128 * i + 128], iota, IB[:, t0 + i:t0 + i + 1], None,
                                           ALU.is_equal, after=free, eng="pool"))
                    on_act = acts[q % len(acts)]
                    ta = []
                    for i in range(on_act):
                        ta = [P.act(A4[:, 128 * i:128 * i + 128], iota, ACT.Abs, free,
                                    bias=NA[:, t0 + i:t0 + i + 1])]
                    for i in range(on_act):
                        A1, col = A4[:, 128 * i:128 * i + 128], slice(t0 + i, t0 + i + 1)
                        tr = P.act(A1, A1, ACT.Relu, ta, bias=WG[:, col], scale=NW[:, col])
                    if on_act:
                        tb.append(tr)
                    for i in range(on_act, 4):
                        A1, col = A4[:, 128 * i:128 * i + 128], slice(t0 + i, t0 + i + 1)
                        ta = P.ts(A1, iota, IA[:, col], WG[:, col], ALU.is_equal, ALU.mult, after=free)
                    P.lag = 0
                    self.put_down()
                    b = P.bank()
                    for i in range(4):
                        c = slice(128 * i, 128 * i + 128)
                        t = P.mm(self.ps[:, b, c], B4[:, c], A4[:, c], True, True,
                                 [ta] + tb + P.bank_free[b] if i == 0 else (), inc=i == 3)
                    oh_free[n % 3] = [t]
                    self.placed = (blk, q, b, t)
                    yield

        self.t_turned, self.t_choice = [], {}
        self.ring([1, 2, 3], [])
        for n, _ in enumerate(choose(0)):
            if n == 8:
                finish = self.mod_batch(range(20, 24))
        finish()
        rest = (s for tt in range(1, 4) for s in choose(tt))
        places = (s for tt in range(4) for s in place(tt, *(((0,), (2, 2, 3, 2)) if tt < 3 else ((0, 2, 4, 6), (1,)))))
        for _ in rest:
            next(places)
        self.dense_stream("peer_uT", "peer_v", 32, (1, 2, 3, 0), (2, 3, 0, 1), 2)
        for i in (2, 3):
            self.split_free[i] = self.split_free[i] + P.done()
        for n, _ in enumerate(places):
            if n in (6, 12):
                self.ready.append(self.prepare(len(self.ready)))
            pass
        put_down()
        ph = P.phase()
        self.gates, self.t_gates, self.gate_ready = G.rearrange("b p (k t) -> p b k t", t=32), t_store[-2:], ph
        for i in (0, 1):
            self.split_free[i] = self.split_free[i] + ph
        self.raw_free[0] = self.raw_free[0] + ph
        self.dense("peer_uT", "peer_v", 32, True, lambda j: self.modv[:, 40 + j:41 + j], [], True)
        P.phase()

    def dense_stream(self, first, second, groups, raws=(0, 1, 2, 3), splits=(0, 1, 2, 3), loads=0):
        self.ring(raws, splits)
        order = [(first, 0), (first, 1)]
        for g in range(groups):
            if g + 1 < groups:
                order += [(first, 2 * g + 2), (first, 2 * g + 3)]
            order += [(second, 2 * g), (second, 2 * g + 1)]
        self.stream(order, loads)

    def dense(self, first, second, groups, gated, scale, tok, preset=False):
        P = self.P
        if not preset:
            self.dense_stream(first, second, groups)
        Gt = [self.scr[:, A_G - A_W2 + 2048 * i:A_G - A_W2 + 2048 * i + 2048] for i in range(2)]
        gt_free = [[], []]
        gel_free = [list(tok) for _ in range(4)]
        th_free = [list(tok), list(tok)]

        def scores(g):
            s2 = g % 2
            if gated:
                tg = P.dma(f"gld{s2}", Gt[s2].rearrange("p (b k) -> p b k", b=16),
                           self.gates[:, :, 4 * g:4 * g + 4, :].rearrange("p b k t -> p b (k t)"),
                           self.t_gates + self.gate_ready + gt_free[s2])
                gv = Gt[s2].rearrange("p (b k t) -> p b k t", b=16, t=32)
            for half in range(2):
                h, wh, wl, tw = self.take()
                wh, wl = (a.rearrange("p (k n) -> p k n", n=256) for a in (wh, wl))
                for j in range(2):
                    e = 2 * half + j
                    b = P.bank()
                    s = slice(128 * j, 128 * j + 128)
                    pairs = []
                    for k in range(8):
                        pairs += self.terms(wh[:, k, s], wl[:, k, s], self.uh[:, k, :], self.ul[:, k, :])
                    t = P.group(b, self.bk(b), pairs, [tw] + list(tok))
                    if j == 0:
                        self.ahead(2)
                    x = self.gel[e]
                    t2 = P.act(x, self.bk(b), ACT.Gelu if gated else ACT.Relu, [t] + gel_free[e])
                    P.bank_free[b] = [t2]
                    if gated:
                        x3 = x.rearrange("p (b t) -> p b t", t=32)
                        t2 = P.tt(x3, x3, gv[:, :, e, :], ALU.mult, [t2, tg])
                        gt_free[s2] = [t2]
                    else:
                        t2 = P.tt(x, x, x, ALU.mult, [t2])
                    t2 = self.split(self.th[s2][:, e, :], self.tl[s2][:, e, :], x, [t2] + th_free[s2])
                    gel_free[e] = [t2]
                self.split_free[h] = [t]
            return t2

        def values(g, t_h):
            s2 = g % 2
            ch = [self.take(), self.take()]
            for j in range(8):
                b = P.bank()
                pairs = []
                for e in range(4):
                    c = slice(1024 * (e % 2) + 128 * j, 1024 * (e % 2) + 128 * j + 128)
                    pairs += self.terms(ch[e // 2][1][:, c], ch[e // 2][2][:, c], self.th[s2][:, e, :],
                                        self.tl[s2][:, e, :])
                t = P.group(b, self.bk(b), pairs, [t_h, ch[0][3], ch[1][3]])
                if j in (1, 4):
                    self.ahead(1 if j == 1 else 2, 2)
                if scale is None:
                    t2 = P.tt(self.xT[:, j, :], self.xT[:, j, :], self.bk(b), ALU.add, [t])
                else:
                    t2 = P.stt(self.xT[:, j, :], self.bk(b), scale(j), self.xT[:, j, :], ALU.mult, ALU.add, [t])
                P.bank_free[b] = [t2]
            for c in ch:
                self.split_free[c[0]] = [t]
            th_free[s2] = [t]

        t_h = scores(0)
        for g in range(groups):
            nxt = scores(g + 1) if g + 1 < groups else None
            values(g, t_h)
            t_h = nxt

    def norm_to_x(self, gain):
        P = self.P
        self.rms(lambda i: self.xT[:, i, :], 8, D, 1e-6, gain, lambda i, y, t: P.copy(self.xT[:, i, :], y, [t]))

    def norm_u(self, name, off):
        return self.rms(lambda i: self.xT[:, i, :], 8, D, 1e-6, lambda i: self.V(name, off + i), self.to_u())

    def add_x(self, j, b, t):
        return self.P.tt(self.xT[:, j, :], self.xT[:, j, :], self.bk(b), ALU.add, [t])

    def rope(self, x, t, tmp):
        P = self.P
        b = P.bank()
        t = P.group(b, self.bk(b), [(self.C("rot"), x)], [t])
        t1 = P.tt(tmp, self.bk(b), self.rs, ALU.mult, [t])
        P.bank_free[b] = [t1]
        P.tt(x, x, self.rc, ALU.mult)
        return P.tt(x, x, tmp, ALU.add)

    def values_T(self, name, nk, chunks, xh, xl, dst, tok):
        P = self.P
        cw = TILES[name][0] // nk
        for n, c in enumerate(chunks):
            h, wh, wl, tw = self.take()
            wh, wl = (a.rearrange("p (k n) -> p k n", n=cw) for a in (wh, wl))
            for c0 in range(0, cw, 512):
                w = min(512, cw - c0)
                for tt in range(4):
                    b = P.bank()
                    s = slice(128 * tt, 128 * tt + 128)
                    pairs = []
                    for k in range(nk):
                        pairs += [(l, r) for r, l in self.terms(wh[:, k, c0:c0 + w], wl[:, k, c0:c0 + w],
                                                                xh(k)[:, s], xl(k)[:, s])]
                    t = P.group(b, self.ps[:, b, 0:w], pairs, [tw] + tok)
                    if tt == 0:
                        self.ahead(2)
                    t2 = P.copy(dst[:, tt, n * cw + c0:n * cw + c0 + w], self.ps[:, b, 0:w], [t],
                                eng="act" if tt % 2 else "dve")
                    P.bank_free[b] = [t2]
            self.split_free[h] = [t]
            self.ahead(2, 0)

    def softmax_rows(self, b, width, scale, e, stat, tok):
        P = self.P
        P.reduce(stat[:, 0:1], self.ps[:, b, 0:width], ALU.max, [tok])
        t = P.ts(stat[:, 1:2], stat[:, 0:1], -scale, None, ALU.mult)
        t = P.act(e[:, 0:width], self.ps[:, b, 0:width], ACT.Exp, [t], bias=stat[:, 1:2], scale=scale,
                  accum=stat[:, 2:3])
        P.bank_free[b] = [t]
        return t

    def turn(self, a, aT, nb, t, free):
        P = self.P
        b = P.bank()
        for kb in range(nb):
            o, i_ = self.ps[:, b, 128 * kb:128 * kb + 128], a[:, 128 * kb:128 * kb + 128]
            t = P.op("pe", lambda e, o=o, i_=i_: e.transpose(o, i_, self.C("ident")),
                     [t] + P.bank_free[b] if kb == 0 else (), inc=kb == nb - 1)
        t2 = P.copy(aT[:, 0:128 * nb], self.ps[:, b, 0:128 * nb], [t] + free, eng="act")
        P.bank_free[b] = [t2]
        return t2, t

    def attend(self, scores, softmaxed, v, o, aT, heads=8):
        P = self.P
        at_free = [[] for _ in range(4)]
        self.e_free = [[] for _ in range(4)]
        blocks = [(hh, qb) for hh in range(heads) for qb in range(4)]
        pend = []

        turned = {}

        ready = {}

        def turn(n):
            hh, qb = blocks[n]
            e, t = ready[n]
            turned[n], tp = self.turn(e, aT[n % 4], qb + 1, t, at_free[n % 4])
            self.e_free[n % 4] = [tp]

        def meet(n):
            hh, qb = blocks[n]
            b = P.bank()
            t = P.group(b, self.ps[:, b, 0:128], [(v[:, kb, 128 * hh:128 * hh + 128],
                                                   aT[n % 4][:, 128 * kb:128 * kb + 128]) for kb in range(qb + 1)],
                        [turned[n]])
            at_free[n % 4] = [t]
            o(hh, qb, b, t)

        last = len(blocks)
        for n in range(last + 3):
            if n < last:
                pend.append(scores(n, *blocks[n]))
            if 1 <= n <= last:
                ready[n - 1] = softmaxed(n - 1, *blocks[n - 1], pend[n - 1])
            if 2 <= n <= last + 1:
                turn(n - 2)
            if n >= 3:
                meet(n - 3)

    def diff(self):
        P, d, scr = self.P, self.d, self.scr
        U = 4096
        self.ring([0, 1, 2, 3], [0, 1])
        self.stream([("w_qkv_a_2", c) for c in range(12)])
        self.rc, self.rs = scr[:, 12288:12800], scr[:, 12800:13312]
        t_cs = P.dma("rope", scr[:, 12288:13312], d["rope"], P.done())
        lp = self.small[:, 100:102]
        P.tt(lp[:, 0:1], self.V("lambda", 0), self.V("lambda", 1), ALU.mult)
        t = P.tt(lp[:, 1:2], self.V("lambda", 2), self.V("lambda", 3), ALU.mult)
        b = P.bank()
        t = P.group(b, self.ps[:, b, 0:2], [(self.C("ones"), lp)], [t])
        t = P.act(lp, self.ps[:, b, 0:2], ACT.Exp, [t])
        P.bank_free[b] = [t]
        nl = self.small[:, 102:103]
        P.tt(nl, lp[:, 1:2], lp[:, 0:1], ALU.subtract, [t])
        P.ts(nl, nl, -0.2, None, ALU.add)
        sg8 = self.small[:, 103:104]
        P.ts(sg8, self.V("subln_g_2"), 0.8, None, ALU.mult)
        tu = self.norm_u("attn_norm_g_2", 0)
        q, k = fmat(scr[:, 0:U]), fmat(scr[:, U:2 * U])
        v = scr[:, 2 * U:3 * U].rearrange("p (t n) -> p t n", n=1024)
        o = [scr[:, 13312 + 512 * i:13824 + 512 * i] for i in range(8)]
        tmps = [scr[:, 13312 + 512 * i:13824 + 512 * i] for i in range(4)]
        P.gate["dve"] = P.gate["dve"] + [t_cs]
        roped = []

        def turn_rope():
            i, x, t = roped.pop(0)
            self.t_rope = self.rope(x, t, tmps[i % 4])

        def evac(j, b, t):
            x = q[:, j, :] if j < 8 else k[:, j - 8, :]
            t = P.copy(x, self.bk(b), [t], eng="act")
            roped.append((j, x, t))
            if len(roped) > 1:
                turn_rope()
            return t

        uh, ul = (lambda kk: self.uh[:, kk, :]), (lambda kk: self.ul[:, kk, :])
        self.gemm("w_qkv_a_2", uh, ul, tu, evac, chunks=range(8), preset=True)
        while roped:
            turn_rope()
        self.values_T("w_qkv_a_2", 8, range(8, 12), uh, ul, v, [])
        ph = P.done()
        self.stream([("w_o_a_2", c) for c in range(4)])
        E = [self.un[:, 1024 + 1024 * i:2048 + 1024 * i] for i in range(4)]
        aT = [scr[:, 20480 + 512 * i:20992 + 512 * i] for i in range(4)]
        P.gate["act"] = P.gate["act"] + ph

        def scores(n, hh, qb):
            w = 128 * (qb + 1)
            qs = slice(128 * qb, 128 * qb + 128)
            ee = E[n % 4]
            for c in range(2):
                st = self.small[:, 104 + 8 * (n % 4) + 4 * c:108 + 8 * (n % 4) + 4 * c]
                p = slice(64 * c, 64 * c + 64)
                b = P.bank()
                P.mm(self.ps[:, b, 0:w], q[p, hh, qs], k[p, hh, 0:w], True, False, ph + P.bank_free[b])
                t = P.mm(self.ps[:, b, 128 * qb:w], self.C("ident"), self.C("causal"), False, True, (), inc=True)
                P.gate["act"] = P.gate["act"] + self.e_free[n % 4]
                t = self.softmax_rows(b, w, 0.125, ee[:, 512 * c:512 * c + 512], st, t)
            return t

        def softmaxed(n, hh, qb, t):
            w = 128 * (qb + 1)
            ee = E[n % 4]
            e0, e1 = ee[:, 0:w], ee[:, 512:512 + w]
            s0 = self.small[:, 104 + 8 * (n % 4):108 + 8 * (n % 4)]
            s1 = self.small[:, 108 + 8 * (n % 4):112 + 8 * (n % 4)]
            P.recip(s0[:, 3:4], s0[:, 2:3], [t])
            P.recip(s1[:, 3:4], s1[:, 2:3])
            P.ts(s1[:, 3:4], s1[:, 3:4], nl, None, ALU.mult)
            P.ts(e1, e1, s1[:, 3:4], None, ALU.mult)
            return ee, P.stt(e0, e0, s0[:, 3:4], e1, ALU.mult, ALU.add)

        stat = self.small[:, 140:172]
        sq = [self.un[:, 512 * i:512 * i + 512] for i in range(2)]
        sq_free = [[], []]
        late = []

        def sums(hh, t):
            b = P.bank()
            for i in range(4):
                t = P.mm(self.ps[:, b, i:i + 1], sq[hh % 2][:, 128 * i:128 * i + 128], self.C("ones")[:, 0:1],
                         True, True, [t] + P.bank_free[b] if i == 0 else (), inc=i == 3)
            sq_free[hh % 2] = [t]
            P.bank_free[b] = [P.copy(stat[:, 4 * hh:4 * hh + 4], self.ps[:, b, 0:4], [t])]

        def put(hh, qb, b, t):
            P.bank_free[b] = [P.copy(o[hh][:, 128 * qb:128 * qb + 128], self.ps[:, b, 0:128], [t], eng="act")]
            if late and qb == 1:
                sums(*late.pop(0))
            if qb == 3:
                late.append((hh, P.act(sq[hh % 2], o[hh], ACT.Square, sq_free[hh % 2])))

        self.attend(scores, softmaxed, v, put, aT)
        sums(*late.pop(0))
        P.ts(stat, stat, 1.0 / 128, 1e-5, ALU.mult, ALU.add)
        t = P.act(stat, stat, ACT.Sqrt, [("dve", P.cnt["dve"]), ("pe", P.cnt["pe"])])
        P.recip(stat, stat, [t])
        toks = []
        for hh in range(8):
            b = P.bank()
            t = self.spread(b, stat[:, 4 * hh:4 * hh + 4])
            t = P.stt(o[hh], o[hh], sg8, self.bk(b), ALU.mult, ALU.mult, [t])
            P.bank_free[b] = [t]
            toks.append(self.split(self.uh[:, hh, :], self.ul[:, hh, :], o[hh], [t]))
        self.gemm("w_o_a_2", uh, ul, toks, self.add_x, preset=True)
        end = P.phase()
        self.split_free = [f + end for f in self.split_free]

    def mlp(self, l):
        P = self.P
        tu = self.norm_u("mlp_norm_g_2", 8 * l)
        self.dense(f"w_up_2_{l}", f"w_down_2_{l}", 8, False, None, tu)
        end = P.phase()

    def mla(self):
        P, d, scr = self.P, self.d, self.scr
        U = 4096
        self.ring([0, 1, 2, 3], [0, 1])
        self.stream([("w_dkv_2", c) for c in range(3)] + [("ukv_k", 0), ("ukv_v", 0)]
                    + [("w_dq_2", c) for c in range(3)] + [("uq_n", 0), ("uq_n", 1), ("uq_r", 0)]
                    + [("w_o_b_2", c) for c in range(4)])
        kn = fmat(scr[:, 0:U])
        v = scr[:, U:2 * U].rearrange("p (t n) -> p t n", n=1024)
        qn = fmat(scr[:, 2 * U:3 * U])
        qr = fmat(scr[:, 12288:14336])
        kr = fmat(scr[:, 14336:15360])
        self.rc, self.rs = scr[:, 15360:15872], scr[:, 15872:16384]
        tmps = [scr[:, 16384 + 512 * i:16896 + 512 * i] for i in range(3)]
        cc = fmat(scr[:, 17920:19456])
        t_cs = P.dma("rope", scr[:, 15360:16384], d["rope"], P.done())
        P.gate["dve"] = P.gate["dve"] + [t_cs]
        uh, ul = (lambda kk: self.uh[:, kk, :]), (lambda kk: self.ul[:, kk, :])
        tu = self.norm_u("kv_in_norm_g_2", 0)
        got = {}

        def evac(j, b, t):
            got[j] = P.copy(cc[:, j, :] if j < 2 else tmps[1], self.bk(b), [t], eng="act")
            return got[j]

        self.gemm("w_dkv_2", uh, ul, tu, evac, preset=True)
        P.memset(kr, 0.0)
        self.rope(tmps[1], got[2], tmps[0])
        P.copy(kr[0:64, 0, :], tmps[1][0:64, :])
        P.copy(kr[64:128, 1, :], tmps[1][64:128, :])
        tc = self.rms(lambda i: cc[:, i, :], 2, 256, 1e-6, lambda i: self.V("kv_norm_g_2", i), self.to_u(),
                      after=[got[2]])

        def evac_k(j, b, t):
            return P.copy(kn[:, j, :], self.bk(b), [t], eng="act" if j % 2 else "dve")

        self.gemm("ukv_k", uh, ul, tc, evac_k, preset=True)
        self.values_T("ukv_v", 2, [0], uh, ul, v, [])
        P.gate["act"] = P.gate["act"] + [("pe", P.cnt["pe"])]
        tu = self.norm_u("attn_norm_g_2", 8)

        def evac_c(j, b, t):
            got[j] = P.copy(cc[:, j, :], self.bk(b), [t], eng="act")
            return got[j]

        self.gemm("w_dq_2", uh, ul, tu, evac_c, preset=True)
        tc = self.rms(lambda i: cc[:, i, :], 3, 384, 1e-6, lambda i: self.V("q_norm_g_2", i), self.to_u(),
                      after=[got[2]])

        def evac_q(j, b, t):
            return P.copy(qn[:, j, :], self.bk(b), [t], eng="act" if j % 2 else "dve")

        def evac_r(j, b, t):
            t = P.copy(qr[:, j, :], self.bk(b), [t], eng="act")
            got[10 + j] = t
            return t

        self.gemm("uq_n", uh, ul, tc, evac_q, preset=True)
        self.gemm("uq_r", uh, ul, tc, evac_r, preset=True)
        for j in range(4):
            self.rope(qr[:, j, :], got[10 + j], tmps[j % 2])
        ph = P.done()
        E = self.gel
        aT = [scr[:, 17920 + 512 * i:18432 + 512 * i] for i in range(4)]
        o = [scr[:, 8192 + 512 * i:8704 + 512 * i] for i in range(8)]
        scale = 192.0 ** -0.5
        P.gate["act"] = P.gate["act"] + ph

        def scores(n, hh, qb):
            w = 128 * (qb + 1)
            qs = slice(128 * qb, 128 * qb + 128)
            st = self.small[:, 104 + 4 * (n % 4):108 + 4 * (n % 4)]
            b = P.bank()
            P.mm(self.ps[:, b, 0:w], qn[:, hh, qs], kn[:, hh, 0:w], True, False, ph + P.bank_free[b])
            P.mm(self.ps[:, b, 0:w], qr[:, hh // 2, qs], kr[:, hh % 2, 0:w], False, False)
            t = P.mm(self.ps[:, b, 128 * qb:w], self.C("ident"), self.C("causal"), False, True, (), inc=True)
            P.gate["act"] = P.gate["act"] + self.e_free[n % 4]
            return self.softmax_rows(b, w, scale, E[n % 4], st, t)

        def softmaxed(n, hh, qb, t):
            w = 128 * (qb + 1)
            st = self.small[:, 104 + 4 * (n % 4):108 + 4 * (n % 4)]
            P.recip(st[:, 3:4], st[:, 2:3], [t])
            return E[n % 4], P.ts(E[n % 4][:, 0:w], E[n % 4][:, 0:w], st[:, 3:4], None, ALU.mult)

        toks = [None] * 8

        def put(hh, qb, b, t):
            hi = self.uh[:, hh, 128 * qb:128 * qb + 128]
            t1 = P.copy(hi, self.ps[:, b, 0:128], [t], eng="act")
            toks[hh] = P.tt(self.ul[:, hh, 128 * qb:128 * qb + 128], self.ps[:, b, 0:128], hi.bitcast(F32),
                            ALU.subtract, [t1])
            P.bank_free[b] = [toks[hh]]

        self.attend(scores, softmaxed, v, put, aT)
        self.gemm("w_o_b_2", uh, ul, toks, self.add_x, preset=True)
        end = P.phase()
        self.split_free = [f + end for f in self.split_free]

    def dump(self, outs, ap, name="out"):
        self.P.dma(name, outs, ap, self.P.done())

    def program(self, out, stop):
        xo = out.rearrange("(k p) n -> p k n", p=128)
        self.start()
        steps = [("mix", self.mixing), ("peer", self.peer), ("peern", lambda: self.norm_to_x(lambda i: self.V("final_g", i))),
                 ("h1", self.diff), ("h2", lambda: self.mlp(0)), ("h3", self.mla), ("h4", lambda: self.mlp(1)),
                 ("final", lambda: self.norm_to_x(lambda i: self.V("final_norm_g_2", i)))]
        skip = stop is not None and stop.startswith("only:")
        if stop == "only:peer":
            for i in range(0, 20, 4):
                self.mod_batch(range(i, i + 4))()
        for name, step in steps:
            if skip and name != stop[5:]:
                continue
            step()
            if name == stop or skip:
                break
        self.dump(xo, self.xT)


def build(nc, dram, out, stop=None):
    with ExitStack() as ctx:
        dram = {**dram, "gates": nc.dram_tensor("gates", (16, 128, 4096), F32).ap()}
        n = Net(nc, ctx, dram, stop)
        P = n.P
        n.t_state = n.t_y = None
        n.program(out, stop)
        final = [(s, v) for s, v in P.cnt.items() if s.startswith("out")]
        P.q["sp"].append((final, lambda e: None, None, 0))
        block = ctx.enter_context(nc.Block())

        @block.sync
        def _(e):
            P.play("sp", e)

        @block.gpsimd
        def _(e):
            P.play("pool", e)

        @block.vector
        def _(e):
            P.play("dve", e)

        @block.scalar
        def _(e):
            P.play("act", e)

        @block.tensor
        def _(e):
            P.play("pe", e)


def columns(a):
    return a.reshape(-1, 128).T


def lay_out(x):
    z = {n: np.asarray(a) for n, a in x.items()}
    arr = {}
    table, arr["rope"] = shape_constants()
    arr["consts"], arr["masks"] = table[:, 0:NC1], table[:, NC1:]
    pack = []
    for n, w in VEC:
        if n == "conv_dw_w":
            a = z[n][0].reshape(CW, 4, 128).transpose(2, 1, 0).reshape(128, 4 * CW)
        elif n == "lambda":
            a = np.zeros((128, 4), np.float32)
            for i, m in enumerate(("lambda_q1_2", "lambda_k1_2", "lambda_q2_2", "lambda_k2_2")):
                a[0:64, i] = z[m][0]
        else:
            a = columns(z[n])
        assert a.shape == (128, w), n
        pack.append(a)
    arr["vecs"] = np.concatenate(pack, axis=1)
    arr["xT"] = z["x"][0].T
    for n in ("rwkv_w2", "rwkv_a2", "rwkv_g2"):
        arr[n] = z[n][0]
    w = {n: z[n][0] for n in ("ada_w", "w_in", "w_out", "peer_w_q", "peer_v", "w_qkv_a_2", "w_o_a_2", "w_dq_2",
                              "w_o_b_2")}
    w["peer_uT"] = z["peer_u"][0].T
    for i in range(2):
        w[f"w_up_2_{i}"], w[f"w_down_2_{i}"] = z["w_up_2"][i], z["w_down_2"][i]
    w["w_dkv_2"] = np.concatenate([z["w_dkv_2"], z["w_dkv_2"][:, 256:320]], axis=1)
    ukv = z["w_ukv_2"].reshape(256, 8, 256)
    w["ukv_k"], w["ukv_v"] = ukv[:, :, 0:128].reshape(256, 1024), ukv[:, :, 128:256].reshape(256, 1024)
    uq = z["w_uq_2"][0].reshape(384, 8, 192)
    w["uq_n"], w["uq_r"] = uq[:, :, 0:128].reshape(384, 1024), uq[:, :, 128:192].reshape(384, 512)
    for n, a in w.items():
        arr[n] = tiled(a, *TILES[n])
    arr["keysT"] = z["peer_sub_keys"][0].transpose(3, 0, 1, 2).reshape(128, 2048)
    return {n: np.ascontiguousarray(a) for n, a in arr.items()}


def kernel(**inputs):
    import concourse.bacc as bacc
    from concourse.bass_utils import run_bass_kernel_spmd

    nc = bacc.Bacc("TRN2", target_bir_lowering=False, num_devices=1)
    arrays, dram = {}, {}
    for n, a in lay_out(inputs).items():
        arrays["in_" + n] = a
        dram[n] = nc.dram_tensor("in_" + n, a.shape, F32, kind="ExternalInput").ap()
    out = nc.dram_tensor("out_x", (D, S), F32, kind="ExternalOutput").ap()
    build(nc, dram, out)
    r = run_bass_kernel_spmd(nc, [arrays], core_ids=[0])
    return np.ascontiguousarray(r.results[0]["out_x"].T)[None]
```

```python
from contextlib import ExitStack
import math

import numpy as np
import concourse.bass as bass
from concourse import mybir

F32 = mybir.dt.float32
F32R = mybir.dt.float32r
U32 = mybir.dt.uint32
ALU = mybir.AluOpType
ACT = mybir.ActivationFunctionType
AX = mybir.AxisListType.X

D, S, H = 1024, 512, 8
NEG = -1.0e30
NBANK = 8
NSLOT = 4
COLS = 53120
A_U = 5504
A_W0 = A_U + 8192
A_RAW = A_W0 + 8192
A_W2 = A_RAW + 8192
A_T = A_W2 + 8192
A_G = A_T + 8192
A_GEL = A_G + 4096
A_TMP = A_GEL + 2048
CW = 31
CDECAY = math.exp(-0.5)

CONST = ["ident", "ones", "bd", "rot", "iota", "causal", "strict", "incl", "m1",
         "t1", "t2", "t4", "t8", "t16", "t32"]
CCOL = {n: 128 * i for i, n in enumerate(CONST)}
NC1 = 768
NC2 = 128 * 9 + 512

VEC = [("c", 8), ("ada_b", 48), ("norm_mix_g", 8), ("conv_dw_w", 4 * CW), ("conv_dw_b", 4), ("conv_ln_w", 4),
       ("conv_ln_b", 4), ("rwkv_mu", 14), ("rwkv_w0", 4), ("rwkv_a0", 4), ("rwkv_k_k", 4), ("rwkv_k_a", 4),
       ("rwkv_r_k", 4), ("rwkv_gn_w", 4), ("rwkv_gn_b", 4), ("norm_ffn_g", 8), ("final_g", 8),
       ("attn_norm_g_2", 16), ("subln_g_2", 1), ("kv_in_norm_g_2", 8), ("kv_norm_g_2", 2), ("q_norm_g_2", 3),
       ("mlp_norm_g_2", 16), ("final_norm_g_2", 8), ("lambda", 4)]
VCOL = {}
NVEC = 0
for _n, _w in VEC:
    VCOL[_n] = NVEC
    NVEC += _w


def shape_constants():
    i = np.arange(128)
    r, c = i[:, None], i[None, :]
    same = (r // 64) == (c // 64)
    m = {"ident": r == c, "ones": np.ones((128, 128)), "bd": same, "iota": np.broadcast_to(c, (128, 128)),
         "causal": np.where(c <= r, 0.0, NEG), "strict": same & (r < c), "incl": same & (r <= c),
         "m1": (r // 2 == c // 2) & (r % 2 == 1) & (c % 2 == 0)}
    for b in (1, 2, 4, 8, 16, 32):
        m[f"t{b}"] = (r // (2 * b) == c // (2 * b)) & (r % (2 * b) < b) & (c % (2 * b) >= b)
    rot = np.zeros((128, 128))
    for o in (0, 64):
        for j in range(32):
            rot[o + 32 + j, o + j] = -1.0
            rot[o + j, o + 32 + j] = 1.0
    m["rot"] = rot
    scan = np.broadcast_to((np.arange(512) % 64 != 0), (128, 512))
    table = np.concatenate([np.asarray(m[n], np.float32) for n in CONST] + [scan.astype(np.float32)], axis=1)
    freq = (np.float32(10000.0) ** (-np.arange(0, 64, 2, dtype=np.float32) / np.float32(64))).astype(np.float32)
    ang = np.arange(S, dtype=np.float32)[None, :] * freq[:, None]
    cs = np.concatenate([np.tile(np.cos(ang), (4, 1)), np.tile(np.sin(ang), (4, 1))], axis=1).astype(np.float32)
    return np.ascontiguousarray(table), np.ascontiguousarray(cs)


TILES = {"ada_w": (2048, 24, 8), "w_in": (2048, 11, 8), "w_out": (2048, 4, 8), "peer_w_q": (2048, 8, 8),
         "peer_uT": (2048, 64, 8), "peer_v": (2048, 64, 2), "w_qkv_a_2": (2048, 12, 8), "w_o_a_2": (2048, 4, 8),
         "w_dkv_2": (1024, 3, 8), "ukv_k": (2048, 1, 2), "ukv_v": (2048, 1, 2), "w_dq_2": (1024, 3, 8),
         "uq_n": (1536, 2, 3), "uq_r": (1536, 1, 3), "w_o_b_2": (2048, 4, 8),
         "w_up_2_0": (2048, 16, 8), "w_up_2_1": (2048, 16, 8), "w_down_2_0": (2048, 16, 2),
         "w_down_2_1": (2048, 16, 2)}


def tiled(w, width, n, nk):
    if w.shape[0] == 128 * nk:
        return w.reshape(nk, 128, n, width // nk).transpose(2, 1, 0, 3).reshape(-1)
    return w.reshape(n, nk, 128, w.shape[1]).transpose(0, 2, 1, 3).reshape(-1)


class Prog:

    def __init__(self, nc, ctx):
        self.nc, self.ctx = nc, ctx
        self.q = {e: [] for e in ("pe", "act", "dve", "pool", "sp")}
        self.sem, self.cnt = {}, {}
        self.known = {e: {} for e in self.q}
        self.gate = {e: [] for e in self.q}
        for e in ("pe", "act", "dve", "pool"):
            self.new_sem(e)
        self.bank_free = [[] for _ in range(NBANK)]
        self.nbank = 0
        self.lag = 0

    def new_sem(self, name):
        self.sem[name] = self.ctx.enter_context(self.nc.semaphore("s_" + name))
        self.cnt[name] = 0

    def waits(self, eng, tokens):
        need = {}
        for t in tokens:
            if t is not None and self.known[eng].get(t[0], 0) < t[1]:
                need[t[0]] = max(need.get(t[0], 0), t[1])
        self.known[eng].update(need)
        return sorted(need.items())

    def op(self, eng, fn, after=(), inc=True):
        tokens = list(after) + self.gate[eng]
        self.gate[eng] = []
        if eng != "pe" and self.lag is not None:
            tokens.append((eng, self.cnt[eng] - self.lag))
        w = self.waits(eng, tokens)
        if inc:
            self.cnt[eng] += 1
        self.q[eng].append((w, fn, eng if inc else None, 1))
        return (eng, self.cnt[eng])

    def dma(self, sem, out, in_, after=(), eng="sp"):
        if sem not in self.sem:
            self.new_sem(sem)
        tokens = list(after) + self.gate[eng]
        self.gate[eng] = []
        w = self.waits(eng, tokens)
        self.cnt[sem] += 16
        self.q[eng].append((w, lambda e: e.dma_start(out, in_), sem, 16))
        return (sem, self.cnt[sem])

    def done(self):
        return [(e, self.cnt[e]) for e in ("pe", "act", "dve", "pool")]

    def phase(self, engines=("pe", "act", "dve", "pool")):
        t = self.done()
        for e in engines:
            self.gate[e] = self.gate[e] + t
        return t

    def bank(self):
        b = self.nbank % NBANK
        self.nbank += 1
        return b

    def mm(self, out, lhsT, rhs, start, stop, after=(), inc=False):
        return self.op("pe", lambda e: e.matmul(out, lhsT, rhs, start=start, stop=stop), after, inc)

    def group(self, b, out, pairs, after=()):
        t = None
        for i, (l, r) in enumerate(pairs):
            t = self.mm(out, l, r, i == 0, i == len(pairs) - 1,
                        list(after) + self.bank_free[b] if i == 0 else (), inc=i == len(pairs) - 1)
        return t

    def tt(self, out, a, b, op, after=(), eng="dve"):
        return self.op(eng, lambda e: e.tensor_tensor(out, a, b, op), after)

    def ts(self, out, a, s1, s2, op0, op1=None, after=(), eng="dve"):
        if op1 is None:
            return self.op(eng, lambda e: e.tensor_scalar(out, a, s1, None, op0), after)
        return self.op(eng, lambda e: e.tensor_scalar(out, a, s1, s2, op0, op1), after)

    def stt(self, out, a, s, b, op0, op1, after=(), eng="dve"):
        return self.op(eng, lambda e: e.scalar_tensor_tensor(out=out, in0=a, scalar=s, in1=b, op0=op0, op1=op1), after)

    def act(self, out, in_, func, after=(), bias=0.0, scale=1.0, accum=None):
        if func == ACT.Copy:
            return self.op("act", lambda e: e.copy(out, in_), after)
        if accum is not None:
            return self.op("act", lambda e: e.activation(out, in_, func, bias=bias, scale=scale, accum_out=accum), after)
        return self.op("act", lambda e: e.activation(out, in_, func, bias=bias, scale=scale), after)

    def copy(self, out, in_, after=(), eng="dve"):
        if eng == "act":
            return self.op("act", lambda e: e.copy(out, in_), after)
        return self.op(eng, lambda e: e.tensor_copy(out, in_), after)

    def memset(self, out, v, after=(), eng="dve"):
        return self.op(eng, lambda e: e.memset(out, v), after)

    def recip(self, out, in_, after=()):
        return self.op("dve", lambda e: e.reciprocal(out, in_), after)

    def reduce(self, out, in_, op, after=()):
        return self.op("dve", lambda e: e.tensor_reduce(out, in_, AX, op), after)

    def play(self, name, e):
        for w, fn, sem, n in self.q[name]:
            for s, v in w:
                e.wait_ge(self.sem[s], v)
            ins = fn(e)
            if sem is not None:
                ins.then_inc(self.sem[sem], n)


def fmat(ap, n=512):
    return ap.rearrange("p (k n) -> p k n", n=n)


class Net:
    def __init__(self, nc, ctx, dram, stop):
        self.P = P = Prog(nc, ctx)
        self.d, self.stop_at = dram, stop
        base, total = 16512, COLS

        def plain(name, a0, a1):
            return nc.alloc_sbuf_tensor_at(name, [128, a1 - a0], F32, offset=base + 4 * a0)

        self.ps = ctx.enter_context(nc.psum_tensor("ps", [128, NBANK, 512], F32))
        m = plain("kept", 0, A_U)
        self.xT = fmat(m[:, 0:4096])
        self.const = m[:, 4096:4096 + NC1]
        at = 4096 + NC1
        self.vec = m[:, at:at + NVEC]
        self.modv = m[:, at + NVEC:at + NVEC + 48]
        self.small = m[:, at + NVEC + 48:at + NVEC + 304]
        assert at + NVEC + 304 <= A_U

        def split(name, at, n):
            return nc.alloc_sbuf_tensor_at(name, [128, n], F32R, offset=base + 4 * at)

        self.uh, self.ul = fmat(split("uh", A_U, 4096)[:, :]), fmat(split("ul", A_U + 4096, 4096)[:, :])
        self.wh, self.wl = [], []
        for i, o in enumerate((A_W0, A_W0 + 4096, A_W2, A_W2 + 4096)):
            self.wh.append(split(f"wh{i}", o, 2048)[:, :])
            self.wl.append(split(f"wl{i}", o + 2048, 2048)[:, :])
        self.th, self.tl = [], []
        for i in range(2):
            self.th.append(fmat(split(f"th{i}", A_T + 4096 * i, 2048)[:, :]))
            self.tl.append(fmat(split(f"tl{i}", A_T + 4096 * i + 2048, 2048)[:, :]))
        self.raw = [plain(f"raw{i}", A_RAW + 2048 * i, A_RAW + 2048 * i + 2048)[:, :] for i in range(4)]
        scr = plain("scratch", A_W2, total)
        self.rtmp = scr[:, A_TMP - A_W2:A_TMP - A_W2 + 512]
        self.scr = scr[:, 0:A_TMP - A_W2]
        self.gel = [scr[:, A_GEL - A_W2 + 512 * i:A_GEL - A_W2 + 512 * i + 512] for i in range(4)]
        self.raw_free, self.split_free = [[] for _ in range(4)], [[] for _ in range(4)]
        self.diag_free, self.lo_dve = [], 0
        self.queued, self.pre, self.two_norms = False, None, False
        self.A = [(self.uh[:, k, :], self.ul[:, k, :]) for k in range(8)]
        self.B = [(self.th[k // 4][:, k % 4, :], self.tl[k // 4][:, k % 4, :]) for k in range(8)]
        self.un = plain("un", A_U, A_U + 8192)[:, :]
        self.w01 = plain("w01", A_W0, A_W0 + 8192)[:, :]

    def C(self, name):
        a = CCOL[name]
        return self.const[:, a:a + 128] if a < NC1 else self.masks[:, a - NC1:a - NC1 + 128]

    def V(self, name, i=0, n=1):
        return self.vec[:, VCOL[name] + i:VCOL[name] + i + n]

    def bk(self, b):
        return self.ps[:, b, :]

    def half(self, i):
        if i < 11:
            return self.scr[:, 2048 * i:2048 * (i + 1)]
        if i < 15:
            return self.un[:, 2048 * (i - 11):2048 * (i - 10)]
        return self.w01[:, 2048 * (i - 15):2048 * (i - 14)]

    def ring(self, raws, splits):
        self.raws, self.splits, self.nraw, self.nsplit = raws, splits, 0, 0

    def fetch(self, name, i):
        width, n = TILES[name][0], TILES[name][1]
        r = self.raws[self.nraw % len(self.raws)]
        self.nraw += 1
        at = i * 128 * width
        src = self.d[name][at:at + 128 * width].rearrange("(p w) -> p w", p=128)
        t = self.P.dma(f"raw{r}", self.raw[r][:, 0:width], src, self.raw_free[r])
        return r, width, t

    def queue(self, todo):
        self.todo += todo
        self.queued = True

    def begin(self, todo):
        if not self.queued:
            self.ring([0, 1, 2, 3], [2, 3])
            self.stream(todo)
            return
        self.queued = False
        pending = [c[0] for c in self.ready[self.taken:]]
        self.rotate([i for i in (2, 3) if i not in pending] + pending)

    def widen(self):
        for i in (0, 1):
            self.split_free[i] = self.split_free[i] + self.P.done()
        pending = [c[0] for c in self.ready[self.taken:]]
        self.rotate([i for i in (2, 3) if i not in pending] + [0, 1] + pending)

    def rotate(self, order):
        self.splits = [None] * len(order)
        for i, slot in enumerate(order):
            self.splits[(self.nsplit + i) % len(order)] = slot

    def load(self, n):
        while len(self.loaded) < n:
            self.loaded.append(self.fetch(*self.todo[len(self.loaded)]))

    def prepare(self, n):
        P = self.P
        self.load(n + 1)
        r, width, t = self.loaded[n]
        h = self.splits[self.nsplit % len(self.splits)]
        self.nsplit += 1
        wh, wl, w = self.wh[h][:, 0:width], self.wl[h][:, 0:width], self.raw[r][:, 0:width]
        t = P.act(wh, w, ACT.Copy, [t] + self.split_free[h])
        eng = "dve" if self.lo_dve and self.nsplit % self.lo_dve == 0 else "pool"
        t = P.tt(wl, w, wh.bitcast(F32), ALU.subtract, [t] + self.split_free[h], eng=eng)
        self.raw_free[r] = [t]
        return h, wh, wl, t

    def stream(self, todo, loads=0):
        self.todo, self.ready, self.taken, self.loaded = list(todo), [], 0, []
        if loads:
            self.load(loads)
        else:
            self.ahead(2, 0)

    def ahead(self, n, held=1):
        n = min(n, len(self.splits) - held)
        while len(self.ready) < min(len(self.todo), self.taken + n):
            self.ready.append(self.prepare(len(self.ready)))

    def take(self):
        self.ahead(1)
        c = self.ready[self.taken]
        self.taken += 1
        return c

    def split(self, hi, lo, x, after, eng="dve", bias=None):
        P = self.P
        if bias is None:
            t = P.act(hi, x, ACT.Copy, after)
            return P.tt(lo, x, hi.bitcast(F32), ALU.subtract, [t], eng=eng)
        t = P.act(hi, x, ACT.Identity, after, bias=bias)
        return P.stt(lo, x, bias, hi.bitcast(F32), ALU.add, ALU.subtract, [t])

    @staticmethod
    def terms(wh, wl, xh, xl):
        return [(wh, xh), (wh, xl), (wl, xh)]

    def rstd(self, b, stat, scale, eps, t):
        P = self.P
        t = P.ts(stat, stat, scale, eps, ALU.mult, ALU.add, [t])
        t = P.act(stat, stat, ACT.Sqrt, [t])
        t = P.recip(stat, stat, [t])
        return self.spread(b, stat)

    def spread(self, b, stat):
        P = self.P
        t = None
        for i in range(4):
            dg = self.rtmp[:, 128 * i:128 * i + 128]
            t = P.ts(dg, self.C("ident"), stat[:, i:i + 1], None, ALU.mult, after=self.diag_free)
            t = P.mm(self.ps[:, b, 128 * i:128 * i + 128], self.C("ones"), dg, True, True,
                     [t] + (P.bank_free[b] if i == 0 else []), inc=True)
        self.diag_free = [t]
        return t

    def squares(self, src, n, after=()):
        P = self.P
        acc, sq = self.gel[0], self.gel[1:3]
        sq_free = [[], []]
        for i in range(n):
            o = acc if i == 0 else sq[i % 2]
            t = P.act(o, src(i), ACT.Square, list(after) + sq_free[i % 2])
            if i:
                t = P.tt(acc, acc, o, ALU.add, [t])
                sq_free[i % 2] = [t]
        return self.token_sums(acc, self.small[:, 200:204], t)

    def token_sums(self, acc, stat, t):
        P = self.P
        b = P.bank()
        for i in range(4):
            t = P.mm(self.ps[:, b, i:i + 1], acc[:, 128 * i:128 * i + 128], self.C("ones")[:, 0:1], True, True,
                     [t] + P.bank_free[b] if i == 0 else (), inc=i == 3)
        t = P.copy(stat, self.ps[:, b, 0:4], [t])
        P.bank_free[b] = [t]
        return t

    def rms(self, src, n, dim, eps, gain, dst, after=(), t=None):
        P = self.P
        t = self.squares(src, n, after) if t is None else t
        b = P.bank()
        t = self.rstd(b, self.small[:, 200:204], 1.0 / dim, eps, t)
        out, free, made = [], [[], [], [], []], None
        for i in range(n + 1):
            y = self.gel[i % 4]
            if i < n:
                t = P.stt(y, src(i), gain(i), self.bk(b), ALU.mult, ALU.mult, [t] + free[i % 4])
                P.bank_free[b] = [t]
            if made is not None:
                out.append(dst(*made))
                free[made[0] % 4] = [out[-1]]
            made = (i, y, t)
        return out

    def head_rsqrt(self, sq, t, scale, eps, least, R):
        P = self.P
        stat = self.small[:, 204:236]
        b = P.bank()
        for q in range(4):
            for i in range(4):
                c = 8 * i + 2 * q
                t = P.mm(self.ps[:, b, c:c + 2], sq[:, q, 128 * i:128 * i + 128], self.C("bd")[:, 0:128:64], True, True,
                         [t] + P.bank_free[b] if q == i == 0 else (), inc=q == i == 3)
        if least is None:
            t = P.ts(stat, self.ps[:, b, 0:32], scale, eps, ALU.mult, ALU.add, [t])
        else:
            t = P.ts(stat, self.ps[:, b, 0:32], least, None, ALU.max, after=[t])
        P.bank_free[b] = [t]
        t = P.act(stat, stat, ACT.Sqrt, [t])
        P.recip(stat, stat, [t])
        banks = [P.bank() for _ in range(4)]
        free = [[], []]
        for i in range(4):
            r = R[i % 2]
            t = P.copy(r.rearrange("p (h n) -> p h n", n=64),
                       stat[:, 8 * i:8 * i + 8].unsqueeze(2).broadcast_to([128, 8, 64]), free[i % 2])
            for q in range(4):
                t = P.mm(self.ps[:, banks[q], 128 * i:128 * i + 128], r[:, 128 * q:128 * q + 128], self.C("ident"),
                         True, True, [t] + (P.bank_free[banks[q]] if i == 0 else []), inc=q == 3)
            free[i % 2] = [t]
        return banks, t

    def gemm(self, name, xh, xl, tok, evac, chunks=None, preset=False):
        P = self.P
        width, n, nk = TILES[name]
        cw = width // nk
        chunks = range(n) if chunks is None else chunks
        if not preset:
            self.stream([(name, c) for c in chunks])
        for c in chunks:
            h, wh, wl, tw = self.take()
            wh, wl = (a.rearrange("p (k n) -> p k n", n=cw) for a in (wh, wl))
            t = None
            for j in range(cw // 128):
                b = P.bank()
                s = slice(128 * j, 128 * j + 128)
                for k in range(nk):
                    for i, (l, r) in enumerate(self.terms(wh[:, k, s], wl[:, k, s], xh(k), xl(k))):
                        first, last = k == 0 and i == 0, k == nk - 1 and i == 2
                        after = ([tok[k]] if i == 0 else []) + ([tw] + P.bank_free[b] if first else [])
                        t = P.mm(self.bk(b), l, r, first, last, after, inc=last)
                if j == 0:
                    self.ahead(2)
                P.bank_free[b] = [evac(c * (cw // 128) + j, b, t)]
            self.split_free[h] = [t]
            self.ahead(2, 0)

    def mod_load(self, chunks, places, after=()):
        out = []
        for n, (ch, place) in enumerate(zip(chunks, places)):
            at = ch * 128 * 2048
            src = self.d["ada_w"][at:at + 128 * 2048].rearrange("(p w) -> p w", p=128)
            out.append((self.P.dma(f"ada{n}", place, src, after), place))
        return out

    def mod_product(self, w, t, eng):
        P = self.P
        c = self.small[:, 0:8].unsqueeze(2).broadcast_to([128, 8, 256])
        t = P.tt(w, w, c, ALU.mult, [t, self.t_silu], eng=eng)
        for m in (4, 2, 1):
            t = P.tt(w[:, 0:m, :], w[:, 0:m, :], w[:, m:2 * m, :], ALU.add, eng=eng)
        return t

    def mod_batch(self, chunks, loads=None, engines=()):
        P = self.P
        b = P.bank()
        for n, ch in enumerate(chunks):
            if loads is None:
                r, width, tw = self.fetch("ada_w", ch)
                w = self.raw[r]
            else:
                tw, w = loads[n]
            eng = engines[n] if n < len(engines) else "pe"
            w = w.rearrange("p (k n) -> p k n", n=256)
            if eng in ("dve", "pool"):
                tw = self.mod_product(w, tw, eng)
            for j in range(2):
                s = slice(128 * j, 128 * j + 128)
                pairs = [(w[:, k, s], self.small[:, k:k + 1]) for k in range(8)]
                if eng != "pe":
                    pairs = [(w[:, 0, s], self.C("ones")[:, 0:1])]
                t = P.group(b, self.ps[:, b, 2 * n + j:2 * n + j + 1], pairs, [tw, self.t_silu])
            if loads is None:
                self.raw_free[r] = [t]
        n, at = 2 * len(chunks), 2 * chunks[0]

        def finish():
            P.bank_free[b] = [P.tt(self.modv[:, at:at + n], self.ps[:, b, 0:n], self.V("ada_b", at, n), ALU.add, [t])]
            return P.bank_free[b][0]
        return finish

    def start(self):
        P = self.P
        d = self.d
        self.t_c = P.dma("cst", self.const, d["consts"])
        self.masks = self.raw[3]
        self.raw_free[3] = [self.t_c]
        self.scanm = self.raw[3][:, 1152:1664]
        self.t_c = P.dma("cst", self.masks[:, 0:NC2], d["masks"])
        self.raw_free[3] = [self.t_c]
        self.ring([0, 1, 2], [0, 1])
        self.t_v = P.dma("vec", self.vec, d["vecs"])
        self.t_x = P.dma("x", self.xT, d["xT"].rearrange("(k p) n -> p k n", p=128))
        self.t_silu = P.act(self.small[:, 0:8], self.V("c", 0, 8), ACT.Silu, [self.t_v])
        for e in ("pe", "act", "dve", "pool"):
            P.gate[e] = [self.t_c, self.t_v, self.t_x]

    def to_u(self, shift=None):
        def dst(i, y, t):
            return self.split(self.uh[:, i, :], self.ul[:, i, :], y, [t], bias=None if shift is None else shift(i))
        return dst

    def mixing(self):
        P, d = self.P, self.d
        h = self.half
        src = lambda i: self.xT[:, i, :]
        t_sq = self.squares(src, 8)
        t = self.mod_batch(range(8), self.mod_load(range(8), [h(i) for i in (0, 1, 2, 3, 4, 5, 7, 8)]),
                           ("pe", "pool", "dve", "dve", "pool", "dve", "pe", "dve"))()
        g1 = self.small[:, 8:16]
        t = P.stt(g1, self.modv[:, 8:16], 1.0, self.V("norm_mix_g", 0, 8), ALU.add, ALU.mult, [t])
        self.stream([("w_in", c) for c in (2, 3, 0, 1, 10, 6, 7, 4, 5, 8, 9)])
        self.ada = self.mod_load(range(8, 13), [h(i) for i in (1, 2, 3, 7, 5)], [t])
        tu = self.rms(src, 8, D, 1e-6, lambda i: g1[:, i:i + 1], self.to_u(lambda i: self.modv[:, i:i + 1]), t=t_sq)
        omu = self.small[:, 16:30]
        P.ts(omu, self.V("rwkv_mu", 0, 14), -1.0, 1.0, ALU.mult, ALU.add)
        oka = self.small[:, 30:34]
        P.ts(oka, self.V("rwkv_k_a", 0, 4), -1.0, 1.0, ALU.mult, ALU.add)
        r, k_, v = fmat(h(0)), fmat(h(10)), fmat(h(4))
        gated, conv, sig = fmat(h(9)), fmat(h(8)), fmat(h(10))
        lo = fmat(h(6)[:, 0:1024])
        w2a2, g2 = h(6)[:, 1024:1536], h(6)[:, 1536:2048]
        t_w2 = P.dma("w2", w2a2[0:64, :], d["rwkv_w2"])
        t_w2 = P.dma("w2", w2a2[64:128, :], d["rwkv_a2"])
        t_g2 = P.dma("g2", g2, d["rwkv_g2"])
        self.conv, self.gated = conv, gated
        self.conv_todo = [(i, sh) for i in range(4) for sh in range(1, CW)]
        self.sig_tok, self.shifted = {}, {}

        def evac(j, b, t):
            if j in (0, 20, 12, 8, 16):
                n = (0, 20, 12, 8, 16).index(j)
                tw, w = self.ada[n]
                self.ada[n] = (self.mod_product(w.rearrange("p (k n) -> p k n", n=256), tw, "pool"), w)
            if 4 <= j < 8:
                self.sig_tok[j - 4] = P.act(sig[:, j - 4, :], self.bk(b), ACT.Sigmoid, [t, tu[-1]])
                return self.sig_tok[j - 4]
            if j < 4:
                t = P.tt(gated[:, j, :], self.bk(b), sig[:, j, :], ALU.mult, [t, self.sig_tok[j]])
                P.ts(conv[:, j, :], gated[:, j, :], self.V("conv_dw_w", CW * j + CW - 1), self.V("conv_dw_b", j),
                     ALU.mult, ALU.add)
                return t
            i = j - 8
            dst = (r, k_, v)[i // 4][:, i % 4, :] if i < 12 else lo[:, i - 12, :]
            t = P.ts(dst, self.bk(b), omu[:, i:i + 1], None, ALU.mult, after=[t, tu[-1]])
            t = P.stt(dst[:, 1:S], self.ps[:, b, 0:S - 1], self.V("rwkv_mu", i), dst[:, 1:S],
                      ALU.mult, ALU.add, [t])
            self.shifted[i] = t
            self.conv_some(7)
            return t

        uh, ul = (lambda k: self.uh[:, k, :]), (lambda k: self.ul[:, k, :])
        self.gemm("w_in", uh, ul, tu, evac, chunks=(2, 3, 0, 1, 10, 6, 7, 4, 5, 8, 9), preset=True)
        self.rwkv(r, k_, v, lo, w2a2, g2, t_w2, t_g2, oka)

    def conv_some(self, n):
        P = self.P
        for i, sh in self.conv_todo[:n]:
            P.stt(self.conv[:, i, sh:], self.gated[:, i, :S - sh], self.V("conv_dw_w", CW * i + CW - 1 - sh),
                  self.conv[:, i, sh:], ALU.mult, ALU.add)
        self.conv_todo = self.conv_todo[n:]

    def conv_norm(self, x2):
        P, conv = self.P, self.conv
        sq, mu = x2[:, 0:512], x2[:, 512:1024]
        b = P.bank()
        t = P.group(b, self.bk(b), [(self.C("ones"), conv[:, i, :]) for i in range(4)])
        t = P.ts(mu, self.bk(b), 1.0 / 512, None, ALU.mult, after=[t])
        P.bank_free[b] = [t]
        yield
        for i in range(4):
            t = P.tt(conv[:, i, :], conv[:, i, :], mu, ALU.subtract)
            yield
        for i in range(4):
            t = P.act(sq if i else mu, conv[:, i, :], ACT.Square, [t, ("dve", P.cnt["dve"])])
            if i:
                t = P.tt(mu, mu, sq, ALU.add, [t])
            yield
        stat = self.small[:, 236:240]
        t = self.token_sums(mu, stat, t)
        b = P.bank()
        t = self.rstd(b, stat, 1.0 / 512, 1e-5, t)
        t = P.copy(mu, self.bk(b), [t])
        P.bank_free[b] = [t]
        yield
        for i in range(4):
            t = P.tt(conv[:, i, :], conv[:, i, :], mu, ALU.mult)
            self.t_conv = P.act(conv[:, i, :], conv[:, i, :], ACT.Silu, [t], bias=self.V("conv_ln_b", i),
                                scale=self.V("conv_ln_w", i))
            yield

    def rwkv(self, r, k_, v, lo, w2a2, g2, t_w2, t_g2, oka):
        P, h = self.P, self.half
        sg, cum, a = fmat(h(11)), fmat(h(12)), fmat(h(13))
        kk, pd, pi = fmat(h(14)), fmat(h(15)), fmat(h(16))
        tmp, sq = fmat(h(17)), fmat(h(18))
        Rf, Af, Bf, Kf = r, fmat(h(1)), fmat(h(2)), fmat(h(3))
        g, bonus = fmat(h(5)), fmat(h(7))
        t_in = [("pe", P.cnt["pe"])]
        R = [h(17)[:, 0:512], h(17)[:, 512:1024]]
        self.mod_batch(range(13, 16))()
        for q in range(4):
            t_sq = P.act(sq[:, q, :], k_[:, q, :], ACT.Square, t_in + [self.shifted[4 + q]], scale=self.V("rwkv_k_k", q))
        t0 = P.act(lo[0:64, 0, :], lo[0:64, 0, :], ACT.Tanh, [self.shifted[12]])
        t1 = P.act(lo[:, 1, :], lo[:, 1, :], ACT.Sigmoid, [self.shifted[13]])
        sums = []
        for q in range(4):
            c = slice(128 * q, 128 * q + 128)
            b = P.bank()
            t = P.group(b, self.bk(b), [(w2a2[0:64, c], lo[0:64, 0, :])], [t0, t_w2])
            t = P.act(sg[:, q, :], self.bk(b), ACT.Sigmoid, [t], bias=self.V("rwkv_w0", q))
            P.bank_free[b] = [t]
            cq, sq_ = cum[:, q, :], sg[:, q, :]
            P.op("dve", lambda e, cq=cq, sq_=sq_: e.tensor_tensor_scan(cq, self.scanm, sq_, 0.0, ALU.mult, ALU.add),
                 [t])
            b = P.bank()
            t = P.group(b, self.bk(b), [(w2a2[64:128, c], lo[64:128, 0, :])])
            t = P.act(a[:, q, :], self.bk(b), ACT.Sigmoid, [t], bias=self.V("rwkv_a0", q))
            P.bank_free[b] = [t]
        finish_ada = self.mod_batch(range(8, 13), self.ada, ["made"] * 5)
        for q in range(4):
            c = slice(128 * q, 128 * q + 128)
            b = P.bank()
            t = P.group(b, self.bk(b), [(g2[:, c], lo[:, 1, :])], [t1, t_g2])
            t = P.copy(g[:, q, :], self.bk(b), [t], eng="act")
            P.bank_free[b] = [t]
        self.conv_some(len(self.conv_todo))
        finish_ada()
        tc = P.tt(sg, cum, sg, ALU.subtract)
        banks, t_rs = self.head_rsqrt(sq, t_sq, None, None, 1e-24, R)
        t_i = P.act(pi, cum, ACT.Exp, [tc], scale=CDECAY)
        t_pp = P.act(sg, sg, ACT.Exp, scale=-CDECAY)
        t_p = P.act(pd, cum, ACT.Exp, scale=-CDECAY)
        finish = self.mod_batch(range(16, 18), None, ["pool"] * 2)
        for q in range(4):
            t = P.stt(kk[:, q, :], k_[:, q, :], self.V("rwkv_k_k", q), self.bk(banks[q]), ALU.mult, ALU.mult, [t_rs])
            P.bank_free[banks[q]] = [t]
        finish()
        P.tt(Bf, kk, a, ALU.mult)
        P.tt(Bf, Bf, pi, ALU.mult, [t_i])
        for q in range(4):
            P.ts(tmp[:, q, :], a[:, q, :], self.V("rwkv_k_a", q), oka[:, q:q + 1], ALU.mult, ALU.add)
        t_k = P.tt(k_, k_, tmp, ALU.mult)
        P.tt(Kf, k_, pi, ALU.mult, [t_k, t_i], eng="pool")
        P.stt(Af, kk, -1.0, sg, ALU.mult, ALU.mult, [t_pp])
        bank = []
        for q in range(4):
            t = P.stt(tmp[:, q, :], r[:, q, :], self.V("rwkv_r_k", q), k_[:, q, :], ALU.mult, ALU.mult)
            b = P.bank()
            bank.append((b, P.group(b, self.bk(b), [(self.C("bd"), tmp[:, q, :])], [t])))
        P.tt(Rf, r, pd, ALU.mult, [t_p])
        finish = self.mod_batch(range(18, 20), None, ["pool"] * 2)
        pc = self.small[:, 64:96]
        P.copy(pc.rearrange("p (q c) -> p q c", q=4), pd[:, :, 63:512:64])
        for q in range(4):
            t = P.tt(bonus[:, q, :], self.bk(bank[q][0]), v[:, q, :], ALU.mult, [bank[q][1]])
            P.bank_free[bank[q][0]] = [t]
        finish()
        if self.stop_at == "rprep":
            return
        y = fmat(h(6))
        self.chunks(Rf, Af, Bf, Kf, v, pc, y)
        sq, yc = fmat(h(10)), fmat(h(1))
        R = [h(2)[:, 0:512], h(2)[:, 512:1024]]
        ph = P.phase()
        self.split_free = [f + ph for f in self.split_free]
        self.raw_free = [f + ph for f in self.raw_free]
        toks = [None] * 8
        conv = self.conv
        for q in range(4):
            b = P.bank()
            t = P.group(b, self.bk(b), [(self.C("bd"), y[:, q, :])])
            t = P.stt(yc[:, q, :], self.bk(b), -1.0 / 64, y[:, q, :], ALU.mult, ALU.add, [t])
            P.bank_free[b] = [t]
            t_sq = P.act(sq[:, q, :], yc[:, q, :], ACT.Square, [t])
        self.stream([("w_out", c) for c in range(4)])
        for i in range(4):
            toks[i] = self.split(self.uh[:, i, :], self.ul[:, i, :], conv[:, i, :], [])
        banks, t = self.head_rsqrt(sq, t_sq, 1.0 / 64, 64e-5, None, R)
        made = []

        def rest(q, t):
            toks[4 + q] = P.tt(self.ul[:, 4 + q, :], y[:, q, :], self.uh[:, 4 + q, :].bitcast(F32), ALU.subtract, [t])

        for q in range(4):
            t = P.stt(yc[:, q, :], yc[:, q, :], self.V("rwkv_gn_w", q), self.bk(banks[q]), ALU.mult, ALU.mult, [t])
            P.bank_free[banks[q]] = [t]
            P.stt(yc[:, q, :], yc[:, q, :], self.V("rwkv_gn_b", q), bonus[:, q, :], ALU.add, ALU.add)
            t = P.tt(y[:, q, :], yc[:, q, :], g[:, q, :], ALU.mult)
            made.append((q, P.act(self.uh[:, 4 + q, :], y[:, q, :], ACT.Copy, [t])))
            if q:
                rest(*made[q - 1])
        rest(*made[3])

        self.pre_start(None, None)

        def evac(j, b, t):
            t = P.stt(self.xT[:, j, :], self.bk(b), self.modv[:, 16 + j:17 + j], self.xT[:, j, :],
                      ALU.mult, ALU.add, [t])
            self.pre_tile(j, t)
            return t

        self.gemm("w_out", lambda k: self.uh[:, k, :], lambda k: self.ul[:, k, :], toks, evac, preset=True)
        end = P.phase()
        self.split_free = [f + end for f in self.split_free]
        self.raw_free = [f + end for f in self.raw_free]

    def chunks(self, Rf, Af, Bf, Kf, v, pc, y):
        P, h = self.P, self.half
        mats = []
        for m in [h(i) for i in range(9, 18)] + self.raw[0:3]:
            mats += [m[:, 0:1024], m[:, 1024:2048]]
        sets = [mats[0:9], mats[9:18]]
        Bb, KM, VW, MT, X, spare = mats[18:24]
        st = [h(18)[:, 0:512], h(18)[:, 512:1024]]
        Z, SA = h(18)[:, 1024:1536], h(18)[:, 1536:2048]
        P.phase()
        for e, ms in (("pool", (Bb, KM, VW)), ("dve", (sets[0][0], sets[0][1])),
                      ("pool", (sets[1][0], sets[1][1], st[0]))):
            for m in ms:
                P.memset(m, 0.0, eng=e)
        zero = [("pool", P.cnt["pool"]), ("dve", P.cnt["dve"])]
        self.t_state = self.t_y = None
        ident = self.C("ident")

        def m4(ap):
            return ap.rearrange("p (u n) -> p u n", n=128)

        def bc(c):
            return c.unsqueeze(1).broadcast_to([128, 4, 128])

        inverse, ran = {}, {}

        def invert(g):
            Ab, Rb, TB, TK, TV, XT, NT, RBT, RKT = sets[g % 2]
            t_bd = []
            own = zero + ran.get(g - 2, [])
            shared = zero + inverse.get(g - 1, [])
            for n, (src, dst, free) in enumerate(((Bf, Bb, shared), (Af, Ab, own), (Kf, KM, shared), (v, VW, shared),
                                                  (Rf, Rb, own))):
                for hd in range(2):
                    p = slice(64 * hd, 64 * hd + 64)
                    for cc in range(2):
                        o = m4(dst)[p, 4 * cc:4 * cc + 4, 64 * hd:64 * hd + 64]
                        s = src[p, :, 64 * (2 * g + cc):64 * (2 * g + cc) + 64]
                        eng = ("act", "dve", "act", "pool", "dve")[n]
                        ld = P.copy(o, s, free, eng=eng)
                t_bd.append(ld)
            yield

            def product(l, rr, dst, mask, after):
                for cc in range(2):
                    b = P.bank()
                    for q in range(4):
                        u = 4 * cc + q
                        t = P.mm(self.ps[:, b, 128 * q:128 * q + 128], m4(l)[:, u, :], m4(rr)[:, u, :], True, True,
                                 after + P.bank_free[b] if q == 0 else (), inc=q == 3)
                    o = dst[:, 512 * cc:512 * cc + 512]
                    t = P.tt(m4(o), m4(self.bk(b)), bc(mask), ALU.mult, [t] + own)
                    P.bank_free[b] = [t]
                    tl.append(t)
                    yield

            tl = []
            yield from product(Bb, Ab, MT, self.C("strict"), t_bd[0:2])
            tm = list(tl)
            yield from product(Ab, Bb, X, self.C("m1"), [])
            t_x = {}
            for cc in range(2):
                c = slice(512 * cc, 512 * cc + 512)
                P.tt(m4(X[:, c]), m4(X[:, c]), bc(ident), ALU.add)
                P.tt(m4(XT[:, c]), m4(MT[:, c]), bc(self.C("t1")), ALU.mult)
                t_x[cc] = P.tt(m4(XT[:, c]), m4(XT[:, c]), bc(ident), ALU.add)
                yield
            for src, dst, ready in ((Bb, TB, []), (KM, TK, [t_bd[2]]), (VW, TV, [t_bd[3]])):
                for cc in range(2):
                    b = P.bank()
                    for q in range(4):
                        u = 4 * cc + q
                        o, i_ = self.ps[:, b, 128 * q:128 * q + 128], m4(src)[:, u, :]
                        t = P.op("pe", lambda e, o=o, i_=i_: e.transpose(o, i_, ident),
                                 ready + P.bank_free[b] if q == 0 else (), inc=q == 3)
                    t = P.copy(dst[:, 512 * cc:512 * cc + 512], self.bk(b), [t] + own, eng="act")
                    P.bank_free[b] = [t]
                    yield
            t_tr = t
            yield from product(KM, Ab, NT, self.C("strict"), [])
            yield from product(KM, Rb, RKT, self.C("incl"), [t_bd[4]])
            t_pe = [t_tr, ("pe", P.cnt["pe"])]
            t_pe = {0: list(t_pe), 1: list(t_pe)}
            extra = product(Bb, Rb, RBT, self.C("incl"), [])
            for lv in (2, 4, 8, 16, 32):
                tw = {}
                for cc in range(2):
                    c = slice(512 * cc, 512 * cc + 512)
                    t = P.tt(m4(KM[:, c]), m4(MT[:, c]), bc(self.C(f"t{lv}")), ALU.mult, tm + t_pe[cc], eng="pool")
                    b = P.bank()
                    for q in range(4):
                        u = 4 * cc + q
                        tp = P.mm(self.ps[:, b, 128 * q:128 * q + 128], m4(KM)[:, u, :], m4(X)[:, u, :], True, True,
                                  [t, t_x[cc]] + P.bank_free[b] if q == 0 else (), inc=q == 3)
                    tw[cc] = P.copy(VW[:, c], self.bk(b), [tp], eng="act")
                    P.bank_free[b] = [tw[cc]]
                    yield
                if lv == 2:
                    yield from extra
                for cc in range(2):
                    c = slice(512 * cc, 512 * cc + 512)
                    done = []
                    for l, rr, dst in ([(XT, VW, X), (VW, XT, XT)] if lv < 32 else [(VW, XT, XT)]):
                        b = P.bank()
                        for q in range(4):
                            u = 4 * cc + q
                            tp = P.mm(self.ps[:, b, 128 * q:128 * q + 128], m4(l)[:, u, :], m4(rr)[:, u, :],
                                      True, True, [tw[cc]] + P.bank_free[b] if q == 0 else (), inc=q == 3)
                        done.append((b, tp, dst))
                    for b, tp, dst in done:
                        t_x[cc] = P.tt(dst[:, c], dst[:, c], self.bk(b), ALU.add, [tp, done[-1][1]])
                        P.bank_free[b] = [t_x[cc]]
                    t_pe[cc] = [done[-1][1]]
                    yield
            self.t_inverse = {g: dict(t_x), **{k: w for k, w in self.t_inverse.items() if k == g - 1}}
            inverse[g] = [("pe", P.cnt["pe"]), ("dve", P.cnt["dve"])]

        def run(g):
            Ab, Rb, TB, TK, TV, XT, NT, RBT, RKT = sets[g % 2]
            t_x = self.t_inverse[g]
            for cc in range(2):
                ch = 2 * g + cc
                S0, S1 = st[ch % 2], st[1 - ch % 2]
                b = P.bank()
                for q in range(4):
                    u = 4 * cc + q
                    o = self.ps[:, b, 128 * q:128 * q + 128]
                    P.mm(o, m4(NT)[:, u, :], m4(TV)[:, u, :], True, False,
                         P.bank_free[b] + zero + [self.t_state] + inverse[g] if q == 0 else ())
                    t = P.mm(o, m4(Ab)[:, u, :], m4(S0)[:, q, :], False, True, (), inc=q == 3)
                tz = P.copy(Z, self.bk(b), [t], eng="act")
                P.bank_free[b] = [tz]
                yield
                b = P.bank()
                for q in range(4):
                    u = 4 * cc + q
                    t = P.mm(self.ps[:, b, 128 * q:128 * q + 128], m4(XT)[:, u, :], m4(Z)[:, q, :], True, True,
                             [tz, t_x[cc]] + P.bank_free[b] if q == 0 else (), inc=q == 3)
                ts = P.copy(SA, self.bk(b), [t, self.t_y])
                P.bank_free[b] = [ts]
                yield
                b = P.bank()
                for q in range(4):
                    u = 4 * cc + q
                    o = self.ps[:, b, 128 * q:128 * q + 128]
                    P.mm(o, ident, m4(S0)[:, q, :], True, False, P.bank_free[b] if q == 0 else ())
                    P.mm(o, m4(TK)[:, u, :], m4(TV)[:, u, :], False, False)
                    t = P.mm(o, m4(TB)[:, u, :], m4(SA)[:, q, :], False, True, [ts], inc=q == 3)
                pcc = pc.rearrange("p (q c) -> p q c", q=4)[:, :, ch:ch + 1].broadcast_to([128, 4, 128])
                self.t_state = P.tt(m4(S1), m4(self.bk(b)), pcc, ALU.mult, [t, self.t_y])
                P.bank_free[b] = [self.t_state]
                yield
                b = P.bank()
                for q in range(4):
                    u = 4 * cc + q
                    o = self.ps[:, b, 128 * q:128 * q + 128]
                    P.mm(o, m4(S0)[:, q, :], m4(Rb)[:, u, :], True, False, P.bank_free[b] if q == 0 else ())
                    P.mm(o, m4(TV)[:, u, :], m4(RKT)[:, u, :], False, False)
                    t = P.mm(o, m4(SA)[:, q, :], m4(RBT)[:, u, :], False, True, (), inc=q == 3)
                self.t_y = t
                for hd in range(2):
                    p = slice(64 * hd, 64 * hd + 64)
                    t = P.copy(y[p, :, 64 * ch:64 * ch + 64],
                               m4(self.bk(b))[p, :, 64 * hd:64 * hd + 64], [t], eng="act")
                P.bank_free[b] = [t]
                yield
            ran[g] = [self.t_y]

        self.t_inverse = {}
        norm = self.conv_norm(spare)
        for _ in invert(0):
            next(norm, None)
        for _ in norm:
            pass
        for g in range(4):
            inv = invert(g + 1) if g < 3 else iter(())
            for _ in run(g):
                for _ in range(4):
                    next(inv, None)
            for _ in inv:
                pass

    def peer(self):
        P, d = self.P, self.d
        scr = self.scr
        U = 4096
        self.ring([0, 1, 2, 3], [0, 1])
        self.stream([("peer_w_q", c) for c in range(8)])
        gf = self.small[:, 8:16]
        P.stt(gf, self.modv[:, 32:40], 1.0, self.V("norm_ffn_g", 0, 8), ALU.add, ALU.mult)
        self.pre_finish(None, None)
        t = self.token_sums(self.gel[0], self.small[:, 200:204], self.sums["acc"][0])
        tu = self.rms(lambda i: self.xT[:, i, :], 8, D, 1e-6, lambda i: gf[:, i:i + 1],
                      self.to_u(lambda i: self.modv[:, 24 + i:25 + i]), t=t)
        qF = fmat(scr[:, 0:2 * U])
        keys = scr[:, 2 * U:2 * U + 2048]
        t_keys = P.dma("keys", keys, d["keysT"], P.done())
        ada_free = P.done()

        base = 2 * U + 2048
        sc = scr[:, base:base + 2048].rearrange("p (j n) -> p j n", n=128)
        base += 2048
        cand = scr[:, base:base + 2048].rearrange("p (h a b) -> p h a b", h=8, a=16)
        base += 2048
        eq = sc.rearrange("p j n -> p (j n)").rearrange("p (h a b) -> p h a b", h=8, a=16)
        sm = []
        for w in (256, 256, 256, 128, 128, 128, 128, 128, 128, 128, 8, 8):
            sm.append(scr[:, base:base + w])
            base += w
        vals, idxu, idxf, best, posu, tmpu, ai, bi, i1, i2, s8, m8 = sm
        gate = tmpu
        IA, IB, WG = (scr[:, base + 512 * i:base + 512 * i + 512] for i in range(3))
        NA, NW = self.raw[0][:, 0:512], self.raw[0][:, 512:1024]
        base += 1536
        gk = scr[:, base:base + 128]
        base += 128
        it16 = self.C("iota")[:, 0:16]
        v3 = vals.rearrange("p (j k) -> p j k", k=16)
        x3 = idxu.bitcast(U32).rearrange("p (j k) -> p j k", k=16)
        f4 = idxf.rearrange("p (h two k) -> p h two k", two=2, k=16)
        v4 = vals.rearrange("p (h two k) -> p h two k", two=2, k=16)
        b3 = best.rearrange("p (h k) -> p h k", k=16)
        p3 = posu.bitcast(U32).rearrange("p (h k) -> p h k", k=16)

        def top16(rows):
            P.lag = 1
            for half in range(2):
                parts = [(s_, v_[:, 8 * half:8 * half + 8], i_[:, 8 * half:8 * half + 8]) for s_, v_, i_ in rows]
                for s_, vv, ii in parts:
                    P.op("dve", lambda e, s_=s_, vv=vv: e.max(vv, s_))
                for s_, vv, ii in parts:
                    P.op("dve", lambda e, s_=s_, vv=vv, ii=ii: e.max_index(ii, vv, s_))
                if half == 0:
                    for s_, vv, ii in parts:
                        P.op("dve", lambda e, s_=s_, vv=vv: e.match_replace(s_, vv, s_, -3.0e38))
            P.lag = 0

        def choose(tt):
            ts_ = slice(128 * tt, 128 * tt + 128)
            free, t_sc = [("dve", P.cnt["dve"])], {}

            def key_scores(j0):
                b = P.bank()
                for j in range(j0, j0 + 4):
                    t = P.mm(self.ps[:, b, 128 * (j - j0):128 * (j - j0) + 128], qF[:, j, ts_],
                             keys[:, 128 * j:128 * j + 128], True, True,
                             t_q[j0:j0 + 4] + [t_keys] + P.bank_free[b] if j == j0 else (), inc=j == j0 + 3)
                t = P.copy(sc[:, j0:j0 + 4, :], self.bk(b), [t] + free, eng="act")
                P.bank_free[b] = [t]
                t_sc[j0] = t

            for j in range(0, 16, 2):
                if j % 4 == 0:
                    for j0 in ((j,) if tt == 0 else (j, j + 4)):
                        if j0 < 16 and j0 not in t_sc:
                            key_scores(j0)
                P.gate["dve"] = P.gate["dve"] + [t_sc[j - j % 4]]
                top16([(sc[:, i, :], v3[:, i, :], x3[:, i, :]) for i in (j, j + 1)])
                yield
                yield
                if j % 4 == 2:
                    heads = (j // 2 - 1, j // 2)
                    for hh in heads:
                        P.tt(cand[:, hh], v4[:, hh, 0, :].unsqueeze(2).broadcast_to([128, 16, 16]),
                             v4[:, hh, 1, :].unsqueeze(1).broadcast_to([128, 16, 16]), ALU.add)
                        P.lag = 1
                    top16([(cand[:, hh].rearrange("p a b -> p (a b)"), b3[:, hh, :], p3[:, hh, :]) for hh in heads])
                    yield
                    yield
            P.copy(idxf, idxu.bitcast(U32))
            g3 = gate.rearrange("p (h k) -> p h k", k=16)
            t = P.tt(g3, b3, b3[:, :, 0:1].broadcast_to([128, 8, 16]), ALU.subtract, self.t_turned)
            t = P.act(gate, gate, ACT.Exp, [t])
            a_u, b_u = ai.bitcast(U32), bi.bitcast(U32)
            pu = posu.bitcast(U32)
            P.ts(a_u, pu, 4, None, ALU.logical_shift_right)
            P.ts(b_u, pu, 15, None, ALU.bitwise_and)
            P.reduce(s8, g3, ALU.add, [t])
            P.recip(s8, s8)
            tg = P.tt(g3, g3, s8.unsqueeze(2).broadcast_to([128, 8, 16]), ALU.mult)
            for src, side, dst in ((a_u, 0, i1), (b_u, 1, i2)):
                P.copy(gk, src)
                P.tt(eq, gk.rearrange("p (h k) -> p h k", k=16).unsqueeze(3).broadcast_to([128, 8, 16, 16]),
                     it16.unsqueeze(1).unsqueeze(1).broadcast_to([128, 8, 16, 16]), ALU.is_equal)
                yield
                P.tt(eq, eq, f4[:, :, side, :].unsqueeze(2).broadcast_to([128, 8, 16, 16]), ALU.mult)
                yield
                ti = P.reduce(dst.rearrange("p (h k) -> p h k", k=16), eq, ALU.add)
                yield
            b = P.bank()
            for n, src in enumerate((i1, i2, gate)):
                o = self.ps[:, b, 128 * n:128 * n + 128]
                t = P.op("pe", lambda e, o=o, src=src: e.transpose(o, src, self.C("ident")),
                         [ti, tg] + P.bank_free[b] if n == 0 else (), inc=n == 2)
            self.t_turned = [t]
            for n, dst in enumerate((IA, IB, WG)):
                t = P.copy(dst[:, ts_], self.ps[:, b, 128 * n:128 * n + 128], [t], eng="act")
            for src, dst in ((0, NA), (2, NW)):
                t = P.act(dst[:, ts_], self.ps[:, b, 128 * src:128 * src + 128], ACT.Identity, [t] + t_end, scale=-1.0)
            P.bank_free[b] = [t]
            self.t_choice[tt] = t
            yield

        t_q, ada, first = [], [], choose(0)

        def evac(j, b, t):
            t_q.append(P.copy(qF[:, j, :], self.bk(b), [t], eng="act"))
            t = t_q[-1]
            if j == 7:
                ada.extend(self.mod_load((20, 21), (scr[:, 18432:20480], scr[:, 20480:22528]), ada_free))
            if j % 4 == 3:
                for _ in range(6):
                    next(first)
            return t

        self.t_turned, self.t_choice = [], {}
        self.gemm("peer_w_q", lambda k: self.uh[:, k, :], lambda k: self.ul[:, k, :], tu, evac, preset=True)
        t_end = P.done()
        G = d["gates"]
        stage = [self.w01[:, 0:U].rearrange("p (k t) -> p k t", t=32),
                 self.w01[:, U:2 * U].rearrange("p (k t) -> p k t", t=32)]
        st_free = [t_end, t_end]
        oh = [scr[:, base + 1024 * i:base + 1024 * i + 1024] for i in range(4)]
        assert base + 4096 <= 22528
        oh_free = [[] for _ in range(4)]
        iota = self.C("iota")
        t_store = []

        def put_down():
            if self.placed is None:
                return
            blk, q, b, t = self.placed
            self.placed, s = None, blk % 2
            t = P.copy(stage[s][:, :, 4 * q:4 * q + 4].rearrange("p k t -> p t k"),
                       self.bk(b).rearrange("p (t k) -> p t k", k=128), [t] + st_free[s], eng="act")
            P.bank_free[b] = [t]
            if q == 7:
                st_free[s] = [P.dma(f"gst{s}", G[blk], stage[s].rearrange("p k t -> p (k t)"), [t])]
                t_store.append(st_free[s][0])

        self.placed, self.put_down = None, put_down

        def place(tt, b_dve, acts):
            for blk in range(4 * tt, 4 * tt + 4):
                for q in range(8):
                    n = blk * 8 + q
                    o = oh[n % 4]
                    B4, A4 = o[:, 0:512], o[:, 512:1024]
                    t0 = blk * 32 + 4 * q
                    free = oh_free[n % 4] + [self.t_choice[tt]]
                    tb = []
                    P.lag = None
                    if q % 8 in b_dve:
                        tb.append(P.tt(B4.rearrange("p (t n) -> p t n", n=128),
                                       iota.unsqueeze(1).broadcast_to([128, 4, 128]),
                                       IB[:, t0:t0 + 4].unsqueeze(2).broadcast_to([128, 4, 128]),
                                       ALU.is_equal, after=free))
                    else:
                        for i in range(4):
                            tb.append(P.ts(B4[:, 128 * i:128 * i + 128], iota, IB[:, t0 + i:t0 + i + 1], None,
                                           ALU.is_equal, after=free, eng="pool"))
                    on_act = acts[q % len(acts)]
                    ta = []
                    for i in range(on_act):
                        ta = [P.act(A4[:, 128 * i:128 * i + 128], iota, ACT.Abs, free,
                                    bias=NA[:, t0 + i:t0 + i + 1])]
                    for i in range(on_act):
                        A1, col = A4[:, 128 * i:128 * i + 128], slice(t0 + i, t0 + i + 1)
                        tr = P.act(A1, A1, ACT.Relu, ta, bias=WG[:, col], scale=NW[:, col])
                    if on_act:
                        tb.append(tr)
                    for i in range(on_act, 4):
                        A1, col = A4[:, 128 * i:128 * i + 128], slice(t0 + i, t0 + i + 1)
                        ta = P.ts(A1, iota, IA[:, col], WG[:, col], ALU.is_equal, ALU.mult, after=free)
                    P.lag = 0
                    self.put_down()
                    b = P.bank()
                    for i in range(4):
                        c = slice(128 * i, 128 * i + 128)
                        t = P.mm(self.ps[:, b, c], B4[:, c], A4[:, c], True, True,
                                 [ta] + tb + P.bank_free[b] if i == 0 else (), inc=i == 3)
                    oh_free[n % 4] = [t]
                    self.placed = (blk, q, b, t)
                    yield

        ada += self.mod_load((22, 23), self.raw[1:3], self.raw_free[1] + self.raw_free[2])
        for n, (tw, w) in enumerate(ada):
            ada[n] = (self.mod_product(w.rearrange("p (k n) -> p k n", n=256), tw, "pool"), w)
        for n, _ in enumerate(first):
            if n == 4:
                self.mod_batch(range(20, 24), ada, ["made"] * 4)()
                self.raw_free[1] = self.raw_free[2] = P.done()
        rest = (s for tt in range(1, 4) for s in choose(tt))
        places = (s for tt in range(4) for s in place(tt, *(((), (2, 1)) if tt < 3 else ((0, 2, 4, 6), (0,)))))
        for _ in rest:
            next(places)
        self.ring([1, 2, 3, 0], [2, 3, 0, 1])
        self.stream(self.dense_order("peer_uT", "peer_v", 32), 2)
        for i in (2, 3):
            self.split_free[i] = self.split_free[i] + P.done()
        for n, _ in enumerate(places):
            if n in (6, 12):
                self.ready.append(self.prepare(len(self.ready)))
            pass
        put_down()
        ph = P.phase()
        self.gates, self.t_gates, self.gate_ready = G.rearrange("b p (k t) -> p b k t", t=32), t_store[-2:], ph
        for i in (0, 1):
            self.split_free[i] = self.split_free[i] + ph
        self.raw_free[0] = self.raw_free[0] + ph
        self.queue([("w_qkv_a_2", c) for c in range(12)] + [("w_o_a_2", c) for c in range(4)])
        self.lambdas()
        self.two_norms = True
        gg = self.small[:, 248:256]
        P.tt(gg, self.V("final_g", 0, 8), self.V("attn_norm_g_2", 0, 8), ALU.mult)
        self.pre_start(self.A, lambda j: gg[:, j:j + 1], lambda j: self.V("final_g", j))
        self.dense("peer_uT", "peer_v", 32, True, lambda j: self.modv[:, 40 + j:41 + j], [], self.A, self.B)
        P.phase(("act", "dve", "pool"))

    def dense_order(self, first, second, groups):
        order = [(first, 0), (first, 1)]
        for g in range(groups):
            if g + 1 < groups:
                order += [(first, 2 * g + 2), (first, 2 * g + 3)]
            order += [(second, 2 * g), (second, 2 * g + 1)]
        return order

    def dense(self, first, second, groups, gated, scale, tok, u, hidden, rs=None):
        P = self.P
        Gt = [self.scr[:, A_G - A_W2 + 2048 * i:A_G - A_W2 + 2048 * i + 2048] for i in range(2)]
        gt_free = [[], []]
        gel_free = [list(tok) for _ in range(4)]
        th_free = [list(tok), list(tok)]

        late = []

        def scores(g):
            s2 = g % 2
            if gated:
                tg = P.dma(f"gld{s2}", Gt[s2].rearrange("p (b k) -> p b k", b=16),
                           self.gates[:, :, 4 * g:4 * g + 4, :].rearrange("p b k t -> p b (k t)"),
                           self.t_gates + self.gate_ready + gt_free[s2])
                gv = Gt[s2].rearrange("p (b k t) -> p b k t", b=16, t=32)
            for half in range(2):
                h, wh, wl, tw = self.take()
                wh, wl = (a.rearrange("p (k n) -> p k n", n=256) for a in (wh, wl))
                for j in range(2):
                    e = 2 * half + j
                    b = P.bank()
                    s = slice(128 * j, 128 * j + 128)
                    for k in range(8):
                        for i, (l, r) in enumerate(self.terms(wh[:, k, s], wl[:, k, s], *u[k])):
                            after = [tok[k]] if tok and i == 0 else []
                            if k == 0 and i == 0:
                                after = after + [tw] + P.bank_free[b]
                            t = P.mm(self.bk(b), l, r, k == 0 and i == 0, k == 7 and i == 2, after,
                                     inc=k == 7 and i == 2)
                    if rs is not None and g == 0 and e == 0:
                        self.pre_stats()
                    if rs is not None and g == 0 and e == 1:
                        self.scale_tile(rs)
                        t2 = finish(*late.pop())
                    if j == 0:
                        self.ahead(2)
                    x = self.gel[e]
                    t2 = P.act(x, self.bk(b), ACT.Gelu if gated else ACT.Relu, [t] + gel_free[e])
                    P.bank_free[b] = [t2]

                    def finish(e, x, t2):
                        if gated:
                            x3 = x.rearrange("p (b t) -> p b t", t=32)
                            t2 = P.tt(x3, x3, gv[:, :, e, :], ALU.mult, [t2, tg])
                            gt_free[s2] = [t2]
                        else:
                            P.tt(x, x, rs, ALU.mult, [t2])
                            t2 = P.tt(x, x, x, ALU.mult)
                        t2 = self.split(*hidden[4 * s2 + e], x, [t2] + th_free[s2])
                        gel_free[e] = [t2]
                        return t2

                    if rs is not None and g == 0 and e == 0:
                        late.append((e, x, t2))
                    else:
                        t2 = finish(e, x, t2)
                self.split_free[h] = [t]
            return t2

        def values(g, t_h):
            s2 = g % 2
            ch = [self.take(), self.take()]
            for j in range(8):
                b = P.bank()
                pairs = []
                for e in range(4):
                    c = slice(1024 * (e % 2) + 128 * j, 1024 * (e % 2) + 128 * j + 128)
                    pairs += self.terms(ch[e // 2][1][:, c], ch[e // 2][2][:, c], *hidden[4 * s2 + e])
                t = P.group(b, self.bk(b), pairs, [t_h, ch[0][3], ch[1][3]])
                if j in (1, 4):
                    self.ahead(1 if j == 1 else 2, 2)
                if scale is None:
                    t2 = P.tt(self.xT[:, j, :], self.xT[:, j, :], self.bk(b), ALU.add, [t])
                else:
                    t2 = P.stt(self.xT[:, j, :], self.bk(b), scale(j), self.xT[:, j, :], ALU.mult, ALU.add, [t])
                P.bank_free[b] = [t2]
                if g == groups - 1:
                    self.pre_tile(j, t2)
            for c in ch:
                self.split_free[c[0]] = [t]
            th_free[s2] = [t]

        t_h = scores(0)
        for g in range(groups):
            nxt = scores(g + 1) if g + 1 < groups else None
            values(g, t_h)
            t_h = nxt

    def pre_start(self, dst, gain, first=None):
        self.pre = dict(dst=dst, gain=gain, first=first, tok=[None] * 8, free=[[], []], t0=None, acc=[None, None],
                        last=None)

    def pre_tile(self, j, t):
        P, p, g = self.P, self.pre, self.gel
        x = self.xT[:, j, :]
        if p["t0"] is None:
            p["t0"] = P.done()
        self.pre_retire()
        after = [t] + p["t0"]
        two = p["first"] is not None
        if two:
            sums = [(g[0], g[1], 1.0, 0, "dve"), (g[2], g[3], p["first"](j), 1, "pool")]
        else:
            sums = [(g[0], g[1 + j % 2], 1.0, j % 2, "dve")]
        th = None
        if p["dst"] is not None:
            th = P.act(p["dst"][j][0], x, ACT.Identity, after, scale=p["gain"](j))
        made = [P.act(sq if j else acc, x, ACT.Square, after + p["free"][n], scale=scale)
                for acc, sq, scale, n, eng in sums]
        p["last"] = (j, x, th, sums, made)

    def pre_retire(self):
        P, p = self.P, self.pre
        if p["last"] is None:
            return
        j, x, th, sums, made = p["last"]
        p["last"] = None
        for m, ((acc, sq, scale, n, eng), t) in enumerate(zip(sums, made)):
            if j:
                t = P.tt(acc, acc, sq, ALU.add, [t], eng=eng)
                p["free"][n] = [t]
            p["acc"][m] = t
        if p["dst"] is not None:
            hi, lo = p["dst"][j]
            p["tok"][j] = P.stt(lo, x, p["gain"](j), hi.bitcast(F32), ALU.mult, ALU.subtract, [th])

    def pre_finish(self, dst, gain):
        if self.pre is None:
            self.pre_start(dst, gain)
            for j in range(8):
                self.pre_tile(j, None)
        self.pre_retire()
        self.sums, self.pre = self.pre, None
        self.two = self.sums["first"] is not None
        return self.sums["tok"]

    def pre_stats(self):
        P, p = self.P, self.sums
        r, r2, both = self.small[:, 200:204], self.small[:, 240:244], self.small[:, 244:248]
        t = self.token_sums(self.gel[0], r, p["acc"][0])
        if self.two:
            self.token_sums(self.gel[2], r2, p["acc"][1])
        t = P.ts(r, r, 1.0 / D, 1e-6, ALU.mult, ALU.add, [t])
        t = P.act(r, r, ACT.Sqrt, [t])
        self.t_r = P.recip(r, r, [t])
        if self.two:
            P.tt(r2, r2, r, ALU.mult)
            P.tt(r2, r2, r, ALU.mult)
            t = P.ts(r2, r2, 1.0 / D, 1e-6, ALU.mult, ALU.add)
            t = P.act(r2, r2, ACT.Sqrt, [t])
            P.recip(r2, r2, [t])
            self.t_r = P.tt(both, r, r2, ALU.mult)

    def scale_tile(self, dst):
        P = self.P
        b = P.bank()
        t = self.spread(b, self.small[:, 200:204])
        t = P.copy(dst, self.bk(b), [t])
        P.bank_free[b] = [t]
        return t

    def last_norm(self, out):
        P = self.P
        self.pre_finish(None, None)
        self.pre_stats()
        b = P.bank()
        t = self.spread(b, self.small[:, 200:204])
        free = [[] for _ in range(4)]
        for i in range(8):
            y = self.gel[i % 4]
            t = P.stt(y, self.xT[:, i, :], self.V("final_norm_g_2", i), self.bk(b), ALU.mult, ALU.mult,
                      [t] + free[i % 4])
            free[i % 4] = [P.dma(f"out{i % 4}", out[:, i, :], y, [t])]

    def add_x(self, j, b, t):
        t = self.P.tt(self.xT[:, j, :], self.xT[:, j, :], self.bk(b), ALU.add, [t])
        self.pre_tile(j, t)
        return t

    def gain(self, name, off=0):
        return lambda j: self.V(name, off + j)

    def rope(self, x, t, tmp):
        P = self.P
        b = P.bank()
        t = P.group(b, self.bk(b), [(self.C("rot"), x)], [t])
        t1 = P.tt(tmp, self.bk(b), self.rs, ALU.mult, [t])
        P.bank_free[b] = [t1]
        P.tt(x, x, self.rc, ALU.mult)
        return P.tt(x, x, tmp, ALU.add)

    def values_T(self, name, nk, chunks, xh, xl, dst, tok, scale=None):
        P = self.P
        cw = TILES[name][0] // nk
        for n, c in enumerate(chunks):
            h, wh, wl, tw = self.take()
            wh, wl = (a.rearrange("p (k n) -> p k n", n=cw) for a in (wh, wl))
            for c0 in range(0, cw, 512):
                w = min(512, cw - c0)
                for tt in range(4):
                    b = P.bank()
                    s = slice(128 * tt, 128 * tt + 128)
                    pairs = []
                    for k in range(nk):
                        pairs += [(l, r) for r, l in self.terms(wh[:, k, c0:c0 + w], wl[:, k, c0:c0 + w],
                                                                xh(k)[:, s], xl(k)[:, s])]
                    t = P.group(b, self.ps[:, b, 0:w], pairs, [tw] + tok)
                    if tt == 0:
                        self.ahead(2)
                    o = dst[:, tt, n * cw + c0:n * cw + c0 + w]
                    if scale is None:
                        t2 = P.copy(o, self.ps[:, b, 0:w], [t], eng="act" if tt % 2 else "dve")
                    elif tt % 2:
                        t2 = P.act(o, self.ps[:, b, 0:w], ACT.Identity, [t, self.t_r], scale=scale[:, tt:tt + 1])
                    else:
                        t2 = P.ts(o, self.ps[:, b, 0:w], scale[:, tt:tt + 1], None, ALU.mult, after=[t])
                    P.bank_free[b] = [t2]
            self.split_free[h] = [t]
            self.ahead(2, 0)

    def softmax_rows(self, b, width, scale, e, stat, tok):
        P = self.P
        P.reduce(stat[:, 0:1], self.ps[:, b, 0:width], ALU.max, [tok])
        t = P.ts(stat[:, 1:2], stat[:, 0:1], -scale, None, ALU.mult)
        t = P.act(e[:, 0:width], self.ps[:, b, 0:width], ACT.Exp, [t], bias=stat[:, 1:2], scale=scale,
                  accum=stat[:, 2:3])
        P.bank_free[b] = [t]
        return t

    def turn(self, a, aT, nb, t, free):
        P = self.P
        b = P.bank()
        for kb in range(nb):
            o, i_ = self.ps[:, b, 128 * kb:128 * kb + 128], a[:, 128 * kb:128 * kb + 128]
            t = P.op("pe", lambda e, o=o, i_=i_: e.transpose(o, i_, self.C("ident")),
                     [t] + P.bank_free[b] if kb == 0 else (), inc=kb == nb - 1)
        t2 = P.copy(aT[:, 0:128 * nb], self.ps[:, b, 0:128 * nb], [t] + free, eng="act")
        P.bank_free[b] = [t2]
        return t2, t

    def attend(self, scores, softmaxed, v, o, aT, heads=8):
        P = self.P
        at_free = [[] for _ in range(4)]
        self.e_free = [[] for _ in range(4)]
        blocks = [(hh, qb) for hh in range(heads) for qb in range(4)]
        pend = []

        turned = {}

        ready = {}

        def turn(n):
            hh, qb = blocks[n]
            e, t = ready[n]
            turned[n], tp = self.turn(e, aT[n % 4], qb + 1, t, at_free[n % 4])
            self.e_free[n % 4] = [tp]

        def meet(n):
            hh, qb = blocks[n]
            b = P.bank()
            t = P.group(b, self.ps[:, b, 0:128], [(v[:, kb, 128 * hh:128 * hh + 128],
                                                   aT[n % 4][:, 128 * kb:128 * kb + 128]) for kb in range(qb + 1)],
                        [turned[n]])
            at_free[n % 4] = [t]
            o(hh, qb, b, t)

        last = len(blocks)
        for n in range(last + 3):
            if n < last:
                pend.append(scores(n, *blocks[n]))
            if 1 <= n <= last:
                ready[n - 1] = softmaxed(n - 1, *blocks[n - 1], pend[n - 1])
            if 2 <= n <= last + 1:
                turn(n - 2)
            if n >= 3:
                meet(n - 3)

    def lambdas(self):
        P = self.P
        lp = self.small[:, 100:102]
        P.tt(lp[:, 0:1], self.V("lambda", 0), self.V("lambda", 1), ALU.mult)
        t = P.tt(lp[:, 1:2], self.V("lambda", 2), self.V("lambda", 3), ALU.mult)
        b = P.bank()
        t = P.group(b, self.ps[:, b, 0:2], [(self.C("ones"), lp)], [t])
        t = P.act(lp, self.ps[:, b, 0:2], ACT.Exp, [t])
        P.bank_free[b] = [t]
        nl = self.small[:, 102:103]
        P.tt(nl, lp[:, 1:2], lp[:, 0:1], ALU.subtract, [t])
        P.ts(nl, nl, -0.2, None, ALU.add)
        sg8 = self.small[:, 103:104]
        P.ts(sg8, self.V("subln_g_2"), 0.8, None, ALU.mult)

    def diff(self):
        P, d, scr = self.P, self.d, self.scr
        U = 4096
        self.begin([("w_qkv_a_2", c) for c in range(12)] + [("w_o_a_2", c) for c in range(4)])
        nl, sg8 = self.small[:, 102:103], self.small[:, 103:104]
        if not self.two_norms:
            self.lambdas()
        tu = self.pre_finish(self.A, self.gain("attn_norm_g_2"))
        both = self.small[:, 244:248] if self.two else self.small[:, 200:204]
        self.rc, self.rs = scr[:, 12288:12800], scr[:, 12800:13312]
        t_cs = P.dma("rope", scr[:, 12288:13312], d["rope"], P.done())
        q, k = fmat(self.w01[:, 0:U]), fmat(self.w01[:, U:2 * U])
        v = scr[:, 2 * U:3 * U].rearrange("p (t n) -> p t n", n=1024)
        o = [scr[:, 13312 + 512 * i:13824 + 512 * i] for i in range(8)]
        tmps = [scr[:, 13312 + 512 * i:13824 + 512 * i] for i in range(4)]
        roped = []

        def scale_tables():
            b = P.bank()
            t = self.spread(b, both)
            P.tt(self.rc, self.rc, self.bk(b), ALU.mult, [t, t_cs])
            P.bank_free[b] = [P.tt(self.rs, self.rs, self.bk(b), ALU.mult)]
            if self.two:
                b = P.bank()
                t = self.spread(b, self.small[:, 200:204])
                for i in range(8):
                    t = P.stt(self.xT[:, i, :], self.xT[:, i, :], self.V("final_g", i), self.bk(b), ALU.mult,
                              ALU.mult, [t])
                P.bank_free[b] = [t]

        def turn_rope():
            i, x, t = roped.pop(0)
            self.t_rope = self.rope(x, t, tmps[i % 4])

        def evac(j, b, t):
            if j == 0:
                self.pre_stats()
            if j == 1:
                scale_tables()
            x = q[:, j, :] if j < 8 else k[:, j - 8, :]
            t = P.copy(x, self.bk(b), [t], eng="act")
            roped.append((j, x, t))
            if len(roped) > 1:
                turn_rope()
            return t

        uh, ul = (lambda kk: self.uh[:, kk, :]), (lambda kk: self.ul[:, kk, :])
        self.gemm("w_qkv_a_2", uh, ul, tu, evac, chunks=range(8), preset=True)
        while roped:
            turn_rope()
        self.values_T("w_qkv_a_2", 8, range(8, 12), uh, ul, v, [], both)
        ph = P.done()
        E = [self.un[:, 1024 + 1024 * i:2048 + 1024 * i] for i in range(4)]
        aT = [scr[:, 20480 + 512 * i:20992 + 512 * i] for i in range(4)]
        P.gate["act"] = P.gate["act"] + ph

        def scores(n, hh, qb):
            w = 128 * (qb + 1)
            qs = slice(128 * qb, 128 * qb + 128)
            ee = E[n % 4]
            for c in range(2):
                st = self.small[:, 104 + 8 * (n % 4) + 4 * c:108 + 8 * (n % 4) + 4 * c]
                p = slice(64 * c, 64 * c + 64)
                b = P.bank()
                P.mm(self.ps[:, b, 0:w], q[p, hh, qs], k[p, hh, 0:w], True, False, ph + P.bank_free[b])
                t = P.mm(self.ps[:, b, 128 * qb:w], self.C("ident"), self.C("causal"), False, True, (), inc=True)
                P.gate["act"] = P.gate["act"] + self.e_free[n % 4]
                t = self.softmax_rows(b, w, 0.125, ee[:, 512 * c:512 * c + 512], st, t)
            return t

        def softmaxed(n, hh, qb, t):
            w = 128 * (qb + 1)
            ee = E[n % 4]
            e0, e1 = ee[:, 0:w], ee[:, 512:512 + w]
            s0 = self.small[:, 104 + 8 * (n % 4):108 + 8 * (n % 4)]
            s1 = self.small[:, 108 + 8 * (n % 4):112 + 8 * (n % 4)]
            P.recip(s0[:, 3:4], s0[:, 2:3], [t])
            P.recip(s1[:, 3:4], s1[:, 2:3])
            P.ts(s1[:, 3:4], s1[:, 3:4], nl, None, ALU.mult)
            P.ts(e1, e1, s1[:, 3:4], None, ALU.mult)
            return ee, P.stt(e0, e0, s0[:, 3:4], e1, ALU.mult, ALU.add)

        stat = self.small[:, 140:172]
        sq = [self.un[:, 512 * i:512 * i + 512] for i in range(2)]
        sq_free = [[], []]
        late = []

        def sums(hh, t):
            b = P.bank()
            for i in range(4):
                t = P.mm(self.ps[:, b, i:i + 1], sq[hh % 2][:, 128 * i:128 * i + 128], self.C("ones")[:, 0:1],
                         True, True, [t] + P.bank_free[b] if i == 0 else (), inc=i == 3)
            sq_free[hh % 2] = [t]
            P.bank_free[b] = [P.copy(stat[:, 4 * hh:4 * hh + 4], self.ps[:, b, 0:4], [t])]

        def put(hh, qb, b, t):
            P.bank_free[b] = [P.copy(o[hh][:, 128 * qb:128 * qb + 128], self.ps[:, b, 0:128], [t], eng="act")]
            if late and qb == 1:
                sums(*late.pop(0))
            if qb == 3:
                late.append((hh, P.act(sq[hh % 2], o[hh], ACT.Square, sq_free[hh % 2])))

        self.attend(scores, softmaxed, v, put, aT)
        self.widen()
        self.queue(self.dense_order("w_up_2_0", "w_down_2_0", 8))
        sums(*late.pop(0))
        P.ts(stat, stat, 1.0 / 128, 1e-5, ALU.mult, ALU.add)
        t = P.act(stat, stat, ACT.Sqrt, [("dve", P.cnt["dve"]), ("pe", P.cnt["pe"])])
        P.recip(stat, stat, [t])
        toks = []
        for hh in range(8):
            b = P.bank()
            t = self.spread(b, stat[:, 4 * hh:4 * hh + 4])
            t = P.stt(o[hh], o[hh], sg8, self.bk(b), ALU.mult, ALU.mult, [t])
            P.bank_free[b] = [t]
            toks.append(self.split(self.uh[:, hh, :], self.ul[:, hh, :], o[hh], [t]))
        self.pre_start(self.B, self.gain("mlp_norm_g_2"))
        self.gemm("w_o_a_2", uh, ul, toks, self.add_x, preset=True)
        P.phase(("act", "dve", "pool"))

    def mlp(self, l):
        P = self.P
        first, second = f"w_up_2_{l}", f"w_down_2_{l}"
        if not self.queued:
            self.ring([0, 1, 2, 3], [2, 3, 0, 1])
            self.stream(self.dense_order(first, second, 8))
        self.queued = False
        tu = self.pre_finish(self.B, self.gain("mlp_norm_g_2", 8 * l))
        if l == 0:
            self.queue(self.mla_order())
            self.pre_start(self.B, self.gain("kv_in_norm_g_2"))
        else:
            self.pre_start(None, None)
        self.dense(first, second, 8, False, None, tu, self.B, self.A, self.scr[:, 16384:16896])
        P.phase(("act", "dve", "pool"))

    def mla_order(self):
        return ([("w_dkv_2", c) for c in range(3)] + [("ukv_k", 0), ("ukv_v", 0)]
                + [("w_dq_2", c) for c in range(3)] + [("uq_n", 0), ("uq_n", 1), ("uq_r", 0)]
                + [("w_o_b_2", c) for c in range(4)])

    def mla(self):
        P, d, scr = self.P, self.d, self.scr
        U = 4096
        self.begin(self.mla_order())
        tu = self.pre_finish(self.B, self.gain("kv_in_norm_g_2"))
        kn = fmat(self.w01[:, 0:U])
        v = self.w01[:, U:2 * U].rearrange("p (t n) -> p t n", n=1024)
        qn = fmat(scr[:, 2 * U:3 * U])
        qr = fmat(scr[:, 12288:14336])
        kr = fmat(scr[:, 14336:15360])
        tmps = [scr[:, 16384 + 512 * i:16896 + 512 * i] for i in range(3)]
        cc = fmat(scr[:, 17920:19456])
        self.rc, self.rs = scr[:, 19456:19968], scr[:, 19968:20480]
        rms = self.gel[3]
        t_cs = P.dma("rope", scr[:, 19456:20480], d["rope"], P.done())
        uh, ul = (lambda kk: self.uh[:, kk, :]), (lambda kk: self.ul[:, kk, :])
        bh, bl = (lambda kk: self.B[kk][0]), (lambda kk: self.B[kk][1])
        got, held = {}, []

        def evac(j, b, t):
            if j == 0:
                self.pre_stats()
                held.append((b, t))
                return None
            if j == 1:
                self.scale_tile(rms)
                b0, t0 = held.pop()
                got[0] = P.tt(cc[:, 0, :], self.bk(b0), rms, ALU.mult, [t0])
                P.bank_free[b0] = [got[0]]
            got[j] = P.tt(cc[:, j, :] if j < 2 else tmps[1], self.bk(b), rms, ALU.mult, [t])
            return got[j]

        self.gemm("w_dkv_2", bh, bl, tu, evac, preset=True)
        t_dkv = [("pe", P.cnt["pe"])]
        P.gate["dve"] = P.gate["dve"] + [t_cs]
        self.rope(tmps[1], got[2], tmps[0])
        tc = self.rms(lambda i: cc[:, i, :], 2, 256, 1e-6, lambda i: self.V("kv_norm_g_2", i), self.to_u(),
                      after=[got[2]])

        def evac_k(j, b, t):
            return P.copy(kn[:, j, :], self.bk(b), [t], eng="act" if j % 2 else "dve")

        tu, g2 = [], self.gain("attn_norm_g_2", 8)
        for j in range(8):
            hi, lo = self.B[j]
            t = P.act(hi, self.xT[:, j, :], ACT.Identity, t_dkv, scale=g2(j))
            tu.append(P.stt(lo, self.xT[:, j, :], g2(j), hi.bitcast(F32), ALU.mult, ALU.subtract, [t]))
        self.gemm("ukv_k", uh, ul, tc, evac_k, preset=True)
        self.values_T("ukv_v", 2, [0], uh, ul, v, [])

        def evac_c(j, b, t):
            got[j] = P.tt(cc[:, j, :], self.bk(b), rms, ALU.mult, [t])
            return got[j]

        self.gemm("w_dq_2", bh, bl, tu, evac_c, preset=True)
        P.memset(kr, 0.0, [("pe", P.cnt["pe"])])
        P.copy(kr[0:64, 0, :], tmps[1][0:64, :])
        P.copy(kr[64:128, 1, :], tmps[1][64:128, :])
        tc = self.rms(lambda i: cc[:, i, :], 3, 384, 1e-6, lambda i: self.V("q_norm_g_2", i), self.to_u(),
                      after=[got[2]])

        def evac_q(j, b, t):
            return P.copy(qn[:, j, :], self.bk(b), [t], eng="act" if j % 2 else "dve")

        def evac_r(j, b, t):
            t = P.copy(qr[:, j, :], self.bk(b), [t], eng="act")
            got[10 + j] = t
            return t

        self.gemm("uq_n", uh, ul, tc, evac_q, preset=True)
        self.gemm("uq_r", uh, ul, tc, evac_r, preset=True)
        for j in range(4):
            self.rope(qr[:, j, :], got[10 + j], tmps[2 * (j % 2)])
        ph = P.done()
        E = self.gel
        aT = [scr[:, 17920 + 512 * i:18432 + 512 * i] for i in range(4)]
        o = [scr[:, 8192 + 512 * i:8704 + 512 * i] for i in range(8)]
        scale = 192.0 ** -0.5
        P.gate["act"] = P.gate["act"] + ph

        def scores(n, hh, qb):
            w = 128 * (qb + 1)
            qs = slice(128 * qb, 128 * qb + 128)
            st = self.small[:, 104 + 4 * (n % 4):108 + 4 * (n % 4)]
            b = P.bank()
            P.mm(self.ps[:, b, 0:w], qn[:, hh, qs], kn[:, hh, 0:w], True, False, ph + P.bank_free[b])
            P.mm(self.ps[:, b, 0:w], qr[:, hh // 2, qs], kr[:, hh % 2, 0:w], False, False)
            t = P.mm(self.ps[:, b, 128 * qb:w], self.C("ident"), self.C("causal"), False, True, (), inc=True)
            P.gate["act"] = P.gate["act"] + self.e_free[n % 4]
            return self.softmax_rows(b, w, scale, E[n % 4], st, t)

        def softmaxed(n, hh, qb, t):
            w = 128 * (qb + 1)
            st = self.small[:, 104 + 4 * (n % 4):108 + 4 * (n % 4)]
            P.recip(st[:, 3:4], st[:, 2:3], [t])
            return E[n % 4], P.ts(E[n % 4][:, 0:w], E[n % 4][:, 0:w], st[:, 3:4], None, ALU.mult)

        toks = [None] * 8

        def put(hh, qb, b, t):
            hi = self.uh[:, hh, 128 * qb:128 * qb + 128]
            t1 = P.copy(hi, self.ps[:, b, 0:128], [t], eng="act")
            toks[hh] = P.tt(self.ul[:, hh, 128 * qb:128 * qb + 128], self.ps[:, b, 0:128], hi.bitcast(F32),
                            ALU.subtract, [t1])
            P.bank_free[b] = [toks[hh]]

        self.attend(scores, softmaxed, v, put, aT)
        self.widen()
        self.queue(self.dense_order("w_up_2_1", "w_down_2_1", 8))
        self.pre_start(self.B, self.gain("mlp_norm_g_2", 8))
        self.gemm("w_o_b_2", uh, ul, toks, self.add_x, preset=True)
        P.phase(("act", "dve", "pool"))

    def dump(self, outs, ap, name="out"):
        self.P.dma(name, outs, ap, self.P.done())

    def program(self, out, stop):
        xo = out.rearrange("(k p) n -> p k n", p=128)
        self.start()
        steps = [("mix", self.mixing), ("peer", self.peer), ("h1", self.diff), ("h2", lambda: self.mlp(0)), ("h3", self.mla), ("h4", lambda: self.mlp(1)),
                 ("final", lambda: self.last_norm(xo))]
        skip = stop is not None and stop.startswith("only:")
        if stop == "only:peer":
            for i in range(0, 20, 4):
                self.mod_batch(range(i, i + 4))()
        for name, step in steps:
            if skip and name != stop[5:]:
                continue
            step()
            if name == stop or skip:
                break
        if stop not in (None, "final"):
            self.dump(xo, self.xT)


def build(nc, dram, out, stop=None):
    with ExitStack() as ctx:
        dram = {**dram, "gates": nc.dram_tensor("gates", (16, 128, 4096), F32).ap()}
        n = Net(nc, ctx, dram, stop)
        P = n.P
        n.t_state = n.t_y = None
        n.program(out, stop)
        final = [(s, v) for s, v in P.cnt.items() if s.startswith("out")]
        P.q["sp"].append((final, lambda e: None, None, 0))
        block = ctx.enter_context(nc.Block())

        @block.sync
        def _(e):
            P.play("sp", e)

        @block.gpsimd
        def _(e):
            P.play("pool", e)

        @block.vector
        def _(e):
            P.play("dve", e)

        @block.scalar
        def _(e):
            P.play("act", e)

        @block.tensor
        def _(e):
            P.play("pe", e)


def columns(a):
    return a.reshape(-1, 128).T


def lay_out(x):
    z = {n: np.asarray(a) for n, a in x.items()}
    arr = {}
    table, arr["rope"] = shape_constants()
    arr["consts"], arr["masks"] = table[:, 0:NC1], table[:, NC1:]
    pack = []
    for n, w in VEC:
        if n == "conv_dw_w":
            a = z[n][0].reshape(CW, 4, 128).transpose(2, 1, 0).reshape(128, 4 * CW)
        elif n == "lambda":
            a = np.zeros((128, 4), np.float32)
            for i, m in enumerate(("lambda_q1_2", "lambda_k1_2", "lambda_q2_2", "lambda_k2_2")):
                a[0:64, i] = z[m][0]
        else:
            a = columns(z[n])
        assert a.shape == (128, w), n
        pack.append(a)
    arr["vecs"] = np.concatenate(pack, axis=1)
    arr["xT"] = z["x"][0].T
    for n in ("rwkv_w2", "rwkv_a2", "rwkv_g2"):
        arr[n] = z[n][0]
    w = {n: z[n][0] for n in ("ada_w", "w_in", "w_out", "peer_w_q", "peer_v", "w_qkv_a_2", "w_o_a_2", "w_dq_2",
                              "w_o_b_2")}
    w["peer_uT"] = z["peer_u"][0].T
    for i in range(2):
        w[f"w_up_2_{i}"], w[f"w_down_2_{i}"] = z["w_up_2"][i], z["w_down_2"][i]
    w["w_dkv_2"] = np.concatenate([z["w_dkv_2"], z["w_dkv_2"][:, 256:320]], axis=1)
    ukv = z["w_ukv_2"].reshape(256, 8, 256)
    w["ukv_k"], w["ukv_v"] = ukv[:, :, 0:128].reshape(256, 1024), ukv[:, :, 128:256].reshape(256, 1024)
    uq = z["w_uq_2"][0].reshape(384, 8, 192)
    w["uq_n"], w["uq_r"] = uq[:, :, 0:128].reshape(384, 1024), uq[:, :, 128:192].reshape(384, 512)
    for n, a in w.items():
        arr[n] = tiled(a, *TILES[n])
    arr["keysT"] = z["peer_sub_keys"][0].transpose(3, 0, 1, 2).reshape(128, 2048)
    return {n: np.ascontiguousarray(a) for n, a in arr.items()}


def kernel(**inputs):
    import concourse.bacc as bacc
    from concourse.bass_utils import run_bass_kernel_spmd

    nc = bacc.Bacc("TRN2", target_bir_lowering=False, num_devices=1)
    arrays, dram = {}, {}
    for n, a in lay_out(inputs).items():
        arrays["in_" + n] = a
        dram[n] = nc.dram_tensor("in_" + n, a.shape, F32, kind="ExternalInput").ap()
    out = nc.dram_tensor("out_x", (D, S), F32, kind="ExternalOutput").ap()
    build(nc, dram, out)
    r = run_bass_kernel_spmd(nc, [arrays], core_ids=[0])
    return np.ascontiguousarray(r.results[0]["out_x"].T)[None]
```
